# Optimizing a Trainium2 kernel written in Bass

```python
import math
import jax
import jax.numpy as jnp
from jax import lax
import numpy as np

D_MODEL = 2048
BATCH = 1
SEQ = 128
DEPTH = 4
DEC_BATCH = 1
DEC_SEQ = 256
PAST_LEN = 128

GRID_W = 64
N_MIXERS = 3
N_A = (DEPTH + 2) // 3
N_B = (DEPTH + 1) // 3
N_C = DEPTH // 3
NORM_EPS = 1e-6

MLA_HEADS = 16
QK_NOPE = 128
QK_ROPE = 64
V_HEAD = 128
KV_LORA = 512
MLA_WIDTH = MLA_HEADS * V_HEAD
MLA_NQ = MLA_HEADS * (QK_NOPE + QK_ROPE)
MLA_IN = MLA_NQ + KV_LORA + QK_ROPE + MLA_WIDTH
ROPE_BASE = 10000.0
Q_BLOCK = 128

S5_WIDTH = D_MODEL
S5_GROUP = 16
S5_GROUPS = S5_WIDTH // S5_GROUP
S5_STATE = 64
DT_MIN = 1e-3
DT_MAX = 1e-1

GLA_HEADS = 4
GLA_DK = D_MODEL // 2 // GLA_HEADS
GLA_DV = D_MODEL // GLA_HEADS
GATE_RANK = 16
GATE_NORM = 16.0
GLA_CHUNK = 64
GLA_NK = GLA_HEADS * GLA_DK
GLA_NV = GLA_HEADS * GLA_DV
GLA_IN = 2 * GLA_NK + 2 * GLA_NV + 2 * GATE_RANK

kernel_name = "hybrid_diffusion_mla_s5_gla_step"

def rms_norm(x, g):
    xf = x.astype(jnp.float32)
    y = xf * lax.rsqrt(jnp.mean(xf * xf, axis=-1, keepdims=True) + NORM_EPS)
    return (y * g.astype(jnp.float32)).astype(x.dtype)

def ada_modulation(cond, w, b):
    m = jax.nn.silu(cond) @ w + b
    shift, scale, gate = jnp.split(m[:, None, :], 3, axis=-1)
    return shift, scale, gate

def axial_rope_angles(n_tok):
    rows = n_tok // GRID_W
    row = jnp.repeat(jnp.arange(rows), GRID_W).astype(jnp.float32)
    col = jnp.tile(jnp.arange(GRID_W), rows).astype(jnp.float32)
    half = QK_ROPE // 2
    inv_freq = 1.0 / (ROPE_BASE ** (jnp.arange(0, half, 2, dtype=jnp.float32) / half))
    return row[:, None] * inv_freq, col[:, None] * inv_freq

def rotate_half_pairs(x, ang):
    x1, x2 = jnp.split(x, 2, axis=-1)
    cos = jnp.cos(ang)[:, None, :].astype(x.dtype)
    sin = jnp.sin(ang)[:, None, :].astype(x.dtype)
    return jnp.concatenate([x1 * cos - x2 * sin, x1 * sin + x2 * cos], axis=-1)

def apply_axial_rope(x, ang_row, ang_col):
    xr, xc = jnp.split(x, 2, axis=-1)
    return jnp.concatenate([rotate_half_pairs(xr, ang_row), rotate_half_pairs(xc, ang_col)], axis=-1)

def blocked_attention(q, k, v):
    b, s, h, dq = q.shape
    nb = s // Q_BLOCK
    scale = dq ** -0.5
    qb = q.reshape(b, nb, Q_BLOCK, h, dq).transpose(1, 0, 2, 3, 4)

    def one_block(qi):
        sc = jnp.einsum('bqhd,bkhd->bhqk', qi, k).astype(jnp.float32) * scale
        p = jax.nn.softmax(sc, axis=-1).astype(v.dtype)
        return jnp.einsum('bhqk,bkhd->bqhd', p, v)

    o = lax.map(one_block, qb)
    return o.transpose(1, 0, 2, 3, 4).reshape(b, s, h, v.shape[-1])

def mla_project(h, w_in, kv_norm):
    b, t, _ = h.shape
    q, ckv, krope, gate = jnp.split(h @ w_in, [MLA_NQ, MLA_NQ + KV_LORA, MLA_NQ + KV_LORA + QK_ROPE], axis=-1)
    q = q.reshape(b, t, MLA_HEADS, QK_NOPE + QK_ROPE)
    return q, rms_norm(ckv, kv_norm), krope, gate

def mla_keys_values(ckv, krope, w_ukv):
    b, t, _ = ckv.shape
    kv = (ckv @ w_ukv).reshape(b, t, MLA_HEADS, QK_NOPE + V_HEAD)
    k_nope, v = jnp.split(kv, [QK_NOPE], axis=-1)
    k_rope = jnp.broadcast_to(krope[:, :, None, :], (b, t, MLA_HEADS, QK_ROPE))
    return jnp.concatenate([k_nope, k_rope], axis=-1), v

def mla_output(o, gate, w_out):
    b, t = o.shape[:2]
    return (o.reshape(b, t, MLA_WIDTH) * jax.nn.silu(gate)) @ w_out

def mla_context(h, w_in, kv_norm, w_ukv, w_out):
    q, ckv, krope, gate = mla_project(h, w_in, kv_norm)
    k, v = mla_keys_values(ckv, krope, w_ukv)
    return mla_output(blocked_attention(q, k, v), gate, w_out), ckv, krope

def mla_latent(h, ckv_ctx, krope_ctx, w_in, kv_norm, w_ukv, w_out):
    ang_r, ang_c = axial_rope_angles(h.shape[1])
    q, ckv, krope, gate = mla_project(h, w_in, kv_norm)
    q_nope, q_rope = jnp.split(q, [QK_NOPE], axis=-1)
    q = jnp.concatenate([q_nope, apply_axial_rope(q_rope, ang_r, ang_c)], axis=-1)
    krope = apply_axial_rope(krope[:, :, None, :], ang_r, ang_c)[:, :, 0]
    ckv_all = jnp.concatenate([ckv, ckv_ctx.astype(ckv.dtype)], axis=1)
    krope_all = jnp.concatenate([krope, krope_ctx.astype(krope.dtype)], axis=1)
    k, v = mla_keys_values(ckv_all, krope_all, w_ukv)
    return mla_output(blocked_attention(q, k, v), gate, w_out)

def s5_discretise(a_re, a_im, log_dt, b_re, b_im):
    a = lax.complex(a_re.astype(jnp.float32), a_im.astype(jnp.float32))
    dt = jnp.exp(log_dt.astype(jnp.float32))[:, None]
    a_bar = jnp.exp(a * dt)
    bmat = lax.complex(b_re.astype(jnp.float32), b_im.astype(jnp.float32))
    b_bar = ((a_bar - 1.0) / a)[..., None] * bmat
    return a_bar, b_bar

def s5_scan(u, a_bar, b_bar, cmat, h0, reverse):
    length = u.shape[1]
    edge = -1 if reverse else 0
    bu = jnp.einsum('gnp,blgp->blgn', b_bar, u)
    bu = bu.at[:, edge].add(a_bar * h0)
    a = jnp.broadcast_to(a_bar, (1, length) + a_bar.shape)

    def combine(e1, e2):
        a1, b1 = e1
        a2, b2 = e2
        return a2 * a1, a2 * b1 + b2

    _, states = lax.associative_scan(combine, (a, bu), reverse=reverse, axis=1)
    y = jnp.einsum('gpn,blgn->blgp', cmat, states).real
    return y, states[:, edge]

def s5_mixer(h, h0, w_in, a_re, a_im, log_dt, b_re, b_im, c_re, c_im, d, w_glu, b_glu, w_out):
    bsz, length, _ = h.shape
    u, gate = jnp.split(h @ w_in, 2, axis=-1)
    uf = u.astype(jnp.float32)
    ug = uf.reshape(bsz, length, S5_GROUPS, S5_GROUP)
    y = d.astype(jnp.float32) * uf
    finals = []
    for di in range(2):
        a_bar, b_bar = s5_discretise(a_re[di], a_im[di], log_dt[di], b_re[di], b_im[di])
        cmat = lax.complex(c_re[di].astype(jnp.float32), c_im[di].astype(jnp.float32))
        h_init = lax.complex(h0[:, di, ..., 0].astype(jnp.float32), h0[:, di, ..., 1].astype(jnp.float32))
        yd, hf = s5_scan(ug, a_bar, b_bar, cmat, h_init, reverse=(di == 1))
        y = y + yd.reshape(bsz, length, S5_WIDTH)
        finals.append(jnp.stack([hf.real, hf.imag], axis=-1))
    y = jax.nn.gelu(y).astype(h.dtype)
    y = y * jax.nn.sigmoid(y @ w_glu + b_glu)
    out = (y * jax.nn.silu(gate)) @ w_out
    return out, jnp.stack(finals, axis=1)

def gla_direction(q, k, v, g, s0):
    bsz, length, nh, dk = q.shape
    dv = v.shape[-1]
    nc = length // GLA_CHUNK

    def chunks(x):
        return x.reshape(bsz, nc, GLA_CHUNK, nh, x.shape[-1])

    qc, kc, vc, gc = chunks(q), chunks(k), chunks(v), chunks(g)
    bcum = jnp.cumsum(gc, axis=2)
    blast = bcum[:, :, -1:]
    q_t = qc * jnp.exp(bcum)
    k_t = kc * jnp.exp(-bcum)
    k_d = kc * jnp.exp(blast - bcum)
    mask = jnp.tril(jnp.ones((GLA_CHUNK, GLA_CHUNK), dtype=bool))
    att = jnp.where(mask, jnp.einsum('bnchk,bnshk->bnhcs', q_t, k_t), 0.0)
    o_intra = jnp.einsum('bnhcs,bnshv->bnchv', att, vc)

    def step(s, xs):
        qn, kn, vn, dn = xs
        o = jnp.einsum('bchk,bhkv->bchv', qn, s)
        s = dn[..., None] * s + jnp.einsum('bchk,bchv->bhkv', kn, vn)
        return s, o

    xs = (q_t.swapaxes(0, 1), k_d.swapaxes(0, 1), vc.swapaxes(0, 1), jnp.exp(blast[:, :, 0]).swapaxes(0, 1))
    s_fin, o_inter = lax.scan(step, s0, xs)
    o = o_intra + o_inter.swapaxes(0, 1)
    return o.reshape(bsz, length, nh, dv), s_fin

def gla_mixer(h, s0, w_in, w_g2, b_g, norm_g, w_out):
    bsz, length, _ = h.shape
    q, k, v, r, glr = jnp.split(h @ w_in, [GLA_NK, 2 * GLA_NK, 2 * GLA_NK + GLA_NV, 2 * GLA_NK + 2 * GLA_NV], axis=-1)
    q = q.astype(jnp.float32).reshape(bsz, length, GLA_HEADS, GLA_DK) * (GLA_DK ** -0.5)
    k = k.astype(jnp.float32).reshape(bsz, length, GLA_HEADS, GLA_DK)
    v = v.astype(jnp.float32).reshape(bsz, length, GLA_HEADS, GLA_DV)
    glr = glr.astype(jnp.float32).reshape(bsz, length, 2, GATE_RANK)
    o = jnp.zeros((bsz, length, GLA_HEADS, GLA_DV), jnp.float32)
    finals = []
    for di in range(2):
        g = jax.nn.log_sigmoid(glr[:, :, di] @ w_g2[di].astype(jnp.float32) + b_g[di].astype(jnp.float32)) / GATE_NORM
        g = g.reshape(bsz, length, GLA_HEADS, GLA_DK)
        rev = (lambda a: jnp.flip(a, axis=1)) if di == 1 else (lambda a: a)
        od, sf = gla_direction(rev(q), rev(k), rev(v), rev(g), s0[:, di].astype(jnp.float32))
        o = o + rev(od)
        finals.append(sf)
    o = rms_norm(o, norm_g).reshape(bsz, length, GLA_NV).astype(h.dtype)
    out = (o * jax.nn.silu(r)) @ w_out
    return out, jnp.stack(finals, axis=1)

def setup_inputs(seed: int = 0) -> dict:
    key = jax.random.key(seed)
    keys = iter(jax.random.split(key, 48))
    f32 = jnp.float32

    def nrm(shape, scale=1.0):
        return jax.random.normal(next(keys), shape, f32) * scale

    x_prompt = nrm((BATCH, SEQ, D_MODEL))
    x_sample = nrm((DEC_BATCH, DEC_SEQ, D_MODEL))
    cache_mla_ckv = nrm((DEC_BATCH, N_A, PAST_LEN, KV_LORA))
    cache_mla_krope = nrm((DEC_BATCH, N_A, PAST_LEN, QK_ROPE))
    state_s5 = nrm((DEC_BATCH, N_B, 2, S5_GROUPS, S5_STATE, 2), 0.5)
    state_gla = nrm((DEC_BATCH, N_C, 2, GLA_HEADS, GLA_DK, GLA_DV))
    c = nrm((DEC_BATCH, D_MODEL))
    c_ctx = nrm((D_MODEL,))
    ada_w = nrm((DEPTH, D_MODEL, 3 * D_MODEL), 0.5 * D_MODEL ** -0.5)
    ada_b = nrm((DEPTH, 3 * D_MODEL), 0.02)
    norm_pre = 1.0 + nrm((DEPTH, D_MODEL), 0.02)
    norm_post = 1.0 + nrm((DEPTH, D_MODEL), 0.02)
    mla_w_in = nrm((N_A, D_MODEL, MLA_IN), D_MODEL ** -0.5)
    mla_kv_norm = 1.0 + nrm((N_A, KV_LORA), 0.02)
    mla_w_ukv = nrm((N_A, KV_LORA, MLA_HEADS * (QK_NOPE + V_HEAD)), KV_LORA ** -0.5)
    mla_w_out = nrm((N_A, MLA_WIDTH, D_MODEL), MLA_WIDTH ** -0.5)
    s5_w_in = nrm((N_B, D_MODEL, 2 * S5_WIDTH), D_MODEL ** -0.5)
    s5_a_re = -0.5 + nrm((N_B, 2, S5_GROUPS, S5_STATE), 0.01)
    s5_a_im = np.pi * jnp.arange(S5_STATE, dtype=f32) + nrm((N_B, 2, S5_GROUPS, S5_STATE), 0.01)
    s5_log_dt = jax.random.uniform(next(keys), (N_B, 2, S5_GROUPS), f32, math.log(DT_MIN), math.log(DT_MAX))
    s5_b_re = nrm((N_B, 2, S5_GROUPS, S5_STATE, S5_GROUP), (2.0 * S5_GROUP) ** -0.5)
    s5_b_im = nrm((N_B, 2, S5_GROUPS, S5_STATE, S5_GROUP), (2.0 * S5_GROUP) ** -0.5)
    s5_c_re = nrm((N_B, 2, S5_GROUPS, S5_GROUP, S5_STATE), (2.0 * S5_STATE) ** -0.5)
    s5_c_im = nrm((N_B, 2, S5_GROUPS, S5_GROUP, S5_STATE), (2.0 * S5_STATE) ** -0.5)
    s5_d = nrm((N_B, S5_WIDTH), 0.5)
    s5_w_glu = nrm((N_B, S5_WIDTH, S5_WIDTH), S5_WIDTH ** -0.5)
    s5_b_glu = nrm((N_B, S5_WIDTH), 0.02)
    s5_w_out = nrm((N_B, S5_WIDTH, D_MODEL), S5_WIDTH ** -0.5)
    gla_w_in = nrm((N_C, D_MODEL, GLA_IN), D_MODEL ** -0.5)
    gla_w_g2 = nrm((N_C, 2, GATE_RANK, GLA_NK), GATE_RANK ** -0.5)
    gla_b_g = nrm((N_C, 2, GLA_NK), 0.02)
    gla_norm = 1.0 + nrm((N_C, GLA_DV), 0.02)
    gla_w_out = nrm((N_C, GLA_NV, D_MODEL), GLA_NV ** -0.5)
    return {
        'x_prompt': x_prompt, 'x_sample': x_sample,
        'cache_mla_ckv': cache_mla_ckv, 'cache_mla_krope': cache_mla_krope,
        'state_s5': state_s5, 'state_gla': state_gla,
        'c': c, 'c_ctx': c_ctx,
        'ada_w': ada_w, 'ada_b': ada_b, 'norm_pre': norm_pre, 'norm_post': norm_post,
        'mla_w_in': mla_w_in, 'mla_kv_norm': mla_kv_norm, 'mla_w_ukv': mla_w_ukv, 'mla_w_out': mla_w_out,
        's5_w_in': s5_w_in, 's5_a_re': s5_a_re, 's5_a_im': s5_a_im, 's5_log_dt': s5_log_dt,
        's5_b_re': s5_b_re, 's5_b_im': s5_b_im, 's5_c_re': s5_c_re, 's5_c_im': s5_c_im,
        's5_d': s5_d, 's5_w_glu': s5_w_glu, 's5_b_glu': s5_b_glu, 's5_w_out': s5_w_out,
        'gla_w_in': gla_w_in, 'gla_w_g2': gla_w_g2, 'gla_b_g': gla_b_g, 'gla_norm': gla_norm,
        'gla_w_out': gla_w_out,
    }

def reference(x_prompt, x_sample, cache_mla_ckv, cache_mla_krope, state_s5, state_gla, c, c_ctx,
              ada_w, ada_b, norm_pre, norm_post,
              mla_w_in, mla_kv_norm, mla_w_ukv, mla_w_out,
              s5_w_in, s5_a_re, s5_a_im, s5_log_dt, s5_b_re, s5_b_im, s5_c_re, s5_c_im,
              s5_d, s5_w_glu, s5_b_glu, s5_w_out,
              gla_w_in, gla_w_g2, gla_b_g, gla_norm, gla_w_out):
    ctx_batch = x_prompt.shape[0]
    xp, xs = x_prompt, x_sample
    ckv_out, krope_out, s5_out, gla_out = [], [], [], []
    for l in range(DEPTH):
        kind, j = l % N_MIXERS, l // N_MIXERS
        shift_p, scale_p, gate_p = ada_modulation(c_ctx[None, :], ada_w[l], ada_b[l])
        shift_s, scale_s, gate_s = ada_modulation(c, ada_w[l], ada_b[l])
        hp = rms_norm(xp, norm_pre[l]) * (1.0 + scale_p) + shift_p
        hs = rms_norm(xs, norm_pre[l]) * (1.0 + scale_s) + shift_s
        if kind == 0:
            wts = (mla_w_in[j], mla_kv_norm[j], mla_w_ukv[j], mla_w_out[j])
            op, ckv, krope = mla_context(hp, *wts)
            os_ = mla_latent(hs, cache_mla_ckv[:, j], cache_mla_krope[:, j], *wts)
            ckv_out.append(ckv)
            krope_out.append(krope)
        elif kind == 1:
            wts = (s5_w_in[j], s5_a_re[j], s5_a_im[j], s5_log_dt[j], s5_b_re[j], s5_b_im[j],
                   s5_c_re[j], s5_c_im[j], s5_d[j], s5_w_glu[j], s5_b_glu[j], s5_w_out[j])
            zero_state = jnp.zeros((ctx_batch, 2, S5_GROUPS, S5_STATE, 2), jnp.float32)
            op, st = s5_mixer(hp, zero_state, *wts)
            os_, _ = s5_mixer(hs, state_s5[:, j], *wts)
            s5_out.append(st)
        else:
            wts = (gla_w_in[j], gla_w_g2[j], gla_b_g[j], gla_norm[j], gla_w_out[j])
            zero_state = jnp.zeros((ctx_batch, 2, GLA_HEADS, GLA_DK, GLA_DV), jnp.float32)
            op, st = gla_mixer(hp, zero_state, *wts)
            os_, _ = gla_mixer(hs, state_gla[:, j], *wts)
            gla_out.append(st)
        xp = xp + gate_p * rms_norm(op, norm_post[l])
        xs = xs + gate_s * rms_norm(os_, norm_post[l])
    y_prompt = xp
    y_sample = xs
    new_mla_ckv = jnp.stack(ckv_out, axis=1)
    new_mla_krope = jnp.stack(krope_out, axis=1)
    new_state_s5 = jnp.stack(s5_out, axis=1)
    new_state_gla = jnp.stack(gla_out, axis=1)
    return (y_prompt, y_sample, new_mla_ckv, new_mla_krope, new_state_s5, new_state_gla)


_drawn_inputs = setup_inputs


def setup_inputs(seed=0):
    import zlib

    import numpy as np

    out = dict(_drawn_inputs(seed))
    spreads = {}
    factors = {'state_gla': 3.664,
     'norm_post': 4.813,
     'mla_kv_norm': 2.67,
     's5_a_re': 64.0,
     's5_b_glu': 8.0,
     'gla_b_g': 5.689,
     'gla_norm': 28.978,
     'cache_mla_krope': 3.26}
    for name, (base, spread) in spreads.items():
        noise = np.random.default_rng([zlib.crc32(name.encode()), seed]).standard_normal(out[name].shape)
        drawn = base * np.exp(spread * noise) if base else spread * noise
        out[name] = jnp.asarray(drawn.astype(out[name].dtype))
    for name, factor in factors.items():
        out[name] = (out[name] * factor).astype(out[name].dtype)
    return out
```

```python
from contextlib import ExitStack

import numpy as np
import concourse.bass as bass
from concourse import mybir

ALU = mybir.AluOpType
ACT = mybir.ActivationFunctionType
AX = mybir.AxisListType
F32 = mybir.dt.float32
U32 = mybir.dt.uint32

P = 128
D = 2048
KT = D // P
CTX, LAT, PAST = 128, 256, 128
TOK = CTX + LAT
NT = TOK // P
COND = ((0, 0, CTX), (1, CTX, TOK))
TILE_COND = (0, 1, 1)
DEPTH = 4
EPS = 1e-6
GC = 512
HEADS, NOPE, ROPE, VH, LORA = 16, 128, 64, 128, 512
NQ = HEADS * (NOPE + ROPE)
KEYS = CTX + LAT + PAST
SM_SCALE = float(NOPE + ROPE) ** -0.5
ROPE_BASE, GRID_W = 10000.0, 64
SG, SC, SN, ST = 128, 16, 64, 8
SCH = TOK // ST
SCX = CTX // ST
GH, GDK, GDV, GRANK, GCH = 4, 256, 512, 16, 64
GATE_NORM = 16.0


def shape_constants():
    c = {}
    c["ident"] = np.eye(P, dtype=np.float32)
    half = ROPE // 2
    inv = 1.0 / (np.float32(ROPE_BASE) ** (np.arange(0, half, 2, dtype=np.float32) / half))
    tok = np.arange(LAT)
    ang = [(tok // GRID_W).astype(np.float32)[:, None] * inv, (tok % GRID_W).astype(np.float32)[:, None] * inv]
    cos, sin = np.zeros((P, LAT), np.float32), np.zeros((P, LAT), np.float32)
    swap = np.zeros((P, P), np.float32)
    for r in range(P):
        d = r % ROPE
        a = ang[d // half].astype(np.float32)[:, d % (half // 2)]
        cos[r], sin[r] = np.cos(a), np.sin(a)
        first = d % half < half // 2
        partner = r + half // 2 if first else r - half // 2
        swap[partner, r] = -1.0 if first else 1.0
    c["rope_cos"], c["rope_sin"], c["rope_swap"] = cos, sin, swap
    s, t = np.arange(P)[:, None], np.arange(P)[None, :]
    same = s // GCH == t // GCH
    c["gla_mask"] = np.stack([same & (s <= t), same & (s >= t)], 1).astype(np.float32)
    edge = np.ones((P, TOK), np.float32)
    edge[:, ::GCH] = 0.0
    c["gla_edge"] = edge
    return c


def first_groups(layers):
    jobs = [(f"ada{l}{part}", 6) for l in range(DEPTH) for part in "ab"]
    for l in layers:
        jobs += {
            0: [(f"q{l}", 8), (f"ckv{l}", 1), (f"krope{l}", 1), (f"gate{l}", 4), (f"ukv{l}", 2), (f"out{l}", 4)],
            1: [(f"u{l}", 4), (f"gate{l}", 4), (f"glu{l}", 4), (f"out{l}", 4)],
            2: [(f"q{l}", 2), (f"k{l}", 2), (f"v{l}", 4), (f"r{l}", 4), (f"glr{l}", 1), (f"out{l}", 4)],
        }[l % 3]
    first, n = {}, 0
    for name, groups in jobs:
        first[name] = n
        n += groups
    return first


def stage_list(layers):
    names = ["rows_in", "rows_transposed", "vectors_ready", "silu_c"]
    names += [f"s5.{s}" for s in ("loaded", "dt", "angle", "reduced", "sines", "poles", "turned_pow0", "copied_pow0",
                                  "turned_pow1", "copied_pow1", "turned_pow2", "copied_pow2")]
    names += [f"s5.{s}{n}" for n in range(4) for s in ("turned_b", "copied_b")]
    names += [f"s5.{s}{n}" for n in range(4) for s in ("turned_c", "copied_c")]
    for l in range(DEPTH):
        names += [f"ada{l}.{s}" for s in ("rows", "transposed", "ready")]
    kinds = {0: ("projected", "kv_rstd", "kv_normed", "kv_transposed", "kv_copied", "rotated", "roped", "attended"),
             1: ("projected", "gate_parked", "contributions", "scanned", "mixed", "gated", "gated_y", "glu"), 2: ("projected", "z0", "z_taken0", "z1", "z_taken1", "abs", "softplus", "log_gates", "attended")}
    for l in layers:
        names += [f"norm{l}.{s}" for s in ("stats", "scales", "scaled", "turned0", "copied0", "turned1", "copied1")]
        names += [f"mix{l}.{s}" for s in kinds[l % 3]]
        names += [f"out{l}.{s}" for s in ("gate", "gate_spread", "gate_copied", "projected", "stats", "rstd", "scaled",
                                          "added")]
    return names


def build(nc, ins, outs, consts, layers=range(DEPTH), dbg=None):
    ctx = ExitStack()
    with ctx:
        def sb(name, shape, dt=F32):
            return ctx.enter_context(nc.sbuf_tensor(name, shape, dt))

        def sem(name):
            return ctx.enter_context(nc.semaphore(name))

        x = sb("x", [P, NT, D])
        hT = sb("hT", [P, KT, TOK])
        ring = sb("ring", [P, 2, 4, 4, GC])
        ident = sb("ident", [P, P])
        vecs = sb("vecs", [P, 4, P])
        mod = sb("mod", [P, DEPTH, 48, 2])
        silu_c = sb("silu_c", [P, KT, 2])
        small = sb("small", [P, 64])
        arena = sb("arena", [P, 23000])
        FIRST_GROUP = first_groups(layers)

        def nth(l):
            return sum(1 for m in layers if m < l and m % 3 == l % 3)

        def view(at, *shape):
            n = int(np.prod(shape))
            assert at + n <= 23000, (at, shape)
            v = arena[:, at:at + n]
            if len(shape) == 2:
                return v.rearrange("p (a b) -> p a b", a=shape[0])
            if len(shape) == 3:
                return v.rearrange("p (a b c) -> p a b c", a=shape[0], b=shape[1])
            if len(shape) == 5:
                return v.rearrange("p (a b c d e) -> p a b c d e", a=shape[0], b=shape[1], c=shape[2], d=shape[3])
            if len(shape) == 4:
                return v.rearrange("p (a b c d) -> p a b c d", a=shape[0], b=shape[1], c=shape[2])
            return v

        banks = [ctx.enter_context(nc.psum_tensor(f"bank{i}", [P, 512], F32)) for i in range(8)]

        landed = [[sem(f"landed{h}{s}") for s in range(4)] for h in range(2)]
        rope_landed = [[sem(f"rope_landed{h}{s}") for s in range(4)] for h in range(2)]
        chunk_used = sem("chunk_used")
        sums_ready = sem("sums_ready")
        sums_taken = [sem("sums_taken0"), sem("sums_taken1")]
        stage_done = sem("stage_done")
        inputs_in = sem("inputs_in")
        small_in = sem("small_in")
        stored = sem("stored")
        stores = [0]

        block = ctx.enter_context(nc.Block())
        w = {k: v for k, v in ins.items()}

        stage_names = stage_list(layers)

        def after(name):
            return 3 * (stage_names.index(name) + 1)

        class Stages:
            def __init__(self, eng):
                self.eng, self.n = eng, 0

            def at(self, name):
                assert stage_names[self.n] == name, (stage_names[self.n], name)
                self.eng.drain().then_inc(stage_done, 1)
                self.n += 1
                self.eng.wait_ge(stage_done, 3 * self.n)

        def load_group(sp, i, g0, u, src, cols, rope=False):
            half = (g0 + u) % 2
            for s in range(4):
                sp.wait_ge(chunk_used, i * 8 + (4 * (g0 + u) + s + 1))
                if rope:
                    parts = src(s, u)
                    at = 0
                    for n, part in enumerate(parts):
                        width = part.shape[2]
                        sp.dma_start(ring[:, half, s, :, at:at + width], part)\
                            .then_inc((rope_landed if n else landed)[half][s], 16)
                        at += width
                else:
                    sp.dma_start(ring[:, half, s, :, 0:cols], src(s, u)).then_inc(landed[half][s], 16)

        def loop_groups(eng, name, groups, body):
            g0 = FIRST_GROUP[name]
            if groups >= 4:
                with eng.Fori(0, groups // 2) as i:
                    for u in range(2):
                        body(i, g0, u)
            else:
                for g in range(groups):
                    body(0, g0, g)

        def load_job(sp, name, groups, weight, col0, cols=GC):
            wv = weight.rearrange("(s k p) n -> s p k n", k=4, p=P)

            def body(i, g0, u):
                load_group(sp, i, g0, u, lambda s, u: wv[s, :, :, bass.ds(i * (2 * GC) + (col0 + u * GC), cols)], cols)
            loop_groups(nc.sync, name, groups, body)

        def group_sums(pe, i, g0, u, tiles, moving=None, cols=GC, row_tiles=None, ntok=TOK):
            half = (g0 + u) % 2
            pe.wait_ge(sums_taken[half], i * 2 + 2 * ((g0 + u) // 2 + 1))
            for s in range(4):
                pe.wait_ge(landed[half][s], i * 16 + 16 * ((g0 + u) // 2 + 1))
                for k in range(4):
                    kt = 4 * s + k
                    if tiles is not None:
                        at = 0
                        for m, width in enumerate(tiles):
                            mm = nc.tensor.matmul(banks[4 * half + m][0:width, 0:TOK],
                                                  ring[:, half, s, k, at:at + width], moving[:, kt, :],
                                                  start=(kt == 0), stop=(kt == KT - 1))
                            at += width
                    else:
                        for t, (rows, lhsT) in enumerate(row_tiles(kt)):
                            mm = nc.tensor.matmul(banks[4 * half + t][0:rows, 0:cols], lhsT,
                                                  ring[:, half, s, k, 0:cols],
                                                  start=(kt == 0), stop=(kt == KT - 1))
                mm.then_inc(chunk_used, 1)
            nc.tensor.drain().then_inc(sums_ready, 1)

        def token_tiles(kt, src=None):
            src = hT if src is None else src
            return [(P, src[:, kt, t * P:(t + 1) * P]) for t in range(NT)]

        def evacuate(eng, sys_eng, name, groups, write, share=1, which=(0, 1)):
            def body(i, g0, u):
                if u in which:
                    eng.wait_ge(sums_ready, i * 2 + (g0 + u + 1))
                    half = (g0 + u) % 2
                    write(i, u, half)
                    eng.drain().then_inc(sums_taken[half], share)
            loop_groups(sys_eng, name, groups, body)

        def act_copy(out, in_):
            return nc.scalar.activation(out, in_, ACT.Copy)

        VEC = {"c_ctx": (0, 0), "c": (0, 16), "b_glu": (0, 32), "d": (0, 48), "norm_pre": (0, 64),
               "norm_post": (1, 0), "gla_b_g": (1, 64), "ada0": (2, 0), "ada1": (3, 0)}
        rows_v = view(0, 4, P)
        mrow = view(0, 6144)

        def vec(name, at=0, n=16):
            tile_, col = VEC[name]
            return vecs[:, tile_, col + at:col + at + n]

        from_layer = {l: {} for l in range(DEPTH)}
        qn = view(0, HEADS, TOK)
        qr = view(6144, HEADS // 2, TOK)
        gateT = view(9216, HEADS, TOK)
        tmp0 = 15360
        ckv_sb = view(tmp0, 4, LORA)
        ckvT = view(tmp0 + 2048, 4, KEYS)
        kr_sb = view(tmp0 + 4096, 4, P)
        gamma = view(tmp0 + 4608, LORA)
        cos_t = view(tmp0 + 5120, LAT)
        sin_t = view(tmp0 + 5376, LAT)
        swap_t = view(tmp0 + 5632, P)
        krT = view(tmp0 + 5760, KEYS)
        rope_tmp = view(tmp0 + 6272, 2, LAT)
        kT = view(tmp0, 2, KEYS)
        v_sb = view(tmp0 + 1024, 4, 2 * VH)
        o_sb = view(0, NT, D)
        gate_bc = view(6144, 2, D)
        sq_junk = view(10240, D)
        xn = view(0, NT, D)
        G_small = view(10240 + 2048, KT, 2)

        p_sb = view(tmp0 + 4096, 3, LAT + PAST)

        ss = small[:, 0:3]
        rs = small[:, 3:6]
        mx = small[:, 8:16]
        sm = small[:, 16:24]
        eps_c = small[:, 63:64]

        maxes_ready = sem("maxes_ready")
        exps_ready = sem("exps_ready")
        qn_junk = view(tmp0 + 5760, LORA)
        G_scale = view(15360, KT, 2)
        INPUT_LOADS = 12
        rows_zero = sem("rows_zero")
        result_out = sem("result_out")
        MLA_LOADS = 7

        def pe_program(pe):
            st = Stages(nc.tensor)
            pe.wait_ge(inputs_in, 16 * INPUT_LOADS)
            pe_start(pe, st)
            pe_s5_basics(pe, st)
            for l in range(DEPTH):
                pe_ada(pe, st, l)
            for l in layers:
                pe_norm(pe, st, l)
                [pe_mla, pe_s5, pe_gla][l % 3](pe, st, l)
                pe_out(pe, st, l)

        def pe_start(pe, st):
            st.at(f"rows_in")
            for a in range(4):
                nc.tensor.transpose(banks[0][:, a * P:(a + 1) * P], rows_v[:, a, :], ident[:, :])
            st.at(f"rows_transposed")
            st.at(f"vectors_ready")
            st.at(f"silu_c")

        def pe_ada(pe, st, l):
            def body(i, g0, u):
                group_sums(pe, i, g0, u, None, row_tiles=lambda kt: [(2, silu_c[:, kt, :])])
            for part in range(2):
                loop_groups(nc.tensor, f"ada{l}{'ab'[part]}", 6, body)
                pe_s5_batch(pe, 2 * l + part)
            st.at(f"ada{l}.rows")
            for j in range(48):
                nc.tensor.transpose(banks[0][:, 2 * j:2 * j + 2], mrow[0:2, j * P:(j + 1) * P], ident[0:2, 0:2])
            st.at(f"ada{l}.transposed")
            st.at(f"ada{l}.ready")

        def pe_norm(pe, st, l):
            st.at(f"norm{l}.stats")
            st.at(f"norm{l}.scales")
            st.at(f"norm{l}.scaled")
            for half in range(2):
                for k in range(8 * half, 8 * half + 8):
                    for t in range(NT):
                        nc.tensor.transpose(banks[k % 8][:, t * P:(t + 1) * P], xn[:, t, k * P:(k + 1) * P],
                                            ident[:, :])
                st.at(f"norm{l}.turned{half}")
                st.at(f"norm{l}.copied{half}")

        def pe_out(pe, st, l):
            st.at(f"out{l}.gate")
            for c in range(2):
                for k in range(KT):
                    nc.tensor.matmul(banks[c * 4 + k // 4][:, (k % 4) * P:(k % 4 + 1) * P],
                                     G_small[:, k, c:c + 1].broadcast_to([P, P]), ident[:, :],
                                     start=True, stop=True)
            st.at(f"out{l}.gate_spread")
            st.at(f"out{l}.gate_copied")

            def body(i, g0, u):
                group_sums(pe, i, g0, u, None, row_tiles=lambda kt: token_tiles(kt, s5_z if l % 3 == 1 else hT))
            loop_groups(nc.tensor, f"out{l}", 4, body)
            st.at(f"out{l}.projected")
            st.at(f"out{l}.stats")
            st.at(f"out{l}.rstd")
            st.at(f"out{l}.scaled")
            st.at(f"out{l}.added")

        def pe_mla(pe, st, l):
            def q_body(i, g0, u):
                half = (g0 + u) % 2
                pe.wait_ge(sums_taken[half], i * 2 + 2 * ((g0 + u) // 2 + 1))
                for s in range(4):
                    pe.wait_ge(landed[half][s], i * 16 + 16 * ((g0 + u) // 2 + 1))
                    pe.wait_ge(rope_landed[half][s], i * 48 + 48 * (4 * nth(l) + 1))
                    for k in range(4):
                        kt = 4 * s + k
                        for m in range(3):
                            mm = nc.tensor.matmul(banks[4 * half + m][:, 0:TOK], ring[:, half, s, k, m * P:(m + 1) * P],
                                                  hT[:, kt, :], start=(kt == 0), stop=(kt == KT - 1))
                    mm.then_inc(chunk_used, 1)
                nc.tensor.drain().then_inc(sums_ready, 1)
            loop_groups(nc.tensor, f"q{l}", 8, q_body)
            group_sums(pe, 0, FIRST_GROUP[f"ckv{l}"], 0, None, row_tiles=token_tiles)
            group_sums(pe, 0, FIRST_GROUP[f"krope{l}"], 0, None, row_tiles=token_tiles, cols=ROPE)

            def gate_body(i, g0, u):
                group_sums(pe, i, g0, u, [P] * 4, moving=hT)
            loop_groups(nc.tensor, f"gate{l}", 4, gate_body)
            st.at(f"mix{l}.projected")
            st.at(f"mix{l}.kv_rstd")
            st.at(f"mix{l}.kv_normed")
            for kt in range(4):
                for t in range(4):
                    nc.tensor.transpose(banks[kt][:, t * P:(t + 1) * P], ckv_sb[:, t, kt * P:(kt + 1) * P], ident[:, :])
            for t in range(4):
                nc.tensor.transpose(banks[4][:, t * P:(t + 1) * P], kr_sb[:, t, :], ident[:, :])
            st.at(f"mix{l}.kv_transposed")
            st.at(f"mix{l}.kv_copied")
            for j in range(9):
                src = qr[:, j, CTX:TOK] if j < 8 else krT[:, CTX:TOK]
                nc.tensor.matmul(banks[j // 2][:, (j % 2) * LAT:(j % 2 + 1) * LAT], swap_t, src, start=True, stop=True)
            st.at(f"mix{l}.rotated")
            st.at(f"mix{l}.roped")
            pe_attention(pe, st, l)

        def seen(t):
            return (0, CTX) if t == 0 else (CTX, KEYS)

        kv_ready = sem("kv_ready")
        kv_copied = sem("kv_copied")
        scores_ready = sem("scores_ready")
        probs_ready = sem("probs_ready")
        probsT_ready = sem("probsT_ready")
        probsT_copied = sem("probsT_copied")
        heads_ready = sem("heads_ready")
        heads_done = sem("heads_done")
        pT = view(tmp0 + 6272, 4, LAT)

        def pe_attention(pe, st, l):
            base = 16 * nth(l)
            for pair in range(8):
                g = FIRST_GROUP[f"ukv{l}"] + pair // 4
                half, s = g % 2, pair % 4
                pe.wait_ge(landed[half][s], 16 * (g // 2 + 1))
                if pair:
                    pe.wait_ge(kv_copied, 2 * (8 * nth(l) + pair))
                for hh in range(2):
                    for kt in range(4):
                        nc.tensor.matmul(banks[4 + hh][:, 0:KEYS], ring[:, half, s, kt, hh * 256:hh * 256 + P],
                                         ckvT[:, kt, :], start=(kt == 0), stop=(kt == 3))
                for t in range(4):
                    for kt in range(4):
                        mm = nc.tensor.matmul(banks[6 + t // 2][:, (t % 2) * 256:(t % 2 + 1) * 256],
                                              ckvT[:, kt, t * P:(t + 1) * P],
                                              ring[:, half, s, kt, :].rearrange("p (h x) -> p h x", h=2)[:, :, NOPE:],
                                              start=(kt == 0), stop=(kt == 3))
                mm.then_inc(chunk_used, 1)
                nc.tensor.drain().then_inc(kv_ready, 1)
                pe.wait_ge(kv_copied, 2 * (8 * nth(l) + pair + 1))
                for hh in range(2):
                    h = 2 * pair + hh
                    n = base + h
                    rp = slice(hh * ROPE, (hh + 1) * ROPE)
                    if h:
                        pe.wait_ge(heads_done, n)
                    for t in range(3):
                        a, b = seen(t)
                        nc.tensor.matmul(banks[t][:, 0:b - a], qn[:, h, t * P:(t + 1) * P], kT[:, hh, a:b],
                                         start=True, stop=False)
                        nc.tensor.matmul(banks[t][:, 0:b - a], qr[rp, pair, t * P:(t + 1) * P], krT[rp, a:b],
                                         start=False, stop=True)
                    nc.tensor.drain().then_inc(scores_ready, 1)
                    pe.wait_ge(probs_ready, n + 1)
                    nc.tensor.transpose(banks[0][:, 0:P], p_sb[:, 0, 0:P], ident[:, :])
                    for kk in range(3):
                        for t in (1, 2):
                            at = (kk % 2) * LAT + (t - 1) * P
                            dst = banks[1 + kk // 2][:, at:at + P]
                            nc.tensor.transpose(dst, p_sb[:, t, kk * P:(kk + 1) * P], ident[:, :])
                    nc.tensor.drain().then_inc(probsT_ready, 1)
                    pe.wait_ge(probsT_copied, 2 * (n + 1))
                    vh = slice(hh * VH, (hh + 1) * VH)
                    nc.tensor.matmul(banks[3][:, 0:CTX], v_sb[:, 0, vh], pT[:, 0, 0:CTX], start=True, stop=True)
                    for kk in range(3):
                        nc.tensor.matmul(banks[3][:, CTX:TOK], v_sb[:, 1 + kk, vh], pT[:, 1 + kk, :],
                                         start=(kk == 0), stop=(kk == 2))
                    nc.tensor.drain().then_inc(heads_ready, 1)
            nc.tensor.sem_inc(sums_ready, 2)
            st.at(f"mix{l}.attended")

        def act_program(act):
            st = Stages(nc.scalar)
            act.wait_ge(inputs_in, 16 * INPUT_LOADS)
            st.at("rows_in")
            st.at("rows_transposed")
            st.at("vectors_ready")
            for c in range(2):
                nc.scalar.activation(silu_c[:, :, c], vecs[:, 0, c * 16:c * 16 + 16], ACT.Silu)
            st.at("silu_c")
            act_s5_basics(act, st)
            for l in range(DEPTH):
                for part in range(2):
                    def write(i, u, half):
                        act_copy(mrow[0:2, bass.ds(i * 1024 + (part * 3072 + u * GC), GC)], banks[4 * half][0:2, :])
                    evacuate(act, nc.scalar, f"ada{l}{'ab'[part]}", 6, write, share=2)
                    act_s5_batch(act, 2 * l + part)
                st.at(f"ada{l}.rows")
                st.at(f"ada{l}.transposed")
                st.at(f"ada{l}.ready")
            act.wait_ge(x_in, 32)
            for l in layers:
                act_norm(act, st, l)
                [act_mla, act_s5, act_gla][l % 3](act, st, l)
                act_out(act, st, l)

        def act_norm(act, st, l):
            for t in range(NT):
                nc.scalar.activation(sq_junk, x[:, t, :], ACT.Square, accum_out=ss[:, t:t + 1])
                nc.scalar.drain()
            nc.scalar.activation(rs, ss, ACT.Sqrt, scale=1.0 / D, bias=eps_c)
            st.at(f"norm{l}.stats")
            st.at(f"norm{l}.scales")
            st.at(f"norm{l}.scaled")
            for half in range(2):
                st.at(f"norm{l}.turned{half}")
                for k in range(8 * half, 8 * half + 8, 2):
                    for c, a, b in COND:
                        nc.scalar.activation(hT[:, k, a:b], banks[k % 8][:, a:b], ACT.Identity,
                                             scale=G_scale[:, k, c:c + 1], bias=mod[:, l, k, c:c + 1])
                st.at(f"norm{l}.copied{half}")

        def act_out(act, st, l):
            st.at(f"out{l}.gate")
            st.at(f"out{l}.gate_spread")
            for b in range(0, 8, 2):
                act_copy(gate_bc[:, b // 4, (b % 4) * 512:(b % 4 + 1) * 512], banks[b][:, :])
            st.at(f"out{l}.gate_copied")

            def write(i, u, half):
                act_copy(o_sb[:, 0, bass.ds(i * 1024 + u * GC, GC)], banks[4 * half][:, :])
                act_copy(o_sb[:, 1, bass.ds(i * 1024 + u * GC, GC)], banks[4 * half + 1][:, :])
            evacuate(act, nc.scalar, f"out{l}", 4, write)
            st.at(f"out{l}.projected")
            for t in range(NT):
                nc.scalar.activation(sq_junk, o_sb[:, t, :], ACT.Square, accum_out=ss[:, t:t + 1])
                nc.scalar.drain()
            nc.scalar.activation(rs, ss, ACT.Sqrt, scale=1.0 / D, bias=eps_c)
            st.at(f"out{l}.stats")
            st.at(f"out{l}.rstd")
            st.at(f"out{l}.scaled")
            st.at(f"out{l}.added")

        def act_mla(act, st, l):
            def q_write(i, u, half):
                act_copy(qn[:, bass.ds(i * 4 + 2 * u, 1), :], banks[4 * half][:, 0:TOK])
                act_copy(qn[:, bass.ds(i * 4 + 2 * u + 1, 1), :], banks[4 * half + 1][:, 0:TOK])
            evacuate(act, nc.scalar, f"q{l}", 8, q_write)

            def ckv_write(i, u, half):
                for t in range(NT):
                    act_copy(ckv_sb[:, t, :], banks[4 * half + t][:, :])
            evacuate(act, nc.scalar, f"ckv{l}", 1, ckv_write, share=2)

            def gate_write(i, u, half):
                for m in range(4):
                    nc.scalar.activation(gateT[:, bass.ds(i * 8 + 4 * u + m, 1), :], banks[4 * half + m][:, 0:TOK], ACT.Silu)
            evacuate(act, nc.scalar, f"gate{l}", 4, gate_write, share=2)
            for t in range(NT):
                nc.scalar.activation(qn_junk, ckv_sb[:, t, :], ACT.Square, accum_out=ss[:, t:t + 1])
                nc.scalar.drain()
            nc.scalar.activation(rs, ss, ACT.Sqrt, scale=1.0 / LORA, bias=eps_c)
            st.at(f"mix{l}.projected")
            st.at(f"mix{l}.kv_rstd")
            st.at(f"mix{l}.kv_normed")
            st.at(f"mix{l}.kv_transposed")
            for kt in range(0, 4, 2):
                act_copy(ckvT[:, kt, :], banks[kt][:, :])
            st.at(f"mix{l}.kv_copied")
            st.at(f"mix{l}.rotated")
            st.at(f"mix{l}.roped")
            for pair in range(8):
                act.wait_ge(kv_ready, 8 * nth(l) + pair + 1)
                if pair:
                    act.wait_ge(heads_ready, 16 * nth(l) + 2 * pair)
                act_copy(kT[:, 0, :], banks[4][:, :])
                act_copy(kT[:, 1, :], banks[5][:, :])
                nc.scalar.drain().then_inc(kv_copied, 1)
                for hh in range(2):
                    n = 16 * nth(l) + 2 * pair + hh
                    act.wait_ge(maxes_ready, n + 1)
                    for t in range(3):
                        a, b = seen(t)
                        nc.scalar.activation(p_sb[:, t, 0:b - a], banks[t][:, 0:b - a], ACT.Exp, scale=SM_SCALE,
                                             bias=mx[:, t:t + 1], accum_out=sm[:, t:t + 1])
                    nc.scalar.drain().then_inc(exps_ready, 1)
                    act.wait_ge(probsT_ready, n + 1)
                    act_copy(pT[:, 1:3, :], banks[1][:, :])
                    nc.scalar.drain().then_inc(probsT_copied, 1)
            st.at(f"mix{l}.attended")


        def dve_program(dve):
            st = Stages(nc.vector)
            nc.vector.memset(eps_c, EPS)
            dve.wait_ge(inputs_in, 16 * INPUT_LOADS)
            st.at("rows_in")
            st.at("rows_transposed")
            nc.vector.tensor_copy(vecs[:, :, :], banks[0][:, :].rearrange("p (a b) -> p a b", a=4))
            st.at("vectors_ready")
            st.at("silu_c")
            dve_s5_basics(dve, st)
            for l in range(DEPTH):
                for part in range(2):
                    dve_s5_batch(dve, 2 * l + part)
                st.at(f"ada{l}.rows")
                st.at(f"ada{l}.transposed")
                bias = vecs[:, 2 + l // 2, (l % 2) * 64:(l % 2) * 64 + 48]
                nc.vector.tensor_tensor(mod[:, l, :, :], banks[0][:, 0:96].rearrange("p (j c) -> p j c", c=2),
                                        bias.unsqueeze(2).broadcast_to([P, 48, 2]), ALU.add)
                st.at(f"ada{l}.ready")
            dve.wait_ge(x_in, 32)
            for l in layers:
                dve_norm(dve, st, l)
                [dve_mla, dve_s5, dve_gla][l % 3](dve, st, l)
                dve_out(dve, st, l)

        def dve_norm(dve, st, l):
            st.at(f"norm{l}.stats")
            nc.vector.reciprocal(rs, rs)
            nc.vector.scalar_tensor_tensor(out=G_scale, in0=mod[:, l, 16:32, :], scalar=1.0,
                                           in1=vec("norm_pre", 16 * l).unsqueeze(2).broadcast_to([P, KT, 2]),
                                           op0=ALU.add, op1=ALU.mult)
            st.at(f"norm{l}.scales")
            for t in range(NT):
                nc.vector.tensor_scalar(xn[:, t, :], x[:, t, :], rs[:, t:t + 1], None, ALU.mult)
            st.at(f"norm{l}.scaled")
            for half in range(2):
                st.at(f"norm{l}.turned{half}")
                for k in range(8 * half + 1, 8 * half + 8, 2):
                    for c, a, b in COND:
                        nc.vector.tensor_scalar(hT[:, k, a:b], banks[k % 8][:, a:b], G_scale[:, k, c:c + 1],
                                                mod[:, l, k, c:c + 1], ALU.mult, ALU.add)
                st.at(f"norm{l}.copied{half}")

        def dve_out(dve, st, l):
            nc.vector.tensor_tensor(G_small, mod[:, l, 32:48, :],
                                    vec("norm_post", 16 * l).unsqueeze(2).broadcast_to([P, KT, 2]), ALU.mult)
            st.at(f"out{l}.gate")
            st.at(f"out{l}.gate_spread")
            for b in range(1, 8, 2):
                nc.vector.tensor_copy(gate_bc[:, b // 4, (b % 4) * 512:(b % 4 + 1) * 512], banks[b][:, :])
            st.at(f"out{l}.gate_copied")

            def write(i, u, half):
                nc.vector.tensor_copy(o_sb[:, 2, bass.ds(i * 1024 + u * GC, GC)], banks[4 * half + 2][:, :])
            evacuate(dve, nc.vector, f"out{l}", 4, write)
            st.at(f"out{l}.projected")
            st.at(f"out{l}.stats")
            nc.vector.reciprocal(rs, rs)
            st.at(f"out{l}.rstd")
            for t in range(NT):
                nc.vector.scalar_tensor_tensor(out=o_sb[:, t, :], in0=o_sb[:, t, :], scalar=rs[:, t:t + 1],
                                               in1=gate_bc[:, TILE_COND[t], :], op0=ALU.mult, op1=ALU.mult)
            if l % 3:
                dve.wait_ge(x_back, 16 * xn_of(l))
            st.at(f"out{l}.scaled")
            for t in range(NT):
                nc.vector.tensor_tensor(x[:, t, :], x[:, t, :], o_sb[:, t, :], ALU.add)
            st.at(f"out{l}.added")

        def dve_mla(dve, st, l):
            def q_write(i, u, half):
                nc.vector.tensor_copy(qr[:, bass.ds(i * 2 + u, 1), :], banks[4 * half + 2][:, 0:TOK])
            evacuate(dve, nc.vector, f"q{l}", 8, q_write)

            def krope_write(i, u, half):
                for t in range(NT):
                    for d in range(2):
                        nc.vector.tensor_copy(kr_sb[:, t, d * ROPE:(d + 1) * ROPE], banks[4 * half + t][:, 0:ROPE])
            evacuate(dve, nc.vector, f"krope{l}", 1, krope_write, share=2)
            st.at(f"mix{l}.projected")
            nc.vector.reciprocal(rs, rs)
            st.at(f"mix{l}.kv_rstd")
            dve.wait_ge(small_in, 16 * MLA_LOADS * (nth(l) + 1))
            for t in range(NT):
                nc.vector.scalar_tensor_tensor(out=ckv_sb[:, t, :], in0=ckv_sb[:, t, :], scalar=rs[:, t:t + 1],
                                               in1=gamma, op0=ALU.mult, op1=ALU.mult)
            st.at(f"mix{l}.kv_normed")
            st.at(f"mix{l}.kv_transposed")
            for kt in range(1, 4, 2):
                nc.vector.tensor_copy(ckvT[:, kt, :], banks[kt][:, :])
            nc.vector.tensor_copy(krT, banks[4][:, :])
            st.at(f"mix{l}.kv_copied")
            st.at(f"mix{l}.rotated")
            for j in range(9):
                dst = qr[:, j, CTX:TOK] if j < 8 else krT[:, CTX:TOK]
                nc.vector.tensor_tensor(rope_tmp[:, j % 2, :], banks[j // 2][:, (j % 2) * LAT:(j % 2 + 1) * LAT], sin_t, ALU.mult)
                nc.vector.tensor_tensor(dst, dst, cos_t, ALU.mult)
                nc.vector.drain()
                nc.vector.tensor_tensor(dst, dst, rope_tmp[:, j % 2, :], ALU.add)
            dve.wait_ge(stored, 32 * (nth(l) + 1))
            st.at(f"mix{l}.roped")
            for pair in range(8):
                dve.wait_ge(kv_ready, 8 * nth(l) + pair + 1)
                if pair:
                    dve.wait_ge(heads_ready, 16 * nth(l) + 2 * pair)
                for t in range(2):
                    nc.vector.tensor_copy(v_sb[:, 2 * t:2 * t + 2, :], banks[6 + t][:, :].rearrange("p (a b) -> p a b", a=2))
                nc.vector.drain().then_inc(kv_copied, 1)
                for hh in range(2):
                    h = 2 * pair + hh
                    n = 16 * nth(l) + h
                    dve.wait_ge(scores_ready, n + 1)
                    if h:
                        dve.wait_ge(exps_ready, n)
                    for t in range(3):
                        a, b = seen(t)
                        nc.vector.reduce_max(mx[:, 4 + t:5 + t], banks[t][:, 0:b - a], AX.X)
                    nc.vector.drain()
                    nc.vector.tensor_scalar(mx[:, 0:3], mx[:, 4:7], -SM_SCALE, None, ALU.mult)
                    nc.vector.drain().then_inc(maxes_ready, 1)
                    dve.wait_ge(exps_ready, n + 1)
                    nc.vector.reciprocal(sm[:, 4:7], sm[:, 0:3])
                    nc.vector.drain()
                    for t in range(3):
                        a, b = seen(t)
                        nc.vector.tensor_scalar(p_sb[:, t, 0:b - a], p_sb[:, t, 0:b - a], sm[:, 4 + t:5 + t], None, ALU.mult)
                    nc.vector.drain().then_inc(probs_ready, 1)
                    dve.wait_ge(probsT_ready, n + 1)
                    nc.vector.tensor_copy(pT[:, 0, 0:P], banks[0][:, 0:P])
                    nc.vector.tensor_copy(pT[:, 3, :], banks[2][:, 0:LAT])
                    nc.vector.drain().then_inc(probsT_copied, 1)
                    dve.wait_ge(heads_ready, n + 1)
                    nc.vector.tensor_tensor(hT[:, h, :], banks[3][:, 0:TOK], gateT[:, h, :], ALU.mult)
                    nc.vector.drain().then_inc(heads_done, 1)
            for half in range(2):
                nc.vector.sem_inc(sums_taken[half], 2)
            st.at(f"mix{l}.attended")




        g_q = view(0, 8, TOK)
        g_k = view(3072, 8, TOK)
        g_v = view(6144, NT, D)
        g_r = view(12288, KT, TOK)
        g_glr = view(18432, TOK)
        g_w2 = view(18816, 2, GH * GDK)
        g_mask = view(20864, 2, P)
        g_edge = view(21120, TOK)
        g_gamma = view(21504, GDV)
        g_dn = view(22016, 2, 6)
        g_stat = view(22028, 8)
        g_qt = view(18432, 2, TOK)
        g_kt = view(19200, 2, TOK)
        g_kd = view(19968, 2, TOK)
        x_flat = x[:, :, :].rearrange("p a b -> p (a b)")
        g_o = x_flat[:, 0:1536].rearrange("p (a b) -> p a b", a=3)
        g_att = x_flat[:, 1536:2304].rearrange("p (d a b) -> p d a b", d=2, a=3)
        g_kdT = x_flat[:, 2304:3072].rearrange("p (a b) -> p a b", a=3)
        g_sc = x_flat[:, 3072:4096].rearrange("p (a b) -> p a b", a=2)
        g_sl = x_flat[:, 4096:6144].rearrange("p (n a b) -> p n a b", n=2, a=2)
        hT_flat = hT[:, :, :].rearrange("p a b -> p (a b)")

        def g_gate(h, d):
            return hT[:, 4 * h + 2 * d:4 * h + 2 * d + 2, :]

        x_saved = sem("x_saved")
        x_back = sem("x_back")
        g_small = sem("g_small")
        g_state_in = [sem("g_state_in0"), sem("g_state_in1")]
        g_cum_ready = sem("g_cum_ready")
        g_exp_ready = sem("g_exp_ready")
        g_decayed = sem("g_decayed")
        g_att_ready = sem("g_att_ready")
        g_att_copied = sem("g_att_copied")
        g_upd_ready = sem("g_upd_ready")
        g_state_new = sem("g_state_new")
        g_unit_done = sem("g_unit_done")
        g_ctx_stored = sem("g_ctx_stored")
        g_o_normed = sem("g_o_normed")
        g_ssq_ready = sem("g_ssq_ready")
        g_o_turned = sem("g_o_turned")
        g_head_done = sem("g_head_done")

        def g_steps(d):
            c = [("c", 0, b) for b in ((0, 1), (1, 0))[d]]
            l_ = [("l", t, b) for t in ((1, 2), (2, 1))[d] for b in ((0, 1), (1, 0))[d]]
            order = [c[0], l_[0], c[1], l_[1], l_[2], l_[3]]
            return [(k, t, b, (k, t, b) in (c[0], l_[0]), (k, t, b) == l_[-1]) for k, t, b in order]

        UPD = 5

        def pe_gla(pe, st, l):
            for name, groups in (("q", 2), ("k", 2)):
                def body(i, g0, u):
                    group_sums(pe, i, g0, u, [P] * 4, moving=hT)
                loop_groups(nc.tensor, f"{name}{l}", groups, body)

            def v_body(i, g0, u):
                group_sums(pe, i, g0, u, None, row_tiles=token_tiles)
            loop_groups(nc.tensor, f"v{l}", 4, v_body)

            def r_body(i, g0, u):
                group_sums(pe, i, g0, u, [P] * 4, moving=hT)
            loop_groups(nc.tensor, f"r{l}", 4, r_body)
            group_sums(pe, 0, FIRST_GROUP[f"glr{l}"], 0, [2 * GRANK], moving=hT)
            st.at(f"mix{l}.projected")
            pe.wait_ge(g_small, 16 * 5)
            for d in range(2):
                for t in range(8):
                    nc.tensor.matmul(banks[t][:, 0:TOK], g_w2[0:2 * GRANK, d, t * P:(t + 1) * P],
                                     g_glr[0:2 * GRANK, :], start=True, stop=True)
                st.at(f"mix{l}.z{d}")
                st.at(f"mix{l}.z_taken{d}")
            for s in ("abs", "softplus", "log_gates"):
                st.at(f"mix{l}.{s}")
            for h in range(GH):
                vh = slice(h * GDV, (h + 1) * GDV)
                for d in range(2):
                    n = 2 * h + d
                    pe.wait_ge(g_decayed, n + 1)
                    if n:
                        pe.wait_ge(g_state_new, UPD * n)
                    for t in range(NT):
                        for j in range(2):
                            at = (2 * t + j) * P
                            nc.tensor.transpose(banks[at // 512][:, at % 512:at % 512 + P],
                                                g_kd[:, j, t * P:(t + 1) * P], ident[:, :])
                    for t in range(NT):
                        for j in range(2):
                            nc.tensor.matmul(banks[2][:, t * P:(t + 1) * P], g_kt[:, j, t * P:(t + 1) * P],
                                             g_qt[:, j, t * P:(t + 1) * P], start=(j == 0), stop=(j == 1))
                    nc.tensor.drain().then_inc(g_att_ready, 1)
                    pe.wait_ge(g_att_copied, 2 * (n + 1))
                    if d == 0 and h:
                        pe.wait_ge(g_o_normed, h)
                    pe.wait_ge(g_state_in[n % 2], 16 * (n // 2 + 1))
                    for t in range(NT):
                        nc.tensor.matmul(banks[3 + t][:, :], g_att[:, d, t, :], g_v[:, t, vh],
                                         start=(d == 0), stop=False, skip_group_check=True)
                    done = {"c": 0, "l": 0}
                    m = 0
                    for step, (chain, t, b, first, last) in enumerate(g_steps(d)):
                        rows = slice(b * GCH, (b + 1) * GCH)
                        toks = slice(t * P + b * GCH, t * P + (b + 1) * GCH)
                        if not first:
                            pe.wait_ge(g_state_new, UPD * n + done[chain])
                        if not (first and chain == "c"):
                            state = g_sc if chain == "c" else g_sl[:, n % 2, :, :]
                            for j in range(2):
                                nc.tensor.matmul(banks[3 + t][rows, :], g_qt[:, j, toks], state[:, j, :],
                                                 start=False, stop=True, skip_group_check=True)
                        if not last:
                            pair = (6, 0)[m % 2]
                            if m >= 2:
                                pe.wait_ge(g_state_new, UPD * n + m - 1)
                            for j in range(2):
                                nc.tensor.matmul(banks[pair + j][:, :], g_kdT[rows, t, j * P:(j + 1) * P],
                                                 g_v[rows, t, vh], start=True, stop=True)
                            nc.tensor.drain().then_inc(g_upd_ready, 1)
                            m += 1
                            done[chain] = m
                    nc.tensor.drain().then_inc(g_unit_done, 1)
                pe.wait_ge(g_o_normed, h + 1)
                pe.wait_ge(g_state_new, UPD * (2 * h + 2))
                for q in range(4):
                    for t in range(NT):
                        nc.tensor.transpose(banks[(0, 1, 2, 6)[q]][:, t * P:(t + 1) * P],
                                            g_o[:, t, q * P:(q + 1) * P], ident[:, :])
                nc.tensor.drain().then_inc(g_o_turned, 1)
                pe.wait_ge(g_head_done, h + 1)
            st.at(f"mix{l}.attended")

        def act_gla(act, st, l):
            for name, dst in (("q", g_q), ("k", g_k)):
                def write(i, u, half, dst=dst):
                    for m in range(2):
                        act_copy(dst[:, 4 * u + m, :], banks[4 * half + m][:, 0:TOK])
                evacuate(act, nc.scalar, f"{name}{l}", 2, write)

            def v_write(i, u, half):
                for t in range(2):
                    act_copy(g_v[:, t, bass.ds(i * 1024 + u * GC, GC)], banks[4 * half + t][:, :])
            evacuate(act, nc.scalar, f"v{l}", 4, v_write)

            def r_write(i, u, half):
                for m in range(4):
                    nc.scalar.activation(g_r[:, bass.ds(i * 8 + 4 * u + m, 1), :], banks[4 * half + m][:, 0:TOK], ACT.Silu)
            evacuate(act, nc.scalar, f"r{l}", 4, r_write, share=2)
            st.at(f"mix{l}.projected")
            for s in ("z0", "z_taken0", "z1", "z_taken1", "abs"):
                st.at(f"mix{l}.{s}")
            nc.scalar.activation(x_flat, x_flat, ACT.Exp)
            nc.scalar.drain()
            nc.scalar.activation(x_flat, x_flat, ACT.Ln, bias=1.0)
            st.at(f"mix{l}.softplus")
            st.at(f"mix{l}.log_gates")
            S = 1.0 / GATE_NORM
            for h in range(GH):
                for d in range(2):
                    n = 2 * h + d
                    act.wait_ge(g_cum_ready, n + 1)
                    if n:
                        act.wait_ge(g_unit_done, n)
                    b = g_gate(h, d)
                    nc.scalar.activation(g_qt, b, ACT.Exp, scale=S)
                    nc.scalar.activation(g_kt, b, ACT.Exp, scale=-S)
                    nc.scalar.activation(g_kd, g_kd, ACT.Exp, scale=S)
                    edge = (GCH - 1, 0)[d]
                    nc.scalar.activation(g_dn, b[:, :, edge::GCH], ACT.Exp, scale=S)
                    nc.scalar.drain().then_inc(g_exp_ready, 1)
                    act.wait_ge(g_att_ready, n + 1)
                    act_copy(g_kdT[:, 0:2, :], banks[0][:, :].rearrange("p (a b) -> p a b", a=2))
                    act_copy(g_kdT[:, 2, :], banks[1][:, 0:2 * P])
                    nc.scalar.drain().then_inc(g_att_copied, 1)
                act.wait_ge(g_unit_done, 2 * h + 2)
                if h:
                    act.wait_ge(g_head_done, h)
                for t in range(NT):
                    nc.scalar.activation(g_o[:, t, :], banks[3 + t][:, :], ACT.Square, accum_out=g_stat[:, t:t + 1])
                nc.scalar.drain()
                nc.scalar.activation(g_stat[:, 3:6], g_stat[:, 0:3], ACT.Sqrt, scale=1.0 / GDV, bias=eps_c)
                nc.scalar.drain().then_inc(g_ssq_ready, 1)
            st.at(f"mix{l}.attended")

        def dve_gla(dve, st, l):
            for name, dst in (("q", g_q), ("k", g_k)):
                def write(i, u, half, dst=dst):
                    for m in range(2, 4):
                        nc.vector.tensor_copy(dst[:, 4 * u + m, :], banks[4 * half + m][:, 0:TOK])
                evacuate(dve, nc.vector, f"{name}{l}", 2, write)

            def v_write(i, u, half):
                nc.vector.tensor_copy(g_v[:, 2, bass.ds(i * 1024 + u * GC, GC)], banks[4 * half + 2][:, :])
            evacuate(dve, nc.vector, f"v{l}", 4, v_write)

            def glr_write(i, u, half):
                nc.vector.tensor_copy(g_glr[0:2 * GRANK, :], banks[4 * half][0:2 * GRANK, 0:TOK])
            evacuate(dve, nc.vector, f"glr{l}", 1, glr_write, share=2)
            st.at(f"mix{l}.projected")
            dve.wait_ge(x_saved, 16 * xn_of(l))
            for d in range(2):
                st.at(f"mix{l}.z{d}")
                for t in range(8):
                    nc.vector.tensor_scalar(hT[:, 4 * (t // 2) + 2 * d + t % 2, :], banks[t][:, 0:TOK],
                                            vec("gla_b_g", 8 * d + t, 1), None, ALU.add)
                st.at(f"mix{l}.z_taken{d}")
            nc.vector.scalar_tensor_tensor(out=x_flat, in0=hT_flat, scalar=-1.0, in1=hT_flat, op0=ALU.mult, op1=ALU.min)
            st.at(f"mix{l}.abs")
            st.at(f"mix{l}.softplus")
            nc.vector.scalar_tensor_tensor(out=hT_flat, in0=hT_flat, scalar=0.0, in1=x_flat, op0=ALU.min,
                                           op1=ALU.subtract)
            st.at(f"mix{l}.log_gates")
            nc.vector.memset(g_att, 0.0)
            nc.vector.drain()
            for h in range(GH):
                for d in range(2):
                    n = 2 * h + d
                    b = g_gate(h, d)
                    for j in range(2):
                        if d == 0:
                            nc.vector.tensor_tensor_scan(b[:, j, :], g_edge, b[:, j, :], 0.0, ALU.mult, ALU.add)
                        else:
                            nc.vector.tensor_tensor_scan(b[:, j, ::-1], g_edge, b[:, j, ::-1], 0.0, ALU.mult, ALU.add)
                    nc.vector.drain()
                    if n:
                        dve.wait_ge(g_unit_done, n)
                    edge = (GCH - 1, 0)[d]
                    for j in range(2):
                        bj = b[:, j, :].rearrange("p (c t) -> p c t", t=GCH)
                        nc.vector.tensor_tensor(g_kd[:, j, :].rearrange("p (c t) -> p c t", t=GCH),
                                                bj[:, :, edge:edge + 1].broadcast_to([P, 6, GCH]), bj, ALU.subtract)
                    nc.vector.drain().then_inc(g_cum_ready, 1)
                    dve.wait_ge(g_exp_ready, n + 1)
                    qh, kh = g_q[:, 2 * h:2 * h + 2, :], g_k[:, 2 * h:2 * h + 2, :]
                    nc.vector.scalar_tensor_tensor(out=g_qt, in0=g_qt, scalar=GDK ** -0.5, in1=qh, op0=ALU.mult,
                                                   op1=ALU.mult)
                    nc.vector.tensor_tensor(g_kt, g_kt, kh, ALU.mult)
                    nc.vector.tensor_tensor(g_kd, g_kd, kh, ALU.mult)
                    nc.vector.drain().then_inc(g_decayed, 1)
                    dve.wait_ge(g_att_ready, n + 1)
                    nc.vector.copy_predicated(g_att[:, d, :, :], g_mask[:, d, :].bitcast(U32).unsqueeze(1).broadcast_to([P, 3, P]),
                                              banks[2][:, 0:TOK].rearrange("p (a b) -> p a b", a=3))
                    nc.vector.drain().then_inc(g_att_copied, 1)
                    m = 0
                    for chain, t, bb, first, last in g_steps(d):
                        if last:
                            continue
                        dve.wait_ge(g_upd_ready, UPD * n + m + 1)
                        state = g_sc if chain == "c" else g_sl[:, n % 2, :, :]
                        pair = (6, 0)[m % 2]
                        c = 2 * t + bb
                        if first and chain == "c" and n:
                            dve.wait_ge(g_ctx_stored, 16 * n)
                        for j in range(2):
                            if first and chain == "c":
                                nc.vector.tensor_copy(state[:, j, :], banks[pair + j][:, :])
                            else:
                                nc.vector.scalar_tensor_tensor(out=state[:, j, :], in0=state[:, j, :],
                                                               scalar=g_dn[:, j, c:c + 1], in1=banks[pair + j][:, :],
                                                               op0=ALU.mult, op1=ALU.add)
                        nc.vector.drain().then_inc(g_state_new, 1)
                        m += 1
                dve.wait_ge(g_ssq_ready, h + 1)
                nc.vector.reciprocal(g_stat[:, 3:6], g_stat[:, 3:6])
                nc.vector.drain()
                for t in range(NT):
                    nc.vector.scalar_tensor_tensor(out=g_o[:, t, :], in0=banks[3 + t][:, :], scalar=g_stat[:, 3 + t:4 + t],
                                                   in1=g_gamma, op0=ALU.mult, op1=ALU.mult)
                nc.vector.drain().then_inc(g_o_normed, 1)
                dve.wait_ge(g_o_turned, h + 1)
                for q in range(4):
                    nc.vector.tensor_tensor(hT[:, 4 * h + q, :], banks[(0, 1, 2, 6)[q]][:, 0:TOK], g_r[:, 4 * h + q, :],
                                            ALU.mult)
                nc.vector.drain().then_inc(g_head_done, 1)
            st.at(f"mix{l}.attended")

        def xn_of(l):
            return sum(1 for m in layers if m <= l and m % 3)

        def pool_gla(pool, l):
            pool.wait_ge(stage_done, after(f"norm{l}.copied1"))
            nc.gpsimd.dma_start(x_dram.rearrange("t p d -> p t d"), x[:, :, :]).then_inc(x_saved, 16)
            nc.gpsimd.memset(g_w2[0:2 * GRANK, :, :], 0.0).then_inc(g_w2_zero, 1)
            pool.wait_ge(g_w2_zero, 1)
            for d in range(2):
                nc.gpsimd.dma_start(g_w2[d * GRANK:(d + 1) * GRANK, d, :], w["gla_w_g2"][0, d]).then_inc(g_small, 16)
            nc.gpsimd.dma_start(g_mask, consts["gla_mask"]).then_inc(g_small, 16)
            nc.gpsimd.dma_start(g_edge, consts["gla_edge"]).then_inc(g_small, 16)
            nc.gpsimd.dma_start(g_gamma, w["gla_norm"][0:1, :].broadcast_to([P, GDV])).then_inc(g_small, 16)
            pool.wait_ge(stage_done, after(f"mix{l}.log_gates"))
            for n in range(2 * GH):
                h, d = n // 2, n % 2
                if n >= 2:
                    pool.wait_ge(g_unit_done, n - 1)
                nc.gpsimd.dma_start(g_sl[:, n % 2, :, :], w["state_gla"][0, 0, d, h].rearrange("(a p) v -> p a v", p=P))\
                    .then_inc(g_state_in[n % 2], 16)
                if n:
                    pool_store_state(pool, n - 1)
            pool_store_state(pool, 2 * GH - 1)
            pool.wait_ge(g_ctx_stored, 16 * 2 * GH)
            pool.wait_ge(stage_done, after(f"mix{l}.attended"))
            nc.gpsimd.dma_start(x[:, :, :], x_dram.rearrange("t p d -> p t d")).then_inc(x_back, 16)

        def pool_store_state(pool, n):
            pool.wait_ge(g_state_new, UPD * n + 3)
            nc.gpsimd.dma_start(outs[5][0, 0, n % 2, n // 2].rearrange("(a p) v -> p a v", p=P), g_sc)\
                .then_inc(g_ctx_stored, 16)

        g_w2_zero = sem("g_w2_zero")
        x_dram = nc.dram_tensor("x_saved_dram", (NT, P, D), F32, kind="Internal").ap()


        x_in = sem("x_in")
        hT_words = hT[:, :, :].rearrange("p a b -> p (a b)")
        x_words = x[:, :, :].rearrange("p a b -> p (a b)")
        DG = P
        b_st = hT_words[:, 0:4096].rearrange("p (r q g) -> p r q g", r=2, q=SC)
        bd = hT_words[:, 4096:5120].rearrange("p (r d g m) -> p r d g m", r=2, d=2, g=8)
        c_st = x_words[:, 0:4096].rearrange("p (r g q) -> p r g q", r=2, q=SC)
        kw = x_words[0:32, 4096:4096 + 1920].rearrange("p (g n) -> p g n", g=8)
        diag = hT_words[0:32, 5120:5136]
        d_st = hT_words[0:32, 5136:5200]
        pw = view(6144, 2, 9, DG)
        wb = view(8448, 2, 2, 8, 128)
        ca = view(12544, 2, 2, 8, 144)
        wbt = view(17152, 8, 2, 4, SN)
        s5_t = view(21248, 1152)
        rowb = view(8448, 2, 2048)
        rowc = view(12544, 2, 2, 16, SN)
        bbar = view(16640, 2, 2048)
        rowt = view(0, 6144)
        def row(n, k=1):
            return rowt[:, n * P:(n + k) * P]
        a_re, a_im, dt2 = row(0), row(1), rowt[:, 256:258]
        er, th, kk_, sn, cs = row(3), row(4), row(5, 2), row(7), row(8)
        f_re, f_im, den, tr = row(9), row(10), row(11), row(12)
        pr = rowt[:, 13 * P:13 * P + 18 * P].rearrange("p (r k n) -> p r k n", r=2, k=9)
        tp = rowt[:, 31 * P:39 * P]
        a8 = sb("a8", [P, 3, DG])
        s5_loaded = sem("s5_loaded")
        s5_ready = sem("s5_ready")
        s5_turned = sem("s5_turned")
        s5_turned_copied = sem("s5_turned_copied")
        s5_k_ready = sem("s5_k_ready")
        s5_k_copied = sem("s5_k_copied")
        s5_k_done = sem("s5_k_done")
        s5_stored = sem("s5_stored")
        wbt_dram = nc.dram_tensor("s5_in_dram", (16, P, 2048), F32, kind="Internal").ap()
        ca_dram = nc.dram_tensor("s5_out_dram", (8, P, 4, 8, 128), F32, kind="Internal").ap()
        k_dram = nc.dram_tensor("s5_k_dram", (SG, SC, 240), F32, kind="Internal").ap()
        ud_dram = nc.dram_tensor("s5_u_dram", (D, TOK), F32, kind="Internal").ap()
        gate_dram = nc.dram_tensor("s5_gate_dram", (P, KT * TOK), F32, kind="Internal").ap()

        def pool_s5_basics(pool):
            pool.wait_ge(stage_done, after("silu_c"))
            ld = lambda dst, src: nc.gpsimd.dma_start(dst, src).then_inc(s5_loaded, 16)
            ld(a_re, w["s5_a_re"].rearrange("b d (g h) n -> (b d g) (h n)", h=2))
            ld(a_im, w["s5_a_im"].rearrange("b d (g h) n -> (b d g) (h n)", h=2))
            ld(dt2, w["s5_log_dt"].rearrange("b d (g h) -> (b d g) h", h=2))
            for r, (bn, cn) in enumerate((("s5_b_re", "s5_c_re"), ("s5_b_im", "s5_c_im"))):
                ld(rowb[:, r, :], w[bn].rearrange("b d (g h) n p -> (b d g) (h n p)", h=2))
                for d in range(2):
                    ld(rowc[:, r, d, :, :], w[cn][0, d].rearrange("(t g) p n -> (g p) t n", g=8))
            for g2 in range(2):
                ld(diag[16 * g2:16 * g2 + 16, :], consts["ident"][0:16, 0:16])

        S5_LOADS = 11

        def pe_s5_basics(pe, st):
            for s in ("loaded", "dt", "angle", "reduced", "sines", "poles"):
                st.at(f"s5.{s}")
            for a in range(4):
                nc.tensor.matmul(banks[7][0:32, a * KT:(a + 1) * KT], ident[:, 32 * a:32 * a + 32], vec("d"),
                                 start=True, stop=True)
            for n in range(3):
                for m in range(6):
                    i = 6 * n + m
                    nc.tensor.transpose(banks[m // 4][:, (m % 4) * P:(m % 4 + 1) * P], pr[:, i // 9, i % 9, :], ident[:, :])
                st.at(f"s5.turned_pow{n}")
                st.at(f"s5.copied_pow{n}")
            for n in range(4):
                for m in range(8):
                    i = 8 * n + m
                    r, q = i // SC, i % SC
                    nc.tensor.transpose(banks[m // 4][:, (m % 4) * P:(m % 4 + 1) * P],
                                        bbar[:, r, q::SC], ident[:, :])
                st.at(f"s5.turned_b{n}")
                st.at(f"s5.copied_b{n}")
            for n in range(4):
                r, d = n // 2, n % 2
                for t in range(16):
                    for g2 in range(2):
                        cols = ident[:, :].rearrange("p (a h q) -> p a h q", h=2, q=SC)[:, :, g2, :]
                        nc.tensor.matmul(banks[t // 8][g2 * 64:(g2 + 1) * 64, (t % 8) * 64:(t % 8 + 1) * 64],
                                         rowc[:, r, d, t, :], cols, start=True, stop=True)
                st.at(f"s5.turned_c{n}")
                st.at(f"s5.copied_c{n}")

        def act_s5_basics(act, st):
            st.at("s5.loaded")
            act.wait_ge(s5_loaded, 16 * S5_LOADS)
            nc.scalar.activation(dt2, dt2, ACT.Exp)
            st.at("s5.dt")
            st.at("s5.angle")
            nc.scalar.activation(er, er, ACT.Exp)
            st.at("s5.reduced")
            nc.scalar.activation(sn, sn, ACT.Sin)
            nc.scalar.activation(cs, cs, ACT.Sin)
            st.at("s5.sines")
            st.at("s5.poles")
            for n in range(3):
                st.at(f"s5.turned_pow{n}")
                st.at(f"s5.copied_pow{n}")
            for n in range(4):
                st.at(f"s5.turned_b{n}")
                i = 8 * n
                act_copy(b_st[:, i // SC, i % SC:i % SC + 4, :], banks[0][:, :].rearrange("p (a b) -> p a b", a=4))
                act_copy(b_st[:, i // SC, i % SC + 4:i % SC + 8, :], banks[1][:, :].rearrange("p (a b) -> p a b", a=4))
                st.at(f"s5.copied_b{n}")
            for n in range(4):
                st.at(f"s5.turned_c{n}")
                r, d = n // 2, n % 2
                for k in range(2):
                    act_copy(c_st[:, r, d * 64 + k * 32:d * 64 + k * 32 + 32, :],
                             banks[k][:, :].rearrange("p (a b) -> p a b", b=SC))
                st.at(f"s5.copied_c{n}")

        def cmul(out_re, out_im, ar_, ai_, br, bi, t):
            v = nc.vector
            v.tensor_tensor(out_re, ar_, br, ALU.mult)
            v.tensor_tensor(t, ai_, bi, ALU.mult)
            v.drain()
            v.tensor_tensor(out_re, out_re, t, ALU.subtract)
            v.tensor_tensor(out_im, ar_, bi, ALU.mult)
            v.drain()
            v.tensor_tensor(t, ai_, br, ALU.mult)
            v.drain()
            v.tensor_tensor(out_im, out_im, t, ALU.add)
            v.drain()

        TWO_PI = 2 * np.pi
        PI_HI = float(np.float32(6.28125))
        PI_MID = float(np.float32(TWO_PI - 6.28125))
        PI_LO = float(np.float32(TWO_PI - 6.28125 - np.float64(np.float32(TWO_PI - 6.28125))))
        ROUND = float(np.float32(1.5 * 2 ** 23))
        PI_IN = float(np.nextafter(np.float32(np.pi), np.float32(0)))

        def dve_s5_basics(dve, st):
            v = nc.vector
            v.memset(bd, 0.0)
            st.at("s5.loaded")
            dve.wait_ge(s5_loaded, 16 * S5_LOADS)
            st.at("s5.dt")
            dtb = dt2.unsqueeze(2).broadcast_to([P, 2, SN])
            v.tensor_tensor(er.rearrange("p (h n) -> p h n", h=2), a_re.rearrange("p (h n) -> p h n", h=2), dtb, ALU.mult)
            v.tensor_tensor(th.rearrange("p (h n) -> p h n", h=2), a_im.rearrange("p (h n) -> p h n", h=2), dtb, ALU.mult)
            st.at("s5.angle")
            for out, quarter, k in ((sn, 0.0, kk_[:, 0:P]), (cs, 0.25, kk_[:, P:2 * P])):
                v.tensor_scalar(k, th, 1.0 / TWO_PI, quarter, ALU.mult, ALU.add)
                v.drain()
                v.tensor_scalar(k, k, ROUND, None, ALU.add)
                v.drain()
                v.tensor_scalar(k, k, -ROUND, None, ALU.add)
                v.drain()
                v.scalar_tensor_tensor(out=out, in0=k, scalar=-PI_HI, in1=th, op0=ALU.mult, op1=ALU.add)
                v.drain()
                v.scalar_tensor_tensor(out=out, in0=k, scalar=-PI_MID, in1=out, op0=ALU.mult, op1=ALU.add)
                v.drain()
                v.scalar_tensor_tensor(out=out, in0=k, scalar=-PI_LO, in1=out, op0=ALU.mult, op1=ALU.add)
                v.drain()
                if quarter:
                    v.tensor_scalar(out, out, float(np.pi / 2), None, ALU.add)
                    v.drain()
                v.tensor_scalar(out, out, PI_IN, -PI_IN, ALU.min, ALU.max)
            st.at("s5.reduced")
            st.at("s5.sines")
            one = pr[:, 0, 0, :]
            v.memset(one, 1.0)
            v.memset(pr[:, 1, 0, :], 0.0)
            v.tensor_tensor(pr[:, 0, 1, :], er, cs, ALU.mult)
            v.tensor_tensor(pr[:, 1, 1, :], er, sn, ALU.mult)
            v.tensor_tensor(den, a_re, a_re, ALU.mult)
            v.tensor_tensor(tr, a_im, a_im, ALU.mult)
            v.drain()
            v.tensor_tensor(den, den, tr, ALU.add)
            v.drain()
            v.reciprocal(den, den)
            v.tensor_scalar(tr, pr[:, 0, 1, :], -1.0, None, ALU.add)
            v.drain()
            v.tensor_tensor(f_re, tr, a_re, ALU.mult)
            v.tensor_tensor(tp[:, 0:P], pr[:, 1, 1, :], a_im, ALU.mult)
            v.tensor_tensor(f_im, pr[:, 1, 1, :], a_re, ALU.mult)
            v.tensor_tensor(tp[:, P:2 * P], tr, a_im, ALU.mult)
            v.drain()
            v.tensor_tensor(f_re, f_re, tp[:, 0:P], ALU.add)
            v.tensor_tensor(f_im, f_im, tp[:, P:2 * P], ALU.subtract)
            v.drain()
            v.tensor_tensor(f_re, f_re, den, ALU.mult)
            v.tensor_tensor(f_im, f_im, den, ALU.mult)
            v.drain()
            for lo, n in ((1, 1), (1, 2), (1, 4)):
                by = n
                def pow_(r, k0, k):
                    return pr[:, r, k0:k0 + k, :]
                def rep_(r):
                    return pr[:, r, by:by + 1, :].broadcast_to([P, n, P])
                cmul(pow_(0, n + 1, n), pow_(1, n + 1, n), pow_(0, 1, n), pow_(1, 1, n), rep_(0), rep_(1),
                     tp[:, 0:n * P].rearrange("p (k n) -> p k n", k=n))
            fb = [f.unsqueeze(2).broadcast_to([P, P, SC]) for f in (f_re, f_im)]
            rb = [rowb[:, r, :].rearrange("p (n q) -> p n q", q=SC) for r in range(2)]
            bb = [bbar[:, r, :].rearrange("p (n q) -> p n q", q=SC) for r in range(2)]
            cmul(bb[0], bb[1], fb[0], fb[1], rb[0], rb[1], view(20736, P, SC))
            st.at("s5.poles")
            for n in range(3):
                st.at(f"s5.turned_pow{n}")
                if n == 0:
                    v.tensor_copy(d_st.rearrange("p (t a) -> p a t", a=4),
                                  banks[7][0:32, 0:64].rearrange("p (a t) -> p a t", a=4))
                for m in range(6):
                    i = 6 * n + m
                    v.tensor_copy(pw[:, i // 9, i % 9, :], banks[m // 4][:, (m % 4) * P:(m % 4 + 1) * P])
                st.at(f"s5.copied_pow{n}")
            v.tensor_copy(a8[:, 0, :], pw[:, 0, 8, :])
            v.tensor_scalar(a8[:, 1, :], pw[:, 1, 8, :], -1.0, None, ALU.mult)
            v.tensor_copy(a8[:, 2, :], pw[:, 1, 8, :])
            for n in range(4):
                st.at(f"s5.turned_b{n}")
                st.at(f"s5.copied_b{n}")
            for n in range(4):
                st.at(f"s5.turned_c{n}")
                st.at(f"s5.copied_c{n}")

        def dve_s5_batch(dve, b):
            v = nc.vector
            if b:
                dve.wait_ge(s5_turned, 8 * b)
                dve.wait_ge(s5_stored, 16 * 7 * b)
            for d in range(2):
                g0 = 64 * d + 8 * b
                def powers(r, ks, n):
                    return pw[:, r, ks, g0:g0 + 8].rearrange("p k g -> p g k").unsqueeze(3).broadcast_to([P, 8, n, SC])
                ks = slice(7, None, -1) if d == 0 else slice(0, 8)
                bsrc = [b_st[:, r, :, g0:g0 + 8].rearrange("p q g -> p g q").unsqueeze(2).broadcast_to([P, 8, 8, SC])
                        for r in range(2)]
                o = [wb[:, r, d, :, :].rearrange("p g (j q) -> p g j q", j=8) for r in range(2)]
                t = s5_t[:, 0:1024].rearrange("p (g j q) -> p g j q", g=8, j=8)
                cmul(o[0], o[1], powers(0, ks, 8), powers(1, ks, 8), bsrc[0], bsrc[1], t)
                ks = slice(0, 9) if d == 0 else slice(8, None, -1)
                csrc = [c_st[:, r, g0:g0 + 8, :].unsqueeze(2).broadcast_to([P, 8, 9, SC]) for r in range(2)]
                o = [ca[:, r, d, :, :].rearrange("p g (j q) -> p g j q", j=9) for r in range(2)]
                t = s5_t[:, 0:1152].rearrange("p (g j q) -> p g j q", g=8, j=9)
                cmul(o[0], o[1], powers(0, ks, 9), powers(1, ks, 9), csrc[0], csrc[1], t)
                v.tensor_scalar(ca[:, 1, d, :, :], ca[:, 1, d, :, :], -1.0, None, ALU.mult)
                for r in range(2):
                    for g2 in range(2):
                        rows = slice(64 * g2, 64 * g2 + 64)
                        v.tensor_copy(bd[rows, r, d, :, 16 * g2:16 * g2 + 16],
                                      b_st[rows, r, :, g0:g0 + 8].rearrange("p q g -> p g q"))
            v.drain().then_inc(s5_ready, 1)
            for n in range(4):
                dve.wait_ge(s5_k_ready, 4 * b + n + 1)
                v.tensor_copy(kw[:, 2 * n:2 * n + 2, :],
                              banks[K_BANKS[n % 2]][0:32, :].rearrange("p (a b) -> p a b", a=2)[:, :, 0:240])
                v.drain().then_inc(s5_k_copied, 1)
            t = s5_t[0:32, 0:128].rearrange("p (g q) -> p g q", g=8)
            v.tensor_tensor(t, d_st[:, 8 * b:8 * b + 8].unsqueeze(2).broadcast_to([32, 8, SC]),
                            diag.unsqueeze(1).broadcast_to([32, 8, SC]), ALU.mult)
            v.drain()
            v.tensor_tensor(kw[:, :, 112:128], kw[:, :, 112:128], t, ALU.add)
            v.drain().then_inc(s5_k_done, 1)

        K_BANKS = (6, 7)
        TURN_BANKS = (1, 2, 3, 5)

        def pe_s5_batch(pe, b):
            pe.wait_ge(s5_ready, b + 1)
            for g in range(8):
                if 8 * b + g >= 4:
                    pe.wait_ge(s5_turned_copied, 8 * b + g - 3)
                for d in range(2):
                    for r in range(2):
                        at = (2 * d + r) * P
                        nc.tensor.transpose(banks[TURN_BANKS[g % 4]][:, at:at + P], wb[:, r, d, g, :], ident[:, :])
                nc.tensor.drain().then_inc(s5_turned, 1)
            for n in range(4):
                if 4 * b + n >= 2:
                    pe.wait_ge(s5_k_copied, 4 * b + n - 1)
                for g in (2 * n, 2 * n + 1):
                    at = (g % 2) * 256
                    for d, q0, c0 in ((1, 1, 0), (0, 0, 112)):
                        for r in range(2):
                            nc.tensor.matmul(banks[K_BANKS[n % 2]][0:32, at + c0:at + c0 + 128], bd[:, r, d, g, :],
                                             ca[:, r, d, g, q0 * SC:q0 * SC + 128],
                                             start=(d == 1 and r == 0), stop=(d == 0 and r == 1), skip_group_check=True)
                nc.tensor.drain().then_inc(s5_k_ready, 1)

        def act_s5_batch(act, b):
            for g in range(8):
                act.wait_ge(s5_turned, 8 * b + g + 1)
                if b and g == 0:
                    act.wait_ge(s5_stored, 16 * 7 * b)
                act_copy(wbt[:, g, :, :, :].rearrange("p h c n -> p c h n"),
                         banks[TURN_BANKS[g % 4]][:, :].rearrange("p (c h n) -> p c h n", c=4, h=2))
                nc.scalar.drain().then_inc(s5_turned_copied, 1)

        def pool_s5_batch(pool, b):
            st_ = lambda dst, src: nc.gpsimd.dma_start(dst, src).then_inc(s5_stored, 16)
            pool.wait_ge(s5_ready, b + 1)
            for r in range(2):
                for d in range(2):
                    q0 = (1, 0)[d]
                    st_(ca_dram[b, :, 2 * r + d, :, :], ca[:, r, d, :, q0 * SC:q0 * SC + 128])
            pool.wait_ge(s5_turned_copied, 8 * b + 8)
            wf = wbt[:, :, :, :, :].rearrange("p g h c n -> p (g h c n)")
            for k in range(2):
                st_(wbt_dram[2 * b + k], wf[:, k * 2048:(k + 1) * 2048])
            pool.wait_ge(s5_k_done, b + 1)
            st_(k_dram[16 * b:16 * b + 16].rearrange("(g h) p n -> (h p) g n", h=2), kw)
            pool.wait_ge(s5_stored, 16 * 7 * (b + 1))

        hs_ = view(0, 2, 49, DG)
        s5_gateT = view(0, KT, TOK)
        s5_uT = view(6144, KT, TOK)
        SCE = SCH + 2
        s5_u = view(12800, SG, SCE)
        s5_z = view(12800, KT, TOK)
        s_cols = view(19200, 2, 512)
        y_cols = view(20224, 2, 8, P)
        scan_t = hT_words[:, 512:1024].rearrange("p (d n r g) -> p d n r g", d=2, n=2, r=2)
        scan_u = hT_words[:, 0:512].rearrange("p (d n r g) -> p d n r g", d=2, n=2, r=2)
        st_rows = view(22272, 256)
        st_out = st_rows
        wk = [x_words[:, n * 3072:n * 3072 + 2048] for n in range(2)]
        cak = [x_words[:, n * 3072:n * 3072 + 2048].rearrange("p (c g n) -> p c g n", c=4, g=4) for n in range(2)]
        tk = [x_words[:, n * 3072 + 2048:n * 3072 + 3072].rearrange("p (g n) -> p g n", g=8) for n in range(2)]
        u_parked = sem("u_parked")
        gate_parked = sem("gate_parked")
        gate_back = sem("gate_back")
        u_in = sem("u_in")
        u_zero = sem("u_zero")
        h0_in = sem("h0_in")
        wk_in = [sem("wk_in0"), sem("wk_in1")]
        cak_in = [sem("cak_in0"), sem("cak_in1")]
        s_ready = sem("s_ready")
        s_copied = sem("s_copied")
        s_turned = sem("s_turned")
        s_taken = sem("s_taken")
        y_ready = sem("y_ready")
        y_copied = sem("y_copied")
        y_turned = sem("y_turned")
        y_taken = sem("y_taken")
        state_stored = sem("state_stored")

        def pool_s5(pool, l):
            pool.wait_ge(stage_done, after(f"norm{l}.copied1"))
            nc.gpsimd.dma_start(x_dram.rearrange("t p d -> p t d"), x[:, :, :]).then_inc(x_saved, 16)
            nc.gpsimd.dma_start(st_rows, w["state_s5"].rearrange("a b d (g h) n r -> (a b d g) (h n r)", h=2))\
                .then_inc(h0_in, 16)
            nc.gpsimd.memset(s5_u[:, :, SCH:SCE], 0.0).then_inc(u_zero, 1)
            pool.wait_ge(u_evacuated, 2)
            nc.gpsimd.dma_start(ud_dram.rearrange("(k p) n -> p k n", p=P), s5_uT).then_inc(u_parked, 16)
            pool.wait_ge(u_parked, 16)
            pool.wait_ge(u_zero, 1)
            for rows, col, tok in ((slice(112, 128), SCH, 0), (slice(0, 16), SCH + 1, CTX - 1)):
                at = tok % ST * SCH + tok // ST
                nc.gpsimd.dma_start(s5_u[rows, :, col:col + 1],
                                    ud_dram[:, at:at + 1].rearrange("(g p) c -> p g c", p=SC),
                                    allow_slow_non_contiguous=True).then_inc(u_in, 16)
            for j in range(ST):
                nc.gpsimd.dma_start(s5_u[16 * j:16 * j + 16, :, 0:SCH],
                                    ud_dram[:, j * SCH:(j + 1) * SCH].rearrange("(g p) c -> p g c", p=SC))\
                    .then_inc(u_in, 16)
            pool.wait_ge(x_saved, 16 * xn_of(l))
            for k in range(16):
                if k >= 2:
                    pool.wait_ge(s_copied, 4 * (k - 1))
                nc.gpsimd.dma_start(wk[k % 2], wbt_dram[k]).then_inc(wk_in[k % 2], 16)
                if k == 1:
                    pool.wait_ge(stage_done, after(f"mix{l}.projected"))
                    nc.gpsimd.dma_start(gate_dram, s5_gateT.rearrange("p a b -> p (a b)")).then_inc(gate_parked, 16)
            pool.wait_ge(stage_done, after(f"mix{l}.contributions"))
            for k in range(16):
                if k >= 2:
                    pool.wait_ge(y_ready, 2 * (k - 1))
                nc.gpsimd.dma_start(cak[k % 2].rearrange("p c g n -> p c (g n)"),
                                    ca_dram[k // 2, :, :, 4 * (k % 2):4 * (k % 2) + 4, :].rearrange("p c g n -> p c (g n)"))\
                    .then_inc(cak_in[k % 2], 16)
                for j in range(ST):
                    nc.gpsimd.dma_start(tk[k % 2][16 * j:16 * j + 16, :, :],
                                        k_dram[8 * k:8 * k + 8, :, (7 - j) * SC:(7 - j) * SC + 128].rearrange("g p n -> p g n"))\
                        .then_inc(cak_in[k % 2], 16)
            pool.wait_ge(stage_done, after(f"mix{l}.mixed"))
            nc.gpsimd.dma_start(s5_gateT.rearrange("p a b -> p (a b)"), gate_dram).then_inc(gate_back, 16)
            nc.gpsimd.dma_start(x[:, :, :], x_dram.rearrange("t p d -> p t d")).then_inc(x_back, 16)
            pool.wait_ge(stage_done, after(f"mix{l}.gated"))
            nc.gpsimd.dma_start(outs[4].rearrange("a b d (g h) n r -> (a b d g) (h n r)", h=2), st_rows)\
                .then_inc(state_stored, 16)
            pool.wait_ge(state_stored, 16)

        u_evacuated = sem("u_evacuated")

        def pe_s5(pe, st, l):
            for name in ("u", "gate"):
                def body(i, g0, u):
                    group_sums(pe, i, g0, u, [P] * 4, moving=hT)
                loop_groups(nc.tensor, f"{name}{l}", 4, body)
            st.at(f"mix{l}.projected")
            pe.wait_ge(h0_in, 16)
            for r in range(2):
                nc.tensor.transpose(banks[7][:, r * P:(r + 1) * P], st_rows[:, r::2], ident[:, :])
            st.at(f"mix{l}.gate_parked")
            pe.wait_ge(u_in, 16 * (ST + 2))
            for gp in range(64):
                k = gp // 4
                pe.wait_ge(wk_in[k % 2], 16 * (k // 2 + 1))
                if gp >= 2:
                    pe.wait_ge(s_copied, gp - 1)
                for h in range(2):
                    g = 2 * (gp % 4) + h
                    nc.tensor.matmul(banks[gp % 2][0:SCE, h * 256:(h + 1) * 256], s5_u[:, 2 * gp + h, :],
                                     wk[k % 2][:, g * 256:(g + 1) * 256], start=True, stop=True)
                nc.tensor.drain().then_inc(s_ready, 1)
                if gp:
                    pe_turn_contributions(pe, gp - 1)
            pe_turn_contributions(pe, 63)
            st.at(f"mix{l}.contributions")
            st.at(f"mix{l}.scanned")
            for k in range(16):
                pe.wait_ge(cak_in[k % 2], 16 * 9 * (k // 2 + 1))
                for half in range(2):
                    if k:
                        pe.wait_ge(y_copied, 2 * (k - 1) + half + 1)
                    for g in range(half, 8, 2):
                        gg, gp, h = 8 * k + g, 4 * k + g // 2, half
                        out = banks[half][0:SCH, (g // 2) * 128:(g // 2 + 1) * 128]
                        nc.tensor.matmul(out, s5_u[:, gg, 0:SCH], tk[k % 2][:, g, :], start=True, stop=False)
                        rows = slice(64 * h, 64 * h + 64)
                        for r in range(2):
                            for d in range(2):
                                nc.tensor.matmul(out, hs_[rows, r, 0:SCH, d * 64 + gp],
                                                 cak[k % 2][rows, 2 * r + d, g // 2, :],
                                                 start=False, stop=(r == 1 and d == 1))
                    nc.tensor.drain().then_inc(y_ready, 1)
                if k:
                    pe_turn_outputs(pe, k - 1)
            pe_turn_outputs(pe, 15)
            for r in range(2):
                nc.tensor.transpose(banks[7][:, r * P:(r + 1) * P], hs_[:, r, 48, :], ident[:, :])
            st.at(f"mix{l}.mixed")
            st.at(f"mix{l}.gated")
            st.at(f"mix{l}.gated_y")

            def glu_body(i, g0, u):
                group_sums(pe, i, g0, u, [P] * 4, moving=hT)
            loop_groups(nc.tensor, f"glu{l}", 4, glu_body)
            st.at(f"mix{l}.glu")

        def pe_turn_contributions(pe, gp):
            pe.wait_ge(s_copied, gp + 1)
            if gp >= 4 and gp % 2 == 0:
                pe.wait_ge(s_taken, gp // 2 - 1)
            for c in range(4):
                at = (gp % 2) * 256 + c * SCE
                nc.tensor.transpose(banks[2 + (gp // 2) % 2][:, at:at + SCE], s_cols[0:SCE, gp % 2, c * P:(c + 1) * P],
                                    ident[0:SCE, 0:SCE])
            if gp % 2:
                nc.tensor.drain().then_inc(s_turned, 1)

        def pe_turn_outputs(pe, k):
            pe.wait_ge(y_copied, 2 * k + 2)
            if k >= 2:
                pe.wait_ge(y_taken, k - 1)
            for j in range(ST):
                nc.tensor.transpose(banks[2 + k % 2][:, j * SCH:(j + 1) * SCH], y_cols[0:SCH, k % 2, j, :],
                                    ident[0:SCH, 0:SCH])
            nc.tensor.drain().then_inc(y_turned, 1)

        def act_s5(act, st, l):
            def u_write(i, u, half):
                for m in range(2):
                    act_copy(s5_uT[:, bass.ds(i * 8 + 4 * u + m, 1), :].rearrange("p a (j c) -> p (a j) c", j=ST),
                             banks[4 * half + m][:, 0:TOK].rearrange("p (c j) -> p j c", j=ST))
            evacuate(act, nc.scalar, f"u{l}", 4, u_write)
            nc.scalar.drain().then_inc(u_evacuated, 1)

            def gate_write(i, u, half):
                for m in range(4):
                    nc.scalar.activation(s5_gateT[:, bass.ds(i * 8 + 4 * u + m, 1), :], banks[4 * half + m][:, 0:TOK], ACT.Silu)
            evacuate(act, nc.scalar, f"gate{l}", 4, gate_write, share=2)
            st.at(f"mix{l}.projected")
            act.wait_ge(gate_parked, 16)
            st.at(f"mix{l}.gate_parked")
            for gp in range(64):
                act.wait_ge(s_ready, gp + 1)
                if gp >= 4:
                    act.wait_ge(s_turned, (gp - 2) // 2)
                act_copy(s_cols[0:SCE, gp % 2, :].rearrange("p (c h n) -> p h c n", c=4, h=2),
                         banks[gp % 2][0:SCE, :].rearrange("p (h c n) -> p h c n", h=2, c=4))
                nc.scalar.drain().then_inc(s_copied, 1)
            st.at(f"mix{l}.contributions")
            st.at(f"mix{l}.scanned")
            for k in range(16):
                for half in range(2):
                    act.wait_ge(y_ready, 2 * k + half + 1)
                    if k >= 2:
                        act.wait_ge(y_turned, k - 1)
                    act_copy(y_cols[0:SCH, k % 2, :, :].rearrange("p j (g h q) -> p h g j q", h=2, q=SC)[:, half],
                             banks[half][0:SCH, :].rearrange("p (g j q) -> p g j q", g=4, j=ST))
                    nc.scalar.drain().then_inc(y_copied, 1)
                if k:
                    act_take_outputs(act, k - 1)
            act_take_outputs(act, 15)
            st.at(f"mix{l}.mixed")
            st.at(f"mix{l}.gated")
            st.at(f"mix{l}.gated_y")

            def glu_write(i, u, half):
                for m in range(4):
                    nc.scalar.activation(s5_z[:, bass.ds(i * 8 + 4 * u + m, 1), :], banks[4 * half + m][:, 0:TOK],
                                         ACT.Sigmoid, bias=glu_bias(i, u, m))
            evacuate(act, nc.scalar, f"glu{l}", 4, glu_write, share=2)
            st.at(f"mix{l}.glu")

        def glu_bias(i, u, m):
            return vecs[:, 0, bass.ds(i * 8 + (32 + 4 * u + m), 1)]

        def act_take_outputs(act, k):
            act.wait_ge(y_turned, k + 1)
            nc.scalar.activation(hT[:, k, :].rearrange("p (c j) -> p j c", j=ST),
                                 banks[2 + k % 2][:, 0:TOK].rearrange("p (j c) -> p j c", j=ST), ACT.Gelu_apprx_tanh)
            nc.scalar.drain().then_inc(y_taken, 1)

        def dve_s5(dve, st, l):
            v = nc.vector

            def u_write(i, u, half):
                for m in range(2, 4):
                    v.tensor_copy(s5_uT[:, bass.ds(i * 8 + 4 * u + m, 1), :].rearrange("p a (j c) -> p (a j) c", j=ST),
                                  banks[4 * half + m][:, 0:TOK].rearrange("p (c j) -> p j c", j=ST))
            evacuate(dve, v, f"u{l}", 4, u_write)
            v.drain().then_inc(u_evacuated, 1)
            st.at(f"mix{l}.projected")
            dve.wait_ge(gate_parked, 16)
            dve.wait_ge(u_parked, 16)
            st.at(f"mix{l}.gate_parked")
            v.memset(hs_[:, :, 0, 0:64], 0.0)
            v.memset(hs_[:, :, SCX - 1, 64:128], 0.0)
            bk = banks[7][:, 0:2 * P].rearrange("p (r g) -> p r g", r=2)
            v.tensor_copy(hs_[:, :, SCX, 0:64], bk[:, :, 0:64])
            v.tensor_copy(hs_[:, :, SCH - 1, 64:128], bk[:, :, 64:128])
            for t in range(32):
                dve.wait_ge(s_turned, t + 1)
                src = banks[2 + t % 2][:, :].rearrange("p (g n) -> p g n", g=2)[:, :, 0:4 * SCE]\
                    .rearrange("p g (d r c) -> p g d r c", d=2, r=2)
                g = 2 * t
                for r in range(2):
                    f = src[:, :, 0, r, :].rearrange("p g c -> p c g")
                    v.tensor_copy(hs_[:, r, 1:SCX, g:g + 2], f[:, 0:SCX - 1, :])
                    v.tensor_copy(hs_[:, r, 48, g:g + 2], f[:, SCH, :])
                    v.tensor_copy(hs_[:, r, SCX + 1:SCH, g:g + 2], f[:, SCX:SCH - 1, :])
                    bw = src[:, :, 1, r, :].rearrange("p g c -> p c g")
                    v.tensor_copy(hs_[:, r, 0:SCX - 1, 64 + g:64 + g + 2], bw[:, 1:SCX, :])
                    v.tensor_copy(hs_[:, r, 48, 64 + g:64 + g + 2], bw[:, SCH + 1, :])
                    v.tensor_copy(hs_[:, r, SCX:SCH - 1, 64 + g:64 + g + 2], bw[:, SCX + 1:SCH, :])
                v.drain().then_inc(s_taken, 1)
            st.at(f"mix{l}.contributions")
            for s in range(SCH - SCX - 1):
                both = int(s < SCX - 1)
                for d in range(2):
                    dd = slice(64 * d, 64 * d + 64)
                    if d == 0:
                        steps = [(SCX + s, SCX + s + 1)] + [(s, s + 1)] * both
                    else:
                        steps = [(SCH - 1 - s, SCH - 2 - s)] + [(SCX - 1 - s, SCX - 2 - s)] * both
                    for n, (a, b) in enumerate(steps):
                        v.tensor_tensor(scan_t[:, d, n, :, :], hs_[:, :, a, dd],
                                        a8[:, 0:1, dd].broadcast_to([P, 2, 64]), ALU.mult)
                        v.tensor_tensor(scan_u[:, d, n, :, :], hs_[:, ::-1, a, dd], a8[:, 1:3, dd], ALU.mult)
                v.drain()
                for d in range(2):
                    v.tensor_tensor(scan_t[:, d, 0:1 + both], scan_t[:, d, 0:1 + both], scan_u[:, d, 0:1 + both], ALU.add)
                v.drain()
                for d in range(2):
                    dd = slice(64 * d, 64 * d + 64)
                    dst = [(SCX + s + 1, s + 1), (SCH - 2 - s, SCX - 2 - s)][d][0:1 + both]
                    for n, b in enumerate(dst):
                        v.tensor_tensor(hs_[:, :, b, dd], hs_[:, :, b, dd], scan_t[:, d, n, :, :], ALU.add)
                v.drain()
            st.at(f"mix{l}.scanned")
            st.at(f"mix{l}.mixed")
            v.tensor_copy(st_out.rearrange("p (n r) -> p r n", r=2), banks[7][:, 0:2 * P].rearrange("p (r n) -> p r n", r=2))
            dve.wait_ge(gate_back, 16)
            st.at(f"mix{l}.gated")
            v.tensor_tensor(s5_gateT, s5_gateT, hT[:, :, :], ALU.mult)
            st.at(f"mix{l}.gated_y")
            st.at(f"mix{l}.glu")
            v.tensor_tensor(s5_z, s5_z, s5_gateT, ALU.mult)


        def pool_program(pool):
            nc.gpsimd.sem_inc(chunk_used, 8)
            for half in range(2):
                nc.gpsimd.sem_inc(sums_taken[half], 2)
            xp = w["x_prompt"].rearrange("b t d -> (b t) d")
            xs = w["x_sample"].rearrange("b (a t) d -> (b t) a d", t=P)
            nc.gpsimd.dma_start(ident[:, :], consts["ident"]).then_inc(inputs_in, 16)
            nc.gpsimd.memset(rows_v, 0.0).then_inc(rows_zero, 1)
            pool.wait_ge(rows_zero, 1)
            for name, src in (("c_ctx", w["c_ctx"].rearrange("(k p) -> k p", p=P)),
                              ("c", w["c"].rearrange("b (k p) -> (b k) p", p=P)),
                              ("b_glu", w["s5_b_glu"].rearrange("b (k p) -> (b k) p", p=P)),
                              ("d", w["s5_d"].rearrange("b (k p) -> (b k) p", p=P)),
                              ("norm_pre", w["norm_pre"].rearrange("l (k p) -> (l k) p", p=P)),
                              ("norm_post", w["norm_post"].rearrange("l (k p) -> (l k) p", p=P)),
                              ("gla_b_g", w["gla_b_g"].rearrange("b d (k p) -> (b d k) p", p=P))):
                tile_, col = VEC[name]
                nc.gpsimd.dma_start(rows_v[col:col + src.shape[0], tile_, :], src).then_inc(inputs_in, 16)
            for l in range(DEPTH):
                nc.gpsimd.dma_start(rows_v[(l % 2) * 64:(l % 2) * 64 + 48, 2 + l // 2, :],
                                    w["ada_b"][l].rearrange("(j p) -> j p", p=P)).then_inc(inputs_in, 16)
            pool_s5_basics(pool)
            for b in range(8):
                pool_s5_batch(pool, b)
            nc.gpsimd.dma_start(x[:, 0, :], xp).then_inc(x_in, 16)
            nc.gpsimd.dma_start(x[:, 1:3, :], xs).then_inc(x_in, 16)
            for l in layers:
                if l % 3 == 1:
                    pool_s5(pool, l)
                if l % 3 == 0:
                    pool_mla(pool, l)
                if l % 3 == 2:
                    pool_gla(pool, l)
            pool.wait_ge(stage_done, after(stage_names[-1]))
            nc.gpsimd.dma_start(outs[0].rearrange("b t d -> (b t) d"), x[:, 0, :]).then_inc(result_out, 16)
            nc.gpsimd.dma_start(outs[1].rearrange("b (a t) d -> (b t) a d", t=P), x[:, 1:3, :]).then_inc(result_out, 16)
            pool.wait_ge(result_out, 32)


        def pool_mla(pool, l):
            j = l // 3
            pool.wait_ge(stage_done, after(f"norm{l}.copied1"))
            nc.gpsimd.dma_start(ckv_sb[:, 3, :], w["cache_mla_ckv"][0, j]).then_inc(small_in, 16)
            for d in range(2):
                nc.gpsimd.dma_start(kr_sb[:, 3, d * ROPE:(d + 1) * ROPE], w["cache_mla_krope"][0, j]).then_inc(small_in, 16)
            nc.gpsimd.dma_start(gamma, w["mla_kv_norm"][j:j + 1, :].broadcast_to([P, LORA])).then_inc(small_in, 16)
            nc.gpsimd.dma_start(cos_t, consts["rope_cos"]).then_inc(small_in, 16)
            nc.gpsimd.dma_start(sin_t, consts["rope_sin"]).then_inc(small_in, 16)
            nc.gpsimd.dma_start(swap_t, consts["rope_swap"]).then_inc(small_in, 16)
            pool.wait_ge(stage_done, after(f"mix{l}.kv_normed"))
            nc.gpsimd.dma_start(outs[2][0, j], ckv_sb[:, 0, :]).then_inc(stored, 16)
            nc.gpsimd.dma_start(outs[3][0, j], kr_sb[:, 0, 0:ROPE]).then_inc(stored, 16)
            pool.wait_ge(stored, 32 * (nth(l) + 1))

        def sp_program(sp):
            for l in range(DEPTH):
                for part in range(2):
                    load_job(sp, f"ada{l}{'ab'[part]}", 6, w["ada_w"][l], part * 6 * GC)
            for l in layers:
                j = l // 3
                if l % 3 == 0:
                    w_in = w["mla_w_in"][j]
                    wv = w_in.rearrange("(s k p) n -> s p k n", k=4, p=P)

                    def body(i, g0, u):
                        def src(s, u):
                            col = i * 768 + u * 384
                            return [wv[s, :, :, bass.ds(col + hh * (NOPE + ROPE) + at, width)]
                                    for at, width in ((0, NOPE), (NOPE, ROPE)) for hh in range(2)]
                        load_group(sp, i, g0, u, src, 384, rope=True)
                    loop_groups(nc.sync, f"q{l}", 8, body)
                    load_job(sp, f"ckv{l}", 1, w_in, NQ)
                    load_job(sp, f"krope{l}", 1, w_in, NQ + LORA, ROPE)
                    load_job(sp, f"gate{l}", 4, w_in, NQ + LORA + ROPE)
                    uk = w["mla_w_ukv"][j].rearrange("(k p) n -> p k n", p=P)
                    for g in range(2):
                        load_group(sp, 0, FIRST_GROUP[f"ukv{l}"], g,
                                   lambda s, u: uk[:, :, (4 * u + s) * GC:(4 * u + s + 1) * GC], GC)
                    load_job(sp, f"out{l}", 4, w["mla_w_out"][j], 0)
                if l % 3 == 1:
                    load_job(sp, f"u{l}", 4, w["s5_w_in"][j], 0)
                    load_job(sp, f"gate{l}", 4, w["s5_w_in"][j], D)
                    load_job(sp, f"glu{l}", 4, w["s5_w_glu"][j], 0)
                    load_job(sp, f"out{l}", 4, w["s5_w_out"][j], 0)
                if l % 3 == 2:
                    w_in = w["gla_w_in"][j]
                    load_job(sp, f"q{l}", 2, w_in, 0)
                    load_job(sp, f"k{l}", 2, w_in, GH * GDK)
                    load_job(sp, f"v{l}", 4, w_in, 2 * GH * GDK)
                    load_job(sp, f"r{l}", 4, w_in, 2 * GH * GDK + D)
                    load_job(sp, f"glr{l}", 1, w_in, 2 * GH * GDK + 2 * D, 2 * GRANK)
                    load_job(sp, f"out{l}", 4, w["gla_w_out"][j], 0)

        block.tensor(pe_program)
        block.scalar(act_program)
        block.vector(dve_program)
        block.gpsimd(pool_program)
        block.sync(sp_program)


_INS = ["x_prompt", "x_sample", "cache_mla_ckv", "cache_mla_krope", "state_s5", "state_gla", "c", "c_ctx",
        "ada_w", "ada_b", "norm_pre", "norm_post", "mla_w_in", "mla_kv_norm", "mla_w_ukv", "mla_w_out",
        "s5_w_in", "s5_a_re", "s5_a_im", "s5_log_dt", "s5_b_re", "s5_b_im", "s5_c_re", "s5_c_im",
        "s5_d", "s5_w_glu", "s5_b_glu", "s5_w_out", "gla_w_in", "gla_w_g2", "gla_b_g", "gla_norm", "gla_w_out"]
_OUTS = [(1, CTX, D), (1, LAT, D), (1, 2, CTX, LORA), (1, 2, CTX, ROPE), (1, 1, 2, SG, SN, 2), (1, 1, 2, GH, GDK, GDV)]


def kernel(**inputs):
    import concourse.bacc as _bacc
    from concourse.bass_utils import run_bass_kernel_spmd
    arrays = {n: np.ascontiguousarray(inputs[n]) for n in _INS}
    nc = _bacc.Bacc("TRN2", target_bir_lowering=False, num_devices=1)
    constants = shape_constants()
    ins = {n: nc.dram_tensor(f"in_{n}", arrays[n].shape, F32, kind="ExternalInput").ap() for n in _INS}
    cs = {n: nc.dram_tensor(f"const_{n}", a.shape, F32, kind="ExternalInput").ap() for n, a in constants.items()}
    outs = [nc.dram_tensor(f"out_{i}", shape, F32, kind="ExternalOutput").ap() for i, shape in enumerate(_OUTS)]
    build(nc, ins, outs, cs)
    data = {f"in_{n}": arrays[n] for n in _INS} | {f"const_{n}": a for n, a in constants.items()}
    got = run_bass_kernel_spmd(nc, [data], core_ids=[0]).results[0]
    return tuple(got[f"out_{i}"] for i in range(len(_OUTS)))
```

```python
from contextlib import ExitStack

import numpy as np
import concourse.bass as bass
from concourse import mybir

ALU = mybir.AluOpType
ACT = mybir.ActivationFunctionType
AX = mybir.AxisListType
F32 = mybir.dt.float32
U32 = mybir.dt.uint32
F32R = mybir.dt.float32r

P = 128
D = 2048
KT = D // P
CTX, LAT, PAST = 128, 256, 128
TOK = CTX + LAT
NT = TOK // P
COND = ((0, 0, CTX), (1, CTX, TOK))
TILE_COND = (0, 1, 1)
DEPTH = 4
EPS = 1e-6
GC = 512
HEADS, NOPE, ROPE, VH, LORA = 16, 128, 64, 128, 512
NQ = HEADS * (NOPE + ROPE)
KEYS = CTX + LAT + PAST
SM_SCALE = float(NOPE + ROPE) ** -0.5
ROPE_BASE, GRID_W = 10000.0, 64
SG, SC, SN, ST = 128, 16, 64, 8
SCH = TOK // ST
SCX = CTX // ST
GH, GDK, GDV, GRANK, GCH = 4, 256, 512, 16, 64
GATE_NORM = 16.0
ARENA = 23000
ADA_GROUPS = DEPTH * 12


def shape_constants():
    c = {}
    c["ident"] = np.eye(P, dtype=np.float32)
    half = ROPE // 2
    inv = 1.0 / (np.float32(ROPE_BASE) ** (np.arange(0, half, 2, dtype=np.float32) / half))
    tok = np.arange(LAT)
    ang = [(tok // GRID_W).astype(np.float32)[:, None] * inv, (tok % GRID_W).astype(np.float32)[:, None] * inv]
    cos, sin = np.zeros((P, LAT), np.float32), np.zeros((P, LAT), np.float32)
    swap = np.zeros((P, P), np.float32)
    for r in range(P):
        d = r % ROPE
        a = ang[d // half].astype(np.float32)[:, d % (half // 2)]
        cos[r], sin[r] = np.cos(a), np.sin(a)
        first = d % half < half // 2
        partner = r + half // 2 if first else r - half // 2
        swap[partner, r] = -1.0 if first else 1.0
    c["rope_cos"], c["rope_sin"], c["rope_swap"] = cos, sin, swap
    s, t = np.arange(P)[:, None], np.arange(P)[None, :]
    same = s // GCH == t // GCH
    c["gla_mask"] = np.stack([same & (s <= t), same & (s >= t)], 1).astype(np.float32)
    edge = np.ones((P, TOK), np.float32)
    edge[:, ::GCH] = 0.0
    c["gla_edge"] = edge
    return c


def layer_jobs(layers):
    jobs = []
    for l in layers:
        jobs += {
            0: [(f"q{l}", 8, 384), (f"ckv{l}", 1, GC), (f"krope{l}", 1, ROPE), (f"gate{l}", 4, GC), (f"ukv{l}", 2, GC),
                (f"out{l}", 4, GC)],
            1: [(f"{name}{l}", 4, GC) for name in ("u", "gate", "glu", "out")],
            2: [(f"q{l}", 2, GC), (f"k{l}", 2, GC), (f"v{l}", 4, GC), (f"r{l}", 4, GC), (f"glr{l}", 1, 2 * GRANK),
                (f"out{l}", 4, GC)],
        }[l % 3]
    return jobs


def first_groups(layers):
    first, n = {}, 0
    for name, groups in [(f"ada{l}{part}", 6) for l in range(DEPTH) for part in "ab"] + \
            [job[:2] for job in layer_jobs(layers)]:
        first[name] = n
        n += groups
    return first


def stage_list(layers):
    names = ["rows_in", "rows_transposed", "vectors_ready", "silu_c"]
    names += [f"s5.{s}" for s in ("loaded", "dt", "angle", "reduced", "sines", "poles", "turned_pow0", "copied_pow0",
                                  "turned_pow1", "copied_pow1", "turned_pow2", "copied_pow2")]
    names += [f"s5.{s}{n}" for n in range(4) for s in ("turned_b", "copied_b")]
    names += [f"s5.{s}{n}" for n in range(4) for s in ("turned_c", "copied_c")]
    for l in range(DEPTH):
        names += [f"ada{l}.{s}" for s in ("rows", "transposed", "ready")]
    kinds = {0: ("projected", "kv_rstd", "kv_normed", "kv_transposed", "kv_copied", "rotated", "roped", "attended", "split"),
             1: ("projected", "gate_parked", "contributions", "scanned", "mixed", "gated", "gated_y", "glu", "split"), 2: ("projected", "z0", "z_taken0", "z1", "z_taken1", "abs", "softplus", "log_gates", "attended", "split")}
    for l in layers:
        names += [f"norm{l}.{s}" for s in ("stats", "scales", "scaled", "turned0", "copied0", "turned1", "copied1", "split")]
        names += [f"mix{l}.{s}" for s in kinds[l % 3]]
        names += [f"out{l}.{s}" for s in ("gate", "gate_spread", "gate_copied", "projected", "stats", "rstd", "scaled",
                                          "added")]
    return names


def build(nc, ins, outs, consts, layers=range(DEPTH), dbg=None):
    ctx = ExitStack()
    with ctx:
        def sb(name, shape, dt=F32):
            return ctx.enter_context(nc.sbuf_tensor(name, shape, dt))

        def sem(name):
            return ctx.enter_context(nc.semaphore(name))

        raw = sb("raw", [P, 4, 4, GC])
        w_hi = sb("w_hi", [P, 2, 4, GC], F32R)
        w_lo = sb("w_lo", [P, 2, 4, GC], F32R)
        ident = sb("ident", [P, P])
        vecs = sb("vecs", [P, 4, P])
        mod = sb("mod", [P, DEPTH, 48, 2])
        silu_c = sb("silu_c", [P, KT, 2])
        small = sb("small", [P, 64])
        arena = sb("arena", [P, ARENA])
        with nc.sbuf_tensor("hT_lo", [P, KT, TOK], F32R) as hT_lo, nc.sbuf_tensor("hT_hi", [P, KT, TOK], F32R) as hT_hi:
            pass
        scratch = sb("scratch", [P, 2 * KT * TOK])
        h32 = scratch[:, 0:KT * TOK].rearrange("p (a b) -> p a b", a=KT)
        FIRST_GROUP = first_groups(layers)

        def nth(l):
            return sum(1 for m in layers if m < l and m % 3 == l % 3)

        def view(at, *shape):
            n = int(np.prod(shape))
            assert at + n <= ARENA, (at, shape)
            v = arena[:, at:at + n]
            if len(shape) == 2:
                return v.rearrange("p (a b) -> p a b", a=shape[0])
            if len(shape) == 3:
                return v.rearrange("p (a b c) -> p a b c", a=shape[0], b=shape[1])
            if len(shape) == 5:
                return v.rearrange("p (a b c d e) -> p a b c d e", a=shape[0], b=shape[1], c=shape[2], d=shape[3])
            if len(shape) == 4:
                return v.rearrange("p (a b c d) -> p a b c d", a=shape[0], b=shape[1], c=shape[2])
            return v

        banks = [ctx.enter_context(nc.psum_tensor(f"bank{i}", [P, 512], F32)) for i in range(8)]

        x = view(16384, NT, D)
        landed = [sem(f"landed{slot}") for slot in range(4)]
        ada_used = sem("ada_used")
        hi_ready = sem("hi_ready")
        lo_ready = sem("lo_ready")
        chunk_used = sem("chunk_used")
        h_ready = sem("h_ready")
        h_hi_ready = sem("h_hi_ready")
        sums_ready = sem("sums_ready")
        sums_taken = [sem("sums_taken0"), sem("sums_taken1")]
        stage_done = sem("stage_done")
        inputs_in = sem("inputs_in")
        small_in = sem("small_in")
        stored = sem("stored")
        stores = [0]

        block = ctx.enter_context(nc.Block())
        w = {k: v for k, v in ins.items()}

        stage_names = stage_list(layers)

        def after(name):
            return 3 * (stage_names.index(name) + 1)

        class Stages:
            def __init__(self, eng):
                self.eng, self.n = eng, 0

            def at(self, name):
                assert stage_names[self.n] == name, (stage_names[self.n], name)
                self.eng.drain().then_inc(stage_done, 1)
                self.n += 1
                self.eng.wait_ge(stage_done, 3 * self.n)

        def layer_chunk(g0, u, s):
            return 4 * (g0 + u - ADA_GROUPS) + s

        def load_group(sp, i, g0, u, src, cols):
            for s in range(4):
                if g0 < ADA_GROUPS:
                    sp.wait_ge(ada_used, i * 8 + (4 * (g0 + u) + s + 1))
                else:
                    sp.wait_ge(lo_ready, i * 8 + (layer_chunk(g0, u, s) + 1))
                sp.dma_start(raw[:, s, :, 0:cols], src(s, u)).then_inc(landed[s], 16)

        def loop_groups(eng, name, groups, body):
            g0 = FIRST_GROUP[name]
            if groups >= 4:
                with eng.Fori(0, groups // 2) as i:
                    for u in range(2):
                        body(i, g0, u)
            else:
                for g in range(groups):
                    body(0, g0, g)

        def load_job(sp, name, groups, weight, col0, cols=GC, only=None):
            wv = weight.rearrange("(s k p) n -> s p k n", k=4, p=P)

            def body(i, g0, u):
                load_group(sp, i, g0, u, lambda s, u: wv[s, :, :, bass.ds(i * (2 * GC) + (col0 + u * GC), cols)], cols)
            if only is None:
                loop_groups(nc.sync, name, groups, body)
            else:
                for g in only:
                    body(g // 2, FIRST_GROUP[name], g % 2)

        def group_sums(pe, i, g0, u, tiles, cols=GC):
            half = (g0 + u) % 2
            pe.wait_ge(sums_taken[half], i * 2 + 2 * ((g0 + u) // 2 + 1))
            for s in range(4):
                pe.wait_ge(lo_ready, i * 8 + (layer_chunk(g0, u, s) + 5))
                for k in range(4):
                    kt = 4 * s + k
                    first, last = kt == 0, kt == KT - 1
                    if tiles is not None:
                        at = 0
                        for m, width in enumerate(tiles):
                            for n, (wp, hp) in enumerate(((w_hi, hT_hi), (w_hi, hT_lo), (w_lo, hT_hi))):
                                mm = nc.tensor.matmul(banks[4 * half + m][0:width, 0:TOK],
                                                      wp[:, s % 2, k, at:at + width], hp[:, kt, :],
                                                      start=(first and n == 0), stop=(last and n == 2))
                            at += width
                    else:
                        for t in range(NT):
                            for n, (hp, wp) in enumerate(((hT_hi, w_hi), (hT_hi, w_lo), (hT_lo, w_hi))):
                                mm = nc.tensor.matmul(banks[4 * half + t][:, 0:cols], hp[:, kt, t * P:(t + 1) * P],
                                                      wp[:, s % 2, k, 0:cols],
                                                      start=(first and n == 0), stop=(last and n == 2))
                mm.then_inc(chunk_used, 1)
            nc.tensor.drain().then_inc(sums_ready, 1)

        def ada_sums(pe, i, g0, u):
            half = (g0 + u) % 2
            pe.wait_ge(sums_taken[half], i * 2 + 2 * ((g0 + u) // 2 + 1))
            for s in range(4):
                pe.wait_ge(landed[s], i * 32 + 16 * (g0 + u + 1))
                for k in range(4):
                    kt = 4 * s + k
                    mm = nc.tensor.matmul(banks[4 * half][0:2, :], silu_c[:, kt, :], raw[:, s, k, :],
                                          start=(kt == 0), stop=(kt == KT - 1))
                mm.then_inc(ada_used, 1)
            nc.tensor.drain().then_inc(sums_ready, 1)

        jobs = layer_jobs(layers)

        def split_chunk(eng, i, g0, u, s, name, cols):
            n = layer_chunk(g0, u, s)
            if name[0] == "q" and cols == 384:
                parts = [(slice(0, 256), 0, NOPE), (slice(256, 384), NOPE, NOPE + ROPE)]
                src = raw[:, s, :, 0:cols].rearrange("p k (h n) -> p k h n", h=2)
                pick = lambda to, out, a, b: (to[:, s % 2, :, out].rearrange("p k (h n) -> p k h n", h=2), src[:, :, :, a:b])
            else:
                parts = [(slice(0, cols), 0, cols)]
                pick = lambda to, out, a, b: (to[:, s % 2, :, out], raw[:, s, :, a:b])
            if eng == "act":
                nc.scalar.wait_ge(landed[s], i * 32 + 16 * (g0 + u + 1))
                nc.scalar.wait_ge(chunk_used, i * 8 + (n + 1))
                for part in parts:
                    dst, src_ = pick(w_hi, *part)
                    nc.scalar.activation(dst, src_, ACT.Copy)
                nc.scalar.drain().then_inc(hi_ready, 1)
            else:
                nc.vector.wait_ge(hi_ready, i * 8 + (n + 1))
                for part in parts:
                    dst, src_ = pick(w_lo, *part)
                    nc.vector.tensor_tensor(dst, src_, pick(w_hi, *part)[0], ALU.subtract)
                nc.vector.drain().then_inc(lo_ready, 1)

        def split_next(eng, name):
            at = 0 if name is None else [j[0] for j in jobs].index(name) + 1
            if at < len(jobs):
                job, _, cols = jobs[at]
                split_chunk(eng, 0, FIRST_GROUP[job], 0, 0, job, cols)

        def stream(eng, name, write=None, share=1):
            unit = {"act": nc.scalar, "dve": nc.vector}[eng]
            g0 = FIRST_GROUP[name]
            _, groups, cols = [j for j in jobs if j[0] == name][0]

            def group(i, u, last):
                for s in range(1, 4):
                    split_chunk(eng, i, g0, u, s, name, cols)
                if last:
                    split_next(eng, name)
                else:
                    split_chunk(eng, i, g0, u + 1, 0, name, cols)
                if write:
                    unit.wait_ge(sums_ready, i * 2 + (g0 + u + 1))
                    half = (g0 + u) % 2
                    write(i, u, half)
                    unit.drain().then_inc(sums_taken[half], share)
            if groups > 4:
                with unit.Fori(0, groups // 2 - 1) as i:
                    for u in range(2):
                        group(i, u, False)
                done = groups - 2
            else:
                done = 0
            for g in range(done, groups):
                group(g // 2, g % 2, g == groups - 1)

        h_splits = {"act": 0, "dve": 0}

        def split_h(eng, quarters=range(4)):
            for q in quarters:
                k = slice(4 * q, 4 * q + 4)
                h_splits[eng] += 1
                if eng == "act":
                    nc.scalar.activation(hT_hi[:, k, :], h32[:, k, :], ACT.Copy)
                    nc.scalar.drain().then_inc(h_hi_ready, 1)
                else:
                    nc.vector.wait_ge(h_hi_ready, h_splits[eng])
                    nc.vector.tensor_tensor(hT_lo[:, k, :], h32[:, k, :], hT_hi[:, k, :], ALU.subtract)

        def act_copy(out, in_):
            return nc.scalar.activation(out, in_, ACT.Copy)

        VEC = {"c_ctx": (0, 0), "c": (0, 16), "b_glu": (0, 32), "d": (0, 48), "norm_pre": (0, 64),
               "norm_post": (1, 0), "gla_b_g": (1, 64), "ada0": (2, 0), "ada1": (3, 0)}
        rows_v = view(0, 4, P)
        mrow = view(0, 6144)

        def vec(name, at=0, n=16):
            tile_, col = VEC[name]
            return vecs[:, tile_, col + at:col + at + n]

        from_layer = {l: {} for l in range(DEPTH)}
        qn = view(0, HEADS, TOK)
        qr = view(6144, HEADS // 2, TOK)
        gateT = view(9216, HEADS, TOK)
        tmp0 = 15360
        ckv_sb = view(tmp0, 4, LORA)
        ckv_hi = hT_hi[:, :, :].rearrange("p a b -> p (a b)")[:, 0:4 * KEYS].rearrange("p (a b) -> p a b", a=4)
        ckv_lo = hT_hi[:, :, :].rearrange("p a b -> p (a b)")[:, 4 * KEYS:8 * KEYS].rearrange("p (a b) -> p a b", a=4)
        kr_sb = view(tmp0 + 4096, 4, P)
        gamma = view(tmp0 + 4608, LORA)
        cos_t = view(tmp0 + 5120, LAT)
        sin_t = view(tmp0 + 5376, LAT)
        swap_t = view(tmp0 + 5632, P)
        krT = view(tmp0 + 5760, KEYS)
        rope_tmp = view(tmp0 + 6272, 2, LAT)
        kT = view(tmp0, 2, 2, KEYS)
        kr_pad = view(tmp0 + 2048, 2, KEYS)
        v_sb = scratch[:, 10240:12288].rearrange("p (b t v) -> p b t v", b=2, t=4)
        o_sb = view(0, NT, D)
        gate_bc = view(6144, 2, D)
        sq_junk = view(10240, D)
        xn = view(0, NT, D)
        G_small = view(10240 + 2048, KT, 2)

        p_sb = view(tmp0 + 4096, 2, 3, LAT + PAST)
        pT = view(tmp0 + 6400, 4, LAT)

        ss = small[:, 0:3]
        rs = small[:, 3:6]
        mx = small[:, 8:16]
        sm = small[:, 16:24]
        eps_c = small[:, 63:64]

        ckv_hi_ready = sem("ckv_hi_ready")
        maxes_ready = sem("maxes_ready")
        exps_ready = sem("exps_ready")
        qn_junk = view(tmp0 + 5760, LORA)
        G_scale = view(15360, KT, 2)
        INPUT_LOADS = 12
        rows_zero = sem("rows_zero")
        result_out = sem("result_out")
        MLA_LOADS = 7

        def pe_program(pe):
            st = Stages(nc.tensor)
            pe.wait_ge(inputs_in, 16 * INPUT_LOADS)
            pe_start(pe, st)
            pe_s5_basics(pe, st)
            for l in range(DEPTH):
                pe_ada(pe, st, l)
            for l in layers:
                pe_norm(pe, st, l)
                [pe_mla, pe_s5, pe_gla][l % 3](pe, st, l)
                pe_out(pe, st, l)

        def pe_start(pe, st):
            st.at(f"rows_in")
            for a in range(4):
                nc.tensor.transpose(banks[0][:, a * P:(a + 1) * P], rows_v[:, a, :], ident[:, :])
            st.at(f"rows_transposed")
            st.at(f"vectors_ready")
            st.at(f"silu_c")

        def pe_ada(pe, st, l):
            def body(i, g0, u):
                ada_sums(pe, i, g0, u)
            for part in range(2):
                loop_groups(nc.tensor, f"ada{l}{'ab'[part]}", 6, body)
                pe_s5_batch(pe, 2 * l + part)
            st.at(f"ada{l}.rows")
            for j in range(48):
                nc.tensor.transpose(banks[0][:, 2 * j:2 * j + 2], mrow[0:2, j * P:(j + 1) * P], ident[0:2, 0:2])
            st.at(f"ada{l}.transposed")
            st.at(f"ada{l}.ready")

        def pe_norm(pe, st, l):
            st.at(f"norm{l}.stats")
            st.at(f"norm{l}.scales")
            st.at(f"norm{l}.scaled")
            for half in range(2):
                for k in range(8 * half, 8 * half + 8):
                    for t in range(NT):
                        nc.tensor.transpose(banks[k % 8][:, t * P:(t + 1) * P], xn[:, t, k * P:(k + 1) * P],
                                            ident[:, :])
                st.at(f"norm{l}.turned{half}")
                st.at(f"norm{l}.copied{half}")
            st.at(f"norm{l}.split")

        def pe_out(pe, st, l):
            st.at(f"out{l}.gate")
            for c in range(2):
                for k in range(KT):
                    nc.tensor.matmul(banks[c * 4 + k // 4][:, (k % 4) * P:(k % 4 + 1) * P],
                                     G_small[:, k, c:c + 1].broadcast_to([P, P]), ident[:, :],
                                     start=True, stop=True)
            st.at(f"out{l}.gate_spread")
            st.at(f"out{l}.gate_copied")

            def body(i, g0, u):
                group_sums(pe, i, g0, u, None)
            loop_groups(nc.tensor, f"out{l}", 4, body)
            st.at(f"out{l}.projected")
            st.at(f"out{l}.stats")
            st.at(f"out{l}.rstd")
            st.at(f"out{l}.scaled")
            st.at(f"out{l}.added")

        def pe_mla(pe, st, l):
            def q_body(i, g0, u):
                group_sums(pe, i, g0, u, [P] * 3)
            loop_groups(nc.tensor, f"q{l}", 8, q_body)
            group_sums(pe, 0, FIRST_GROUP[f"ckv{l}"], 0, None)
            group_sums(pe, 0, FIRST_GROUP[f"krope{l}"], 0, None, cols=ROPE)

            def gate_body(i, g0, u):
                group_sums(pe, i, g0, u, [P] * 4)
            loop_groups(nc.tensor, f"gate{l}", 4, gate_body)
            st.at(f"mix{l}.projected")
            st.at(f"mix{l}.kv_rstd")
            st.at(f"mix{l}.kv_normed")
            for kt in range(4):
                for t in range(4):
                    nc.tensor.transpose(banks[kt][:, t * P:(t + 1) * P], ckv_sb[:, t, kt * P:(kt + 1) * P], ident[:, :])
            for t in range(4):
                nc.tensor.transpose(banks[4][:, t * P:(t + 1) * P], kr_sb[:, t, :], ident[:, :])
            st.at(f"mix{l}.kv_transposed")
            st.at(f"mix{l}.kv_copied")
            for j in range(9):
                src = qr[:, j, CTX:TOK] if j < 8 else krT[:, CTX:TOK]
                nc.tensor.matmul(banks[j // 2][:, (j % 2) * LAT:(j % 2 + 1) * LAT], swap_t, src, start=True, stop=True)
            st.at(f"mix{l}.rotated")
            st.at(f"mix{l}.roped")
            pe_attention(pe, st, l)

        def seen(t):
            return (0, CTX) if t == 0 else (CTX, KEYS)

        kv_ready = sem("kv_ready")
        kv_copied = sem("kv_copied")
        scores_ready = sem("scores_ready")
        probs_ready = sem("probs_ready")
        probsT_ready = sem("probsT_ready")
        probsT_copied = sem("probsT_copied")
        heads_ready = sem("heads_ready")
        heads_done = sem("heads_done")
        def split_pair(eng, l, pair):
            if pair < 8:
                split_chunk(eng, 0, FIRST_GROUP[f"ukv{l}"], pair // 4, pair % 4, f"ukv{l}", GC)
            else:
                split_next(eng, f"ukv{l}")

        def score_bank(h, t):
            return banks[2 * (h % 2) + (t == 2)][:, 384:512] if t == 0 else banks[2 * (h % 2) + (t == 2)][:, 0:384]

        def copy_piece(eng, l, pair, j):
            unit, copy = {"act": (nc.scalar, act_copy), "dve": (nc.vector, nc.vector.tensor_copy)}[eng]
            if j % 2 != (eng == "dve"):
                return
            unit.wait_ge(kv_ready, 32 * nth(l) + 4 * pair + j + 1)
            if j < 2:
                copy(kT[:, pair % 2, j, :], banks[7][:, :])
            else:
                t = 2 * (j - 2)
                copy(v_sb[:, pair % 2, t:t + 2, :], banks[7][:, :].rearrange("p (a b) -> p a b", a=2))
            unit.drain().then_inc(kv_copied, 1)

        def pe_attention(pe, st, l):
            base = 16 * nth(l)

            def piece(pair, j):
                n = 2 * base + 4 * pair + j
                if j == 0:
                    pe.wait_ge(lo_ready, layer_chunk(FIRST_GROUP[f"ukv{l}"], 0, pair) + 5)
                if n:
                    pe.wait_ge(kv_copied, n)
                slot = pair % 2
                if j < 2:
                    for kt in range(4):
                        for m, (wp, cp) in enumerate(((w_hi, ckv_hi), (w_hi, ckv_lo), (w_lo, ckv_hi))):
                            mm = nc.tensor.matmul(banks[7][:, 0:KEYS], wp[:, slot, kt, j * 256:j * 256 + P],
                                                  cp[:, kt, :], start=(kt == 0 and m == 0), stop=(kt == 3 and m == 2))
                else:
                    for t in (2 * (j - 2), 2 * (j - 2) + 1):
                        for kt in range(4):
                            for m, (cp, wp) in enumerate(((ckv_hi, w_hi), (ckv_hi, w_lo), (ckv_lo, w_hi))):
                                mm = nc.tensor.matmul(banks[7][:, (t % 2) * 256:(t % 2 + 1) * 256],
                                                      cp[:, kt, t * P:(t + 1) * P],
                                                      wp[:, slot, kt, :].rearrange("p (h x) -> p h x", h=2)[:, :, NOPE:],
                                                      start=(kt == 0 and m == 0), stop=(kt == 3 and m == 2))
                    if j == 3:
                        mm.then_inc(chunk_used, 1)
                nc.tensor.drain().then_inc(kv_ready, 1)

            def scores(h):
                pe.wait_ge(kv_copied, 2 * base + 4 * (h // 2) + 2)
                if h >= 2:
                    pe.wait_ge(exps_ready, base + h - 1)
                for t in range(3):
                    a, b = seen(t)
                    out = score_bank(h, t)
                    nc.tensor.matmul(out, qn[:, h, t * P:(t + 1) * P], kT[:, (h // 2) % 2, h % 2, a:b],
                                     start=True, stop=False)
                    nc.tensor.matmul(out, qr[:, h // 2, t * P:(t + 1) * P], kr_pad[:, h % 2, a:b],
                                     start=False, stop=True)
                nc.tensor.drain().then_inc(scores_ready, 1)

            for j in range(4):
                piece(0, j)
            scores(0)
            for h in range(HEADS):
                n, pair, hh = base + h, h // 2, h % 2
                if h + 1 < HEADS:
                    scores(h + 1)
                if pair + 1 < 8:
                    piece(pair + 1, 2 * hh)
                pe.wait_ge(probs_ready, n + 1)
                p = p_sb[:, hh]
                for kk in range(3):
                    for t in (1, 2):
                        at = (kk % 2) * LAT + (t - 1) * P
                        nc.tensor.transpose(banks[4 + kk // 2][:, at:at + P], p[:, t, kk * P:(kk + 1) * P], ident[:, :])
                nc.tensor.transpose(banks[5][:, LAT:LAT + P], p[:, 0, 0:P], ident[:, :])
                nc.tensor.drain().then_inc(probsT_ready, 1)
                if pair + 1 < 8:
                    piece(pair + 1, 2 * hh + 1)
                pe.wait_ge(probsT_copied, 2 * (n + 1))
                pe.wait_ge(kv_copied, 2 * base + 4 * pair + 4)
                if h:
                    pe.wait_ge(heads_done, n)
                v_ = v_sb[:, pair % 2, :, hh * VH:(hh + 1) * VH]
                nc.tensor.matmul(banks[6][:, 0:CTX], v_[:, 0, :], pT[:, 0, 0:CTX], start=True, stop=True)
                for kk in range(3):
                    nc.tensor.matmul(banks[6][:, CTX:TOK], v_[:, 1 + kk, :], pT[:, 1 + kk, :],
                                     start=(kk == 0), stop=(kk == 2))
                nc.tensor.drain().then_inc(heads_ready, 1)
            nc.tensor.sem_inc(sums_ready, 2)
            st.at(f"mix{l}.attended")
            st.at(f"mix{l}.split")

        def act_program(act):
            st = Stages(nc.scalar)
            act.wait_ge(inputs_in, 16 * INPUT_LOADS)
            st.at("rows_in")
            st.at("rows_transposed")
            st.at("vectors_ready")
            for c in range(2):
                nc.scalar.activation(silu_c[:, :, c], vecs[:, 0, c * 16:c * 16 + 16], ACT.Silu)
            st.at("silu_c")
            act_s5_basics(act, st)
            for l in range(DEPTH):
                for part in range(2):
                    def write(i, u, half):
                        act_copy(mrow[0:2, bass.ds(i * 1024 + (part * 3072 + u * GC), GC)], banks[4 * half][0:2, :])

                    def take(i, g0, u):
                        act.wait_ge(sums_ready, i * 2 + (g0 + u + 1))
                        half = (g0 + u) % 2
                        write(i, u, half)
                        nc.scalar.drain().then_inc(sums_taken[half], 2)
                    loop_groups(nc.scalar, f"ada{l}{'ab'[part]}", 6, take)
                    act_s5_batch(act, 2 * l + part)
                st.at(f"ada{l}.rows")
                st.at(f"ada{l}.transposed")
                st.at(f"ada{l}.ready")
            act.wait_ge(x_in, 32)
            split_next("act", None)
            for l in layers:
                act_norm(act, st, l)
                [act_mla, act_s5, act_gla][l % 3](act, st, l)
                act_out(act, st, l)

        def act_norm(act, st, l):
            for t in range(NT):
                nc.scalar.activation(sq_junk, x[:, t, :], ACT.Square, accum_out=ss[:, t:t + 1])
                nc.scalar.drain()
            nc.scalar.activation(rs, ss, ACT.Sqrt, scale=1.0 / D, bias=eps_c)
            st.at(f"norm{l}.stats")
            st.at(f"norm{l}.scales")
            st.at(f"norm{l}.scaled")
            for half in range(2):
                st.at(f"norm{l}.turned{half}")
                for k in range(8 * half, 8 * half + 8, 2):
                    for c, a, b in COND:
                        nc.scalar.activation(h32[:, k, a:b], banks[k % 8][:, a:b], ACT.Identity,
                                             scale=G_scale[:, k, c:c + 1], bias=mod[:, l, k, c:c + 1])
                st.at(f"norm{l}.copied{half}")
                split_h("act", range(2 * half, 2 * half + 2))
            st.at(f"norm{l}.split")

        def act_out(act, st, l):
            st.at(f"out{l}.gate")
            st.at(f"out{l}.gate_spread")
            for b in range(0, 8, 2):
                act_copy(gate_bc[:, b // 4, (b % 4) * 512:(b % 4 + 1) * 512], banks[b][:, :])
            st.at(f"out{l}.gate_copied")

            def write(i, u, half):
                act_copy(o_sb[:, 0, bass.ds(i * 1024 + u * GC, GC)], banks[4 * half][:, :])
                act_copy(o_sb[:, 1, bass.ds(i * 1024 + u * GC, GC)], banks[4 * half + 1][:, :])
            stream("act", f"out{l}", write)
            st.at(f"out{l}.projected")
            for t in range(NT):
                nc.scalar.activation(sq_junk, o_sb[:, t, :], ACT.Square, accum_out=ss[:, t:t + 1])
                nc.scalar.drain()
            nc.scalar.activation(rs, ss, ACT.Sqrt, scale=1.0 / D, bias=eps_c)
            st.at(f"out{l}.stats")
            st.at(f"out{l}.rstd")
            st.at(f"out{l}.scaled")
            st.at(f"out{l}.added")

        def act_mla(act, st, l):
            def q_write(i, u, half):
                act_copy(qn[:, bass.ds(i * 4 + 2 * u, 1), :], banks[4 * half][:, 0:TOK])
                act_copy(qn[:, bass.ds(i * 4 + 2 * u + 1, 1), :], banks[4 * half + 1][:, 0:TOK])
            stream("act", f"q{l}", q_write)

            act.wait_ge(x_saved, 16 * parked(l))

            def ckv_write(i, u, half):
                for t in range(NT):
                    act_copy(ckv_sb[:, t, :], banks[4 * half + t][:, :])
            stream("act", f"ckv{l}", ckv_write, share=2)

            stream("act", f"krope{l}")

            def gate_write(i, u, half):
                for m in range(4):
                    nc.scalar.activation(gateT[:, bass.ds(i * 8 + 4 * u + m, 1), :], banks[4 * half + m][:, 0:TOK], ACT.Silu)
            stream("act", f"gate{l}", gate_write, share=2)
            for t in range(NT):
                nc.scalar.activation(qn_junk, ckv_sb[:, t, :], ACT.Square, accum_out=ss[:, t:t + 1])
                nc.scalar.drain()
            nc.scalar.activation(rs, ss, ACT.Sqrt, scale=1.0 / LORA, bias=eps_c)
            st.at(f"mix{l}.projected")
            st.at(f"mix{l}.kv_rstd")
            st.at(f"mix{l}.kv_normed")
            st.at(f"mix{l}.kv_transposed")
            for kt in range(4):
                act_copy(ckv_hi[:, kt, :], banks[kt][:, :])
                nc.scalar.drain().then_inc(ckv_hi_ready, 1)
            st.at(f"mix{l}.kv_copied")
            st.at(f"mix{l}.rotated")
            st.at(f"mix{l}.roped")
            base = 16 * nth(l)

            def exps(h):
                act.wait_ge(maxes_ready, base + h + 1)
                for t in range(3):
                    a, b = seen(t)
                    nc.scalar.activation(p_sb[:, h % 2, t, 0:b - a], score_bank(h, t), ACT.Exp, scale=SM_SCALE,
                                         bias=mx[:, t:t + 1], accum_out=sm[:, t:t + 1])
                nc.scalar.drain().then_inc(exps_ready, 1)

            for j in (0, 2):
                copy_piece("act", l, 0, j)
            split_pair("act", l, 1)
            exps(0)
            for h in range(HEADS):
                if h + 1 < HEADS:
                    exps(h + 1)
                if h // 2 + 1 < 8:
                    copy_piece("act", l, h // 2 + 1, 2 * (h % 2))
                act.wait_ge(probsT_ready, base + h + 1)
                act_copy(pT[:, 1:3, :], banks[4][:, :].rearrange("p (a b) -> p a b", a=2))
                nc.scalar.drain().then_inc(probsT_copied, 1)
                if h % 2 and h < 14:
                    split_pair("act", l, (h + 3) // 2)
            st.at(f"mix{l}.attended")
            split_h("act")
            st.at(f"mix{l}.split")


        def dve_program(dve):
            st = Stages(nc.vector)
            nc.vector.memset(eps_c, EPS)
            dve.wait_ge(inputs_in, 16 * INPUT_LOADS)
            st.at("rows_in")
            st.at("rows_transposed")
            nc.vector.tensor_copy(vecs[:, :, :], banks[0][:, :].rearrange("p (a b) -> p a b", a=4))
            st.at("vectors_ready")
            st.at("silu_c")
            dve_s5_basics(dve, st)
            for l in range(DEPTH):
                for part in range(2):
                    dve_s5_batch(dve, 2 * l + part)
                st.at(f"ada{l}.rows")
                st.at(f"ada{l}.transposed")
                bias = vecs[:, 2 + l // 2, (l % 2) * 64:(l % 2) * 64 + 48]
                nc.vector.tensor_tensor(mod[:, l, :, :], banks[0][:, 0:96].rearrange("p (j c) -> p j c", c=2),
                                        bias.unsqueeze(2).broadcast_to([P, 48, 2]), ALU.add)
                st.at(f"ada{l}.ready")
            dve.wait_ge(x_in, 32)
            split_next("dve", None)
            for l in layers:
                dve_norm(dve, st, l)
                [dve_mla, dve_s5, dve_gla][l % 3](dve, st, l)
                dve_out(dve, st, l)

        def dve_norm(dve, st, l):
            st.at(f"norm{l}.stats")
            nc.vector.reciprocal(rs, rs)
            nc.vector.scalar_tensor_tensor(out=G_scale, in0=mod[:, l, 16:32, :], scalar=1.0,
                                           in1=vec("norm_pre", 16 * l).unsqueeze(2).broadcast_to([P, KT, 2]),
                                           op0=ALU.add, op1=ALU.mult)
            st.at(f"norm{l}.scales")
            for t in range(NT):
                nc.vector.tensor_scalar(xn[:, t, :], x[:, t, :], rs[:, t:t + 1], None, ALU.mult)
            st.at(f"norm{l}.scaled")
            for half in range(2):
                st.at(f"norm{l}.turned{half}")
                for k in range(8 * half + 1, 8 * half + 8, 2):
                    for c, a, b in COND:
                        nc.vector.tensor_scalar(h32[:, k, a:b], banks[k % 8][:, a:b], G_scale[:, k, c:c + 1],
                                                mod[:, l, k, c:c + 1], ALU.mult, ALU.add)
                st.at(f"norm{l}.copied{half}")
                split_h("dve", range(2 * half, 2 * half + 2))
            st.at(f"norm{l}.split")

        def dve_out(dve, st, l):
            nc.vector.tensor_tensor(G_small, mod[:, l, 32:48, :],
                                    vec("norm_post", 16 * l).unsqueeze(2).broadcast_to([P, KT, 2]), ALU.mult)
            st.at(f"out{l}.gate")
            st.at(f"out{l}.gate_spread")
            for b in range(1, 8, 2):
                nc.vector.tensor_copy(gate_bc[:, b // 4, (b % 4) * 512:(b % 4 + 1) * 512], banks[b][:, :])
            st.at(f"out{l}.gate_copied")

            def write(i, u, half):
                nc.vector.tensor_copy(o_sb[:, 2, bass.ds(i * 1024 + u * GC, GC)], banks[4 * half + 2][:, :])
            stream("dve", f"out{l}", write)
            st.at(f"out{l}.projected")
            st.at(f"out{l}.stats")
            nc.vector.reciprocal(rs, rs)
            st.at(f"out{l}.rstd")
            for t in range(NT):
                nc.vector.scalar_tensor_tensor(out=o_sb[:, t, :], in0=o_sb[:, t, :], scalar=rs[:, t:t + 1],
                                               in1=gate_bc[:, TILE_COND[t], :], op0=ALU.mult, op1=ALU.mult)
            dve.wait_ge(x_back, 16 * parked(l))
            st.at(f"out{l}.scaled")
            for t in range(NT):
                nc.vector.tensor_tensor(x[:, t, :], x[:, t, :], o_sb[:, t, :], ALU.add)
            st.at(f"out{l}.added")

        def dve_mla(dve, st, l):
            def q_write(i, u, half):
                nc.vector.tensor_copy(qr[:, bass.ds(i * 2 + u, 1), :], banks[4 * half + 2][:, 0:TOK])
            stream("dve", f"q{l}", q_write)
            stream("dve", f"ckv{l}")
            dve.wait_ge(x_saved, 16 * parked(l))

            def krope_write(i, u, half):
                for t in range(NT):
                    for d in range(2):
                        nc.vector.tensor_copy(kr_sb[:, t, d * ROPE:(d + 1) * ROPE], banks[4 * half + t][:, 0:ROPE])
            stream("dve", f"krope{l}", krope_write, share=2)
            stream("dve", f"gate{l}")
            st.at(f"mix{l}.projected")
            nc.vector.reciprocal(rs, rs)
            st.at(f"mix{l}.kv_rstd")
            dve.wait_ge(small_in, 16 * MLA_LOADS * (nth(l) + 1))
            for t in range(NT):
                nc.vector.scalar_tensor_tensor(out=ckv_sb[:, t, :], in0=ckv_sb[:, t, :], scalar=rs[:, t:t + 1],
                                               in1=gamma, op0=ALU.mult, op1=ALU.mult)
            st.at(f"mix{l}.kv_normed")
            st.at(f"mix{l}.kv_transposed")
            nc.vector.tensor_copy(krT, banks[4][:, :])
            for kt in range(4):
                dve.wait_ge(ckv_hi_ready, 4 * nth(l) + kt + 1)
                nc.vector.tensor_tensor(ckv_lo[:, kt, :], banks[kt][:, :], ckv_hi[:, kt, :], ALU.subtract)
            st.at(f"mix{l}.kv_copied")
            st.at(f"mix{l}.rotated")
            for j in range(9):
                dst = qr[:, j, CTX:TOK] if j < 8 else krT[:, CTX:TOK]
                nc.vector.tensor_tensor(rope_tmp[:, j % 2, :], banks[j // 2][:, (j % 2) * LAT:(j % 2 + 1) * LAT], sin_t, ALU.mult)
                nc.vector.tensor_tensor(dst, dst, cos_t, ALU.mult)
                nc.vector.drain()
                nc.vector.tensor_tensor(dst, dst, rope_tmp[:, j % 2, :], ALU.add)
            nc.vector.memset(kr_pad, 0.0)
            nc.vector.drain()
            for hh in range(2):
                rows = slice(hh * ROPE, (hh + 1) * ROPE)
                nc.vector.tensor_copy(kr_pad[rows, hh, :], krT[rows, :])
            dve.wait_ge(stored, 32 * (nth(l) + 1))
            st.at(f"mix{l}.roped")
            base = 16 * nth(l)

            def maxes(h):
                dve.wait_ge(scores_ready, base + h + 1)
                for t in range(3):
                    nc.vector.reduce_max(mx[:, 4 + t:5 + t], score_bank(h, t), AX.X)
                nc.vector.drain()
                nc.vector.tensor_scalar(mx[:, 0:3], mx[:, 4:7], -SM_SCALE, None, ALU.mult)
                nc.vector.drain().then_inc(maxes_ready, 1)

            def normalize(h):
                dve.wait_ge(exps_ready, base + h + 1)
                nc.vector.reciprocal(sm[:, 4:7], sm[:, 0:3])
                nc.vector.drain()
                for t in range(3):
                    a, b = seen(t)
                    p = p_sb[:, h % 2, t, 0:b - a]
                    nc.vector.tensor_scalar(p, p, sm[:, 4 + t:5 + t], None, ALU.mult)
                nc.vector.drain().then_inc(probs_ready, 1)

            def gate_head(h):
                dve.wait_ge(heads_ready, base + h + 1)
                nc.vector.tensor_tensor(h32[:, h, :], banks[6][:, 0:TOK], gateT[:, h, :], ALU.mult)
                nc.vector.drain().then_inc(heads_done, 1)

            for j in (1, 3):
                copy_piece("dve", l, 0, j)
            split_pair("dve", l, 1)
            maxes(0)
            normalize(0)
            for h in range(HEADS):
                if h + 1 < HEADS:
                    maxes(h + 1)
                if h:
                    gate_head(h - 1)
                if h + 1 < HEADS:
                    normalize(h + 1)
                dve.wait_ge(probsT_ready, base + h + 1)
                nc.vector.tensor_copy(pT[:, 3, :], banks[5][:, 0:LAT])
                nc.vector.tensor_copy(pT[:, 0, 0:P], banks[5][:, LAT:LAT + P])
                nc.vector.drain().then_inc(probsT_copied, 1)
                if h // 2 + 1 < 8:
                    copy_piece("dve", l, h // 2 + 1, 2 * (h % 2) + 1)
                if h % 2 and h < 14:
                    split_pair("dve", l, (h + 3) // 2)
            gate_head(HEADS - 1)
            for half in range(2):
                nc.vector.sem_inc(sums_taken[half], 2)
            st.at(f"mix{l}.attended")
            split_h("dve")
            st.at(f"mix{l}.split")




        g_q = view(0, 8, TOK)
        g_k = view(3072, 8, TOK)
        g_v = view(6144, NT, D)
        g_r = view(12288, KT, TOK)
        g_glr = view(18432, TOK)
        g_w2 = view(18816, 2, GH * GDK)
        g_mask = view(20864, 2, P)
        g_edge = view(21120, TOK)
        g_gamma = view(21504, GDV)
        g_dn = view(22016, 2, 6)
        g_stat = view(22028, 8)
        g_qt = view(18432, 2, TOK)
        g_kt = view(19200, 2, TOK)
        g_kd = view(19968, 2, TOK)
        g_tmp = scratch[:, 6144:12288]
        g_o = g_tmp[:, 0:1536].rearrange("p (a b) -> p a b", a=3)
        g_att = g_tmp[:, 1536:2304].rearrange("p (d a b) -> p d a b", d=2, a=3)
        g_kdT = [g_tmp[:, 2304:3072].rearrange("p (a b) -> p a b", a=3), view(22040, 3, 2 * P)]
        g_sc = g_tmp[:, 3072:4096].rearrange("p (a b) -> p a b", a=2)
        g_sl = g_tmp[:, 4096:6144].rearrange("p (n a b) -> p n a b", n=2, a=2)
        hT_flat = scratch[:, 0:6144]

        def g_gate(h, d):
            return h32[:, 4 * h + 2 * d:4 * h + 2 * d + 2, :]

        x_saved = sem("x_saved")
        x_back = sem("x_back")
        g_small = sem("g_small")
        g_state_in = [sem("g_state_in0"), sem("g_state_in1")]
        g_cum_ready = sem("g_cum_ready")
        g_exp_ready = sem("g_exp_ready")
        g_decayed = sem("g_decayed")
        g_att_ready = sem("g_att_ready")
        g_att_copied = sem("g_att_copied")
        g_upd_ready = sem("g_upd_ready")
        g_state_new = sem("g_state_new")
        g_unit_done = sem("g_unit_done")
        g_ctx_stored = sem("g_ctx_stored")
        g_o_normed = sem("g_o_normed")
        g_ssq_ready = sem("g_ssq_ready")
        g_o_turned = sem("g_o_turned")
        g_head_done = sem("g_head_done")

        def g_steps(d):
            c = [("c", 0, b) for b in ((0, 1), (1, 0))[d]]
            l_ = [("l", t, b) for t in ((1, 2), (2, 1))[d] for b in ((0, 1), (1, 0))[d]]
            order = [c[0], l_[0], c[1], l_[1], l_[2], l_[3]]
            return [(k, t, b, (k, t, b) in (c[0], l_[0]), (k, t, b) == l_[-1]) for k, t, b in order]

        UPD = 5

        def pe_gla(pe, st, l):
            for name, groups in (("q", 2), ("k", 2)):
                def body(i, g0, u):
                    group_sums(pe, i, g0, u, [P] * 4)
                loop_groups(nc.tensor, f"{name}{l}", groups, body)

            def v_body(i, g0, u):
                group_sums(pe, i, g0, u, None)
            loop_groups(nc.tensor, f"v{l}", 4, v_body)

            def r_body(i, g0, u):
                group_sums(pe, i, g0, u, [P] * 4)
            loop_groups(nc.tensor, f"r{l}", 4, r_body)
            group_sums(pe, 0, FIRST_GROUP[f"glr{l}"], 0, [2 * GRANK])
            st.at(f"mix{l}.projected")
            pe.wait_ge(g_small, 16 * 5)
            for d in range(2):
                for t in range(8):
                    nc.tensor.matmul(banks[t][:, 0:TOK], g_w2[0:2 * GRANK, d, t * P:(t + 1) * P],
                                     g_glr[0:2 * GRANK, :], start=True, stop=True)
                st.at(f"mix{l}.z{d}")
                st.at(f"mix{l}.z_taken{d}")
            for s in ("abs", "softplus", "log_gates"):
                st.at(f"mix{l}.{s}")
            for h in range(GH):
                vh = slice(h * GDV, (h + 1) * GDV)
                for d in range(2):
                    n = 2 * h + d
                    pe.wait_ge(g_decayed, n + 1)
                    if n:
                        pe.wait_ge(g_state_new, UPD * n)
                    for t in range(NT):
                        for j in range(2):
                            at = (2 * t + j) * P
                            nc.tensor.transpose(banks[at // 512][:, at % 512:at % 512 + P],
                                                g_kd[:, j, t * P:(t + 1) * P], ident[:, :])
                    for t in range(NT):
                        for j in range(2):
                            nc.tensor.matmul(banks[2][:, t * P:(t + 1) * P], g_kt[:, j, t * P:(t + 1) * P],
                                             g_qt[:, j, t * P:(t + 1) * P], start=(j == 0), stop=(j == 1))
                    nc.tensor.drain().then_inc(g_att_ready, 1)
                    pe.wait_ge(g_att_copied, 2 * (n + 1))
                    if d == 0 and h:
                        pe.wait_ge(g_o_normed, h)
                    pe.wait_ge(g_state_in[n % 2], 16 * (n // 2 + 1))
                    for t in range(NT):
                        nc.tensor.matmul(banks[3 + t][:, :], g_att[:, d, t, :], g_v[:, t, vh],
                                         start=(d == 0), stop=False, skip_group_check=True)
                    done = {"c": 0, "l": 0}
                    m = 0
                    for step, (chain, t, b, first, last) in enumerate(g_steps(d)):
                        rows = slice(b * GCH, (b + 1) * GCH)
                        toks = slice(t * P + b * GCH, t * P + (b + 1) * GCH)
                        if not last:
                            pair = (6, 0)[m % 2]
                            if m >= 2:
                                pe.wait_ge(g_state_new, UPD * n + m - 1)
                            for j in range(2):
                                nc.tensor.matmul(banks[pair + j][:, :], g_kdT[b][:, t, j * P:(j + 1) * P],
                                                 g_v[:, t, vh], start=True, stop=True)
                        if not first:
                            pe.wait_ge(g_state_new, UPD * n + done[chain])
                        if not (first and chain == "c"):
                            state = g_sc if chain == "c" else g_sl[:, n % 2, :, :]
                            for j in range(2):
                                nc.tensor.matmul(banks[3 + t][rows, :], g_qt[:, j, toks], state[:, j, :],
                                                 start=False, stop=True, skip_group_check=True)
                        if not last:
                            nc.tensor.drain().then_inc(g_upd_ready, 1)
                            m += 1
                            done[chain] = m
                    nc.tensor.drain().then_inc(g_unit_done, 1)
                pe.wait_ge(g_o_normed, h + 1)
                pe.wait_ge(g_state_new, UPD * (2 * h + 2))
                for q in range(4):
                    for t in range(NT):
                        nc.tensor.transpose(banks[(0, 1, 2, 6)[q]][:, t * P:(t + 1) * P],
                                            g_o[:, t, q * P:(q + 1) * P], ident[:, :])
                nc.tensor.drain().then_inc(g_o_turned, 1)
                pe.wait_ge(g_head_done, h + 1)
            st.at(f"mix{l}.attended")
            st.at(f"mix{l}.split")

        def act_gla(act, st, l):
            for name, dst in (("q", g_q), ("k", g_k)):
                def write(i, u, half, dst=dst):
                    for m in range(2):
                        act_copy(dst[:, 4 * u + m, :], banks[4 * half + m][:, 0:TOK])
                stream("act", f"{name}{l}", write)

            def v_write(i, u, half):
                for t in range(2):
                    act_copy(g_v[:, t, bass.ds(i * 1024 + u * GC, GC)], banks[4 * half + t][:, :])
            stream("act", f"v{l}", v_write)

            def r_write(i, u, half):
                for m in range(4):
                    nc.scalar.activation(g_r[:, bass.ds(i * 8 + 4 * u + m, 1), :], banks[4 * half + m][:, 0:TOK], ACT.Silu)
            act.wait_ge(x_saved, 16 * parked(l))
            stream("act", f"r{l}", r_write, share=2)
            stream("act", f"glr{l}")
            st.at(f"mix{l}.projected")
            for s in ("z0", "z_taken0", "z1", "z_taken1", "abs"):
                st.at(f"mix{l}.{s}")
            nc.scalar.activation(g_tmp, g_tmp, ACT.Exp)
            nc.scalar.drain()
            nc.scalar.activation(g_tmp, g_tmp, ACT.Ln, bias=1.0)
            st.at(f"mix{l}.softplus")
            st.at(f"mix{l}.log_gates")
            S = 1.0 / GATE_NORM
            for h in range(GH):
                for d in range(2):
                    n = 2 * h + d
                    act.wait_ge(g_cum_ready, n + 1)
                    if n:
                        act.wait_ge(g_unit_done, n)
                    b = g_gate(h, d)
                    nc.scalar.activation(g_qt, b, ACT.Exp, scale=S)
                    nc.scalar.activation(g_kt, b, ACT.Exp, scale=-S)
                    nc.scalar.activation(g_kd, g_kd, ACT.Exp, scale=S)
                    edge = (GCH - 1, 0)[d]
                    nc.scalar.activation(g_dn, b[:, :, edge::GCH], ACT.Exp, scale=S)
                    nc.scalar.drain().then_inc(g_exp_ready, 1)
                    act.wait_ge(g_att_ready, n + 1)
                    for b_ in range(2):
                        rows = slice(b_ * GCH, (b_ + 1) * GCH)
                        act_copy(g_kdT[b_][rows, 0:2, :], banks[0][rows, :].rearrange("p (a b) -> p a b", a=2))
                        act_copy(g_kdT[b_][rows, 2, :], banks[1][rows, 0:2 * P])
                    nc.scalar.drain().then_inc(g_att_copied, 1)
                act.wait_ge(g_unit_done, 2 * h + 2)
                if h:
                    act.wait_ge(g_head_done, h)
                for t in range(NT):
                    nc.scalar.activation(g_o[:, t, :], banks[3 + t][:, :], ACT.Square, accum_out=g_stat[:, t:t + 1])
                nc.scalar.drain()
                nc.scalar.activation(g_stat[:, 3:6], g_stat[:, 0:3], ACT.Sqrt, scale=1.0 / GDV, bias=eps_c)
                nc.scalar.drain().then_inc(g_ssq_ready, 1)
            st.at(f"mix{l}.attended")
            act.wait_ge(g_ctx_stored, 16 * 2 * GH)
            split_h("act")
            st.at(f"mix{l}.split")

        def dve_gla(dve, st, l):
            for name, dst in (("q", g_q), ("k", g_k)):
                def write(i, u, half, dst=dst):
                    for m in range(2, 4):
                        nc.vector.tensor_copy(dst[:, 4 * u + m, :], banks[4 * half + m][:, 0:TOK])
                stream("dve", f"{name}{l}", write)

            def v_write(i, u, half):
                nc.vector.tensor_copy(g_v[:, 2, bass.ds(i * 1024 + u * GC, GC)], banks[4 * half + 2][:, :])
            stream("dve", f"v{l}", v_write)

            def glr_write(i, u, half):
                nc.vector.tensor_copy(g_glr[0:2 * GRANK, :], banks[4 * half][0:2 * GRANK, 0:TOK])
            stream("dve", f"r{l}")
            dve.wait_ge(x_saved, 16 * parked(l))
            stream("dve", f"glr{l}", glr_write, share=2)
            st.at(f"mix{l}.projected")
            for d in range(2):
                st.at(f"mix{l}.z{d}")
                for t in range(8):
                    nc.vector.tensor_scalar(h32[:, 4 * (t // 2) + 2 * d + t % 2, :], banks[t][:, 0:TOK],
                                            vec("gla_b_g", 8 * d + t, 1), None, ALU.add)
                st.at(f"mix{l}.z_taken{d}")
            nc.vector.scalar_tensor_tensor(out=g_tmp, in0=hT_flat, scalar=-1.0, in1=hT_flat, op0=ALU.mult, op1=ALU.min)
            st.at(f"mix{l}.abs")
            st.at(f"mix{l}.softplus")
            nc.vector.scalar_tensor_tensor(out=hT_flat, in0=hT_flat, scalar=0.0, in1=g_tmp, op0=ALU.min,
                                           op1=ALU.subtract)
            st.at(f"mix{l}.log_gates")
            nc.vector.memset(g_att, 0.0)
            for b_ in range(2):
                nc.vector.memset(g_kdT[b_], 0.0)

            def cumulate(n):
                b, way = g_gate(n // 2, n % 2), slice(None, None, (1, -1)[n % 2])
                for j in range(2):
                    nc.vector.tensor_tensor_scan(b[:, j, way], g_edge, b[:, j, way], 0.0, ALU.mult, ALU.add)

            cumulate(0)
            nc.vector.drain()
            for h in range(GH):
                for d in range(2):
                    n = 2 * h + d
                    b = g_gate(h, d)
                    if n:
                        dve.wait_ge(g_unit_done, n)
                    edge = (GCH - 1, 0)[d]
                    for j in range(2):
                        bj = b[:, j, :].rearrange("p (c t) -> p c t", t=GCH)
                        nc.vector.tensor_tensor(g_kd[:, j, :].rearrange("p (c t) -> p c t", t=GCH),
                                                bj[:, :, edge:edge + 1].broadcast_to([P, 6, GCH]), bj, ALU.subtract)
                    nc.vector.drain().then_inc(g_cum_ready, 1)
                    dve.wait_ge(g_exp_ready, n + 1)
                    qh, kh = g_q[:, 2 * h:2 * h + 2, :], g_k[:, 2 * h:2 * h + 2, :]
                    nc.vector.scalar_tensor_tensor(out=g_qt, in0=g_qt, scalar=GDK ** -0.5, in1=qh, op0=ALU.mult,
                                                   op1=ALU.mult)
                    nc.vector.tensor_tensor(g_kt, g_kt, kh, ALU.mult)
                    nc.vector.tensor_tensor(g_kd, g_kd, kh, ALU.mult)
                    nc.vector.drain().then_inc(g_decayed, 1)
                    if n + 1 < 2 * GH:
                        cumulate(n + 1)
                    dve.wait_ge(g_att_ready, n + 1)
                    nc.vector.copy_predicated(g_att[:, d, :, :], g_mask[:, d, :].bitcast(U32).unsqueeze(1).broadcast_to([P, 3, P]),
                                              banks[2][:, 0:TOK].rearrange("p (a b) -> p a b", a=3))
                    nc.vector.drain().then_inc(g_att_copied, 1)
                    m = 0
                    for chain, t, bb, first, last in g_steps(d):
                        if last:
                            continue
                        dve.wait_ge(g_upd_ready, UPD * n + m + 1)
                        state = g_sc if chain == "c" else g_sl[:, n % 2, :, :]
                        pair = (6, 0)[m % 2]
                        c = 2 * t + bb
                        if first and chain == "c" and n:
                            dve.wait_ge(g_ctx_stored, 16 * n)
                        for j in range(2):
                            if first and chain == "c":
                                nc.vector.tensor_copy(state[:, j, :], banks[pair + j][:, :])
                            else:
                                nc.vector.scalar_tensor_tensor(out=state[:, j, :], in0=state[:, j, :],
                                                               scalar=g_dn[:, j, c:c + 1], in1=banks[pair + j][:, :],
                                                               op0=ALU.mult, op1=ALU.add)
                        nc.vector.drain().then_inc(g_state_new, 1)
                        m += 1
                dve.wait_ge(g_ssq_ready, h + 1)
                nc.vector.reciprocal(g_stat[:, 3:6], g_stat[:, 3:6])
                nc.vector.drain()
                for t in range(NT):
                    nc.vector.scalar_tensor_tensor(out=g_o[:, t, :], in0=banks[3 + t][:, :], scalar=g_stat[:, 3 + t:4 + t],
                                                   in1=g_gamma, op0=ALU.mult, op1=ALU.mult)
                nc.vector.drain().then_inc(g_o_normed, 1)
                dve.wait_ge(g_o_turned, h + 1)
                for q in range(4):
                    nc.vector.tensor_tensor(h32[:, 4 * h + q, :], banks[(0, 1, 2, 6)[q]][:, 0:TOK], g_r[:, 4 * h + q, :],
                                            ALU.mult)
                nc.vector.drain().then_inc(g_head_done, 1)
            st.at(f"mix{l}.attended")
            split_h("dve")
            st.at(f"mix{l}.split")

        def parked(l):
            return sum(1 for m in layers if m <= l)

        def park_x(pool, l):
            pool.wait_ge(stage_done, after(f"norm{l}.stats"))
            nc.gpsimd.dma_start(x_dram.rearrange("t p d -> p t d"), x).then_inc(x_saved, 16)
            pool.wait_ge(x_saved, 16 * parked(l))

        def fetch_x(pool, l):
            pool.wait_ge(stage_done, after(f"mix{l}.split"))
            nc.gpsimd.dma_start(x, x_dram.rearrange("t p d -> p t d")).then_inc(x_back, 16)

        def pool_gla(pool, l):
            pool.wait_ge(stage_done, after(f"norm{l}.copied1"))
            nc.gpsimd.memset(g_w2[0:2 * GRANK, :, :], 0.0).then_inc(g_w2_zero, 1)
            pool.wait_ge(g_w2_zero, 1)
            for d in range(2):
                nc.gpsimd.dma_start(g_w2[d * GRANK:(d + 1) * GRANK, d, :], w["gla_w_g2"][0, d]).then_inc(g_small, 16)
            nc.gpsimd.dma_start(g_mask, consts["gla_mask"]).then_inc(g_small, 16)
            nc.gpsimd.dma_start(g_edge, consts["gla_edge"]).then_inc(g_small, 16)
            nc.gpsimd.dma_start(g_gamma, w["gla_norm"][0:1, :].broadcast_to([P, GDV])).then_inc(g_small, 16)
            pool.wait_ge(stage_done, after(f"mix{l}.log_gates"))
            for n in range(2 * GH):
                h, d = n // 2, n % 2
                if n >= 2:
                    pool.wait_ge(g_unit_done, n - 1)
                nc.gpsimd.dma_start(g_sl[:, n % 2, :, :], w["state_gla"][0, 0, d, h].rearrange("(a p) v -> p a v", p=P))\
                    .then_inc(g_state_in[n % 2], 16)
                if n:
                    pool_store_state(pool, n - 1)
            pool_store_state(pool, 2 * GH - 1)
            pool.wait_ge(g_ctx_stored, 16 * 2 * GH)

        def pool_store_state(pool, n):
            pool.wait_ge(g_state_new, UPD * n + 3)
            nc.gpsimd.dma_start(outs[5][0, 0, n % 2, n // 2].rearrange("(a p) v -> p a v", p=P), g_sc)\
                .then_inc(g_ctx_stored, 16)

        g_w2_zero = sem("g_w2_zero")
        x_dram = nc.dram_tensor("x_saved_dram", (NT, P, D), F32, kind="Internal").ap()


        x_in = sem("x_in")
        hT_words = scratch[:, 0:6144]
        x_words = scratch[:, 6144:12288]
        DG = P
        b_st = hT_words[:, 0:4096].rearrange("p (r q g) -> p r q g", r=2, q=SC)
        bd = hT_words[:, 4096:5120].rearrange("p (r d g m) -> p r d g m", r=2, d=2, g=8)
        c_st = x_words[:, 0:4096].rearrange("p (r g q) -> p r g q", r=2, q=SC)
        kw = x_words[0:32, 4096:4096 + 1920].rearrange("p (g n) -> p g n", g=8)
        diag = hT_words[0:32, 5120:5136]
        d_st = hT_words[0:32, 5136:5200]
        pw = view(6144, 2, 9, DG)
        wb = view(8448, 2, 2, 8, 128)
        ca = view(12544, 2, 2, 8, 144)
        wbt = view(17152, 8, 2, 4, SN)
        s5_t = view(21248, 1152)
        rowb = view(8448, 2, 2048)
        rowc = view(12544, 2, 2, 16, SN)
        bbar = view(16640, 2, 2048)
        rowt = view(0, 6144)
        def row(n, k=1):
            return rowt[:, n * P:(n + k) * P]
        a_re, a_im, dt2 = row(0), row(1), rowt[:, 256:258]
        er, th, kk_, sn, cs = row(3), row(4), row(5, 2), row(7), row(8)
        f_re, f_im, den, tr = row(9), row(10), row(11), row(12)
        pr = rowt[:, 13 * P:13 * P + 18 * P].rearrange("p (r k n) -> p r k n", r=2, k=9)
        tp = rowt[:, 31 * P:39 * P]
        a8 = sb("a8", [P, 3, DG])
        s5_loaded = sem("s5_loaded")
        s5_ready = sem("s5_ready")
        s5_turned = sem("s5_turned")
        s5_turned_copied = sem("s5_turned_copied")
        s5_k_ready = sem("s5_k_ready")
        s5_k_copied = sem("s5_k_copied")
        s5_k_done = sem("s5_k_done")
        s5_stored = sem("s5_stored")
        S5_STORES = 4 + 2 + 2 * ST
        wbt_dram = nc.dram_tensor("s5_in_dram", (16, P, 2048), F32, kind="Internal").ap()
        ca_dram = nc.dram_tensor("s5_out_dram", (8, P, 2, 8, 2, 128), F32, kind="Internal").ap()
        k_dram = nc.dram_tensor("s5_k_dram", (8, ST, SC, 16, 128), F32, kind="Internal").ap()
        ud_dram = nc.dram_tensor("s5_u_dram", (D, TOK), F32, kind="Internal").ap()
        gate_dram = nc.dram_tensor("s5_gate_dram", (P, KT * TOK), F32, kind="Internal").ap()

        def pool_s5_basics(pool):
            pool.wait_ge(stage_done, after("silu_c"))
            ld = lambda dst, src: nc.gpsimd.dma_start(dst, src).then_inc(s5_loaded, 16)
            ld(a_re, w["s5_a_re"].rearrange("b d (g h) n -> (b d g) (h n)", h=2))
            ld(a_im, w["s5_a_im"].rearrange("b d (g h) n -> (b d g) (h n)", h=2))
            ld(dt2, w["s5_log_dt"].rearrange("b d (g h) -> (b d g) h", h=2))
            for r, (bn, cn) in enumerate((("s5_b_re", "s5_c_re"), ("s5_b_im", "s5_c_im"))):
                ld(rowb[:, r, :], w[bn].rearrange("b d (g h) n p -> (b d g) (h n p)", h=2))
                for d in range(2):
                    ld(rowc[:, r, d, :, :], w[cn][0, d].rearrange("(t g) p n -> (g p) t n", g=8))
            for g2 in range(2):
                ld(diag[16 * g2:16 * g2 + 16, :], consts["ident"][0:16, 0:16])

        S5_LOADS = 11

        def pe_s5_basics(pe, st):
            for s in ("loaded", "dt", "angle", "reduced", "sines", "poles"):
                st.at(f"s5.{s}")
            for a in range(4):
                nc.tensor.matmul(banks[7][0:32, a * KT:(a + 1) * KT], ident[:, 32 * a:32 * a + 32], vec("d"),
                                 start=True, stop=True)
            for n in range(3):
                for m in range(6):
                    i = 6 * n + m
                    nc.tensor.transpose(banks[m // 4][:, (m % 4) * P:(m % 4 + 1) * P], pr[:, i // 9, i % 9, :], ident[:, :])
                st.at(f"s5.turned_pow{n}")
                st.at(f"s5.copied_pow{n}")
            for n in range(4):
                for m in range(8):
                    i = 8 * n + m
                    r, q = i // SC, i % SC
                    nc.tensor.transpose(banks[m // 4][:, (m % 4) * P:(m % 4 + 1) * P],
                                        bbar[:, r, q::SC], ident[:, :])
                st.at(f"s5.turned_b{n}")
                st.at(f"s5.copied_b{n}")
            for n in range(4):
                r, d = n // 2, n % 2
                for t in range(16):
                    for g2 in range(2):
                        cols = ident[:, :].rearrange("p (a h q) -> p a h q", h=2, q=SC)[:, :, g2, :]
                        nc.tensor.matmul(banks[t // 8][g2 * 64:(g2 + 1) * 64, (t % 8) * 64:(t % 8 + 1) * 64],
                                         rowc[:, r, d, t, :], cols, start=True, stop=True)
                st.at(f"s5.turned_c{n}")
                st.at(f"s5.copied_c{n}")

        def act_s5_basics(act, st):
            st.at("s5.loaded")
            act.wait_ge(s5_loaded, 16 * S5_LOADS)
            nc.scalar.activation(dt2, dt2, ACT.Exp)
            st.at("s5.dt")
            st.at("s5.angle")
            nc.scalar.activation(er, er, ACT.Exp)
            st.at("s5.reduced")
            nc.scalar.activation(sn, sn, ACT.Sin)
            nc.scalar.activation(cs, cs, ACT.Sin)
            st.at("s5.sines")
            st.at("s5.poles")
            for n in range(3):
                st.at(f"s5.turned_pow{n}")
                st.at(f"s5.copied_pow{n}")
            for n in range(4):
                st.at(f"s5.turned_b{n}")
                i = 8 * n
                act_copy(b_st[:, i // SC, i % SC:i % SC + 4, :], banks[0][:, :].rearrange("p (a b) -> p a b", a=4))
                act_copy(b_st[:, i // SC, i % SC + 4:i % SC + 8, :], banks[1][:, :].rearrange("p (a b) -> p a b", a=4))
                st.at(f"s5.copied_b{n}")
            for n in range(4):
                st.at(f"s5.turned_c{n}")
                r, d = n // 2, n % 2
                for k in range(2):
                    act_copy(c_st[:, r, d * 64 + k * 32:d * 64 + k * 32 + 32, :],
                             banks[k][:, :].rearrange("p (a b) -> p a b", b=SC))
                st.at(f"s5.copied_c{n}")

        def cmul(out_re, out_im, ar_, ai_, br, bi, t):
            v = nc.vector
            v.tensor_tensor(out_re, ar_, br, ALU.mult)
            v.tensor_tensor(t, ai_, bi, ALU.mult)
            v.drain()
            v.tensor_tensor(out_re, out_re, t, ALU.subtract)
            v.tensor_tensor(out_im, ar_, bi, ALU.mult)
            v.drain()
            v.tensor_tensor(t, ai_, br, ALU.mult)
            v.drain()
            v.tensor_tensor(out_im, out_im, t, ALU.add)
            v.drain()

        TWO_PI = 2 * np.pi
        PI_HI = float(np.float32(6.28125))
        PI_MID = float(np.float32(TWO_PI - 6.28125))
        PI_LO = float(np.float32(TWO_PI - 6.28125 - np.float64(np.float32(TWO_PI - 6.28125))))
        ROUND = float(np.float32(1.5 * 2 ** 23))
        PI_IN = float(np.nextafter(np.float32(np.pi), np.float32(0)))

        def dve_s5_basics(dve, st):
            v = nc.vector
            v.memset(bd, 0.0)
            st.at("s5.loaded")
            dve.wait_ge(s5_loaded, 16 * S5_LOADS)
            st.at("s5.dt")
            dtb = dt2.unsqueeze(2).broadcast_to([P, 2, SN])
            v.tensor_tensor(er.rearrange("p (h n) -> p h n", h=2), a_re.rearrange("p (h n) -> p h n", h=2), dtb, ALU.mult)
            v.tensor_tensor(th.rearrange("p (h n) -> p h n", h=2), a_im.rearrange("p (h n) -> p h n", h=2), dtb, ALU.mult)
            st.at("s5.angle")
            for out, quarter, k in ((sn, 0.0, kk_[:, 0:P]), (cs, 0.25, kk_[:, P:2 * P])):
                v.tensor_scalar(k, th, 1.0 / TWO_PI, quarter, ALU.mult, ALU.add)
                v.drain()
                v.tensor_scalar(k, k, ROUND, None, ALU.add)
                v.drain()
                v.tensor_scalar(k, k, -ROUND, None, ALU.add)
                v.drain()
                v.scalar_tensor_tensor(out=out, in0=k, scalar=-PI_HI, in1=th, op0=ALU.mult, op1=ALU.add)
                v.drain()
                v.scalar_tensor_tensor(out=out, in0=k, scalar=-PI_MID, in1=out, op0=ALU.mult, op1=ALU.add)
                v.drain()
                v.scalar_tensor_tensor(out=out, in0=k, scalar=-PI_LO, in1=out, op0=ALU.mult, op1=ALU.add)
                v.drain()
                if quarter:
                    v.tensor_scalar(out, out, float(np.pi / 2), None, ALU.add)
                    v.drain()
                v.tensor_scalar(out, out, PI_IN, -PI_IN, ALU.min, ALU.max)
            st.at("s5.reduced")
            st.at("s5.sines")
            one = pr[:, 0, 0, :]
            v.memset(one, 1.0)
            v.memset(pr[:, 1, 0, :], 0.0)
            v.tensor_tensor(pr[:, 0, 1, :], er, cs, ALU.mult)
            v.tensor_tensor(pr[:, 1, 1, :], er, sn, ALU.mult)
            v.tensor_tensor(den, a_re, a_re, ALU.mult)
            v.tensor_tensor(tr, a_im, a_im, ALU.mult)
            v.drain()
            v.tensor_tensor(den, den, tr, ALU.add)
            v.drain()
            v.reciprocal(den, den)
            v.tensor_scalar(tr, pr[:, 0, 1, :], -1.0, None, ALU.add)
            v.drain()
            v.tensor_tensor(f_re, tr, a_re, ALU.mult)
            v.tensor_tensor(tp[:, 0:P], pr[:, 1, 1, :], a_im, ALU.mult)
            v.tensor_tensor(f_im, pr[:, 1, 1, :], a_re, ALU.mult)
            v.tensor_tensor(tp[:, P:2 * P], tr, a_im, ALU.mult)
            v.drain()
            v.tensor_tensor(f_re, f_re, tp[:, 0:P], ALU.add)
            v.tensor_tensor(f_im, f_im, tp[:, P:2 * P], ALU.subtract)
            v.drain()
            v.tensor_tensor(f_re, f_re, den, ALU.mult)
            v.tensor_tensor(f_im, f_im, den, ALU.mult)
            v.drain()
            for lo, n in ((1, 1), (1, 2), (1, 4)):
                by = n
                def pow_(r, k0, k):
                    return pr[:, r, k0:k0 + k, :]
                def rep_(r):
                    return pr[:, r, by:by + 1, :].broadcast_to([P, n, P])
                cmul(pow_(0, n + 1, n), pow_(1, n + 1, n), pow_(0, 1, n), pow_(1, 1, n), rep_(0), rep_(1),
                     tp[:, 0:n * P].rearrange("p (k n) -> p k n", k=n))
            fb = [f.unsqueeze(2).broadcast_to([P, P, SC]) for f in (f_re, f_im)]
            rb = [rowb[:, r, :].rearrange("p (n q) -> p n q", q=SC) for r in range(2)]
            bb = [bbar[:, r, :].rearrange("p (n q) -> p n q", q=SC) for r in range(2)]
            cmul(bb[0], bb[1], fb[0], fb[1], rb[0], rb[1], view(20736, P, SC))
            st.at("s5.poles")
            for n in range(3):
                st.at(f"s5.turned_pow{n}")
                if n == 0:
                    v.tensor_copy(d_st.rearrange("p (t a) -> p a t", a=4),
                                  banks[7][0:32, 0:64].rearrange("p (a t) -> p a t", a=4))
                for m in range(6):
                    i = 6 * n + m
                    v.tensor_copy(pw[:, i // 9, i % 9, :], banks[m // 4][:, (m % 4) * P:(m % 4 + 1) * P])
                st.at(f"s5.copied_pow{n}")
            v.tensor_copy(a8[:, 0, :], pw[:, 0, 8, :])
            v.tensor_scalar(a8[:, 1, :], pw[:, 1, 8, :], -1.0, None, ALU.mult)
            v.tensor_copy(a8[:, 2, :], pw[:, 1, 8, :])
            for n in range(4):
                st.at(f"s5.turned_b{n}")
                st.at(f"s5.copied_b{n}")
            for n in range(4):
                st.at(f"s5.turned_c{n}")
                st.at(f"s5.copied_c{n}")

        def dve_s5_batch(dve, b):
            v = nc.vector
            if b:
                dve.wait_ge(s5_turned, 8 * b)
                dve.wait_ge(s5_stored, 16 * S5_STORES * b)
            for d in range(2):
                g0 = 64 * d + 8 * b
                def powers(r, ks, n):
                    return pw[:, r, ks, g0:g0 + 8].rearrange("p k g -> p g k").unsqueeze(3).broadcast_to([P, 8, n, SC])
                ks = slice(7, None, -1) if d == 0 else slice(0, 8)
                bsrc = [b_st[:, r, :, g0:g0 + 8].rearrange("p q g -> p g q").unsqueeze(2).broadcast_to([P, 8, 8, SC])
                        for r in range(2)]
                o = [wb[:, r, d, :, :].rearrange("p g (j q) -> p g j q", j=8) for r in range(2)]
                t = s5_t[:, 0:1024].rearrange("p (g j q) -> p g j q", g=8, j=8)
                cmul(o[0], o[1], powers(0, ks, 8), powers(1, ks, 8), bsrc[0], bsrc[1], t)
                ks = slice(0, 9) if d == 0 else slice(8, None, -1)
                csrc = [c_st[:, r, g0:g0 + 8, :].unsqueeze(2).broadcast_to([P, 8, 9, SC]) for r in range(2)]
                o = [ca[:, r, d, :, :].rearrange("p g (j q) -> p g j q", j=9) for r in range(2)]
                t = s5_t[:, 0:1152].rearrange("p (g j q) -> p g j q", g=8, j=9)
                cmul(o[0], o[1], powers(0, ks, 9), powers(1, ks, 9), csrc[0], csrc[1], t)
                v.tensor_scalar(ca[:, 1, d, :, :], ca[:, 1, d, :, :], -1.0, None, ALU.mult)
                for r in range(2):
                    for g2 in range(2):
                        rows = slice(64 * g2, 64 * g2 + 64)
                        v.tensor_copy(bd[rows, r, d, :, 16 * g2:16 * g2 + 16],
                                      b_st[rows, r, :, g0:g0 + 8].rearrange("p q g -> p g q"))
            v.drain().then_inc(s5_ready, 1)
            for n in range(4):
                dve.wait_ge(s5_k_ready, 4 * b + n + 1)
                v.tensor_copy(kw[:, 2 * n:2 * n + 2, :],
                              banks[K_BANKS[n % 2]][0:32, :].rearrange("p (a b) -> p a b", a=2)[:, :, 0:240])
                v.drain().then_inc(s5_k_copied, 1)
            t = s5_t[0:32, 0:128].rearrange("p (g q) -> p g q", g=8)
            v.tensor_tensor(t, d_st[:, 8 * b:8 * b + 8].unsqueeze(2).broadcast_to([32, 8, SC]),
                            diag.unsqueeze(1).broadcast_to([32, 8, SC]), ALU.mult)
            v.drain()
            v.tensor_tensor(kw[:, :, 112:128], kw[:, :, 112:128], t, ALU.add)
            v.drain().then_inc(s5_k_done, 1)

        K_BANKS = (6, 7)
        TURN_BANKS = (1, 2, 3, 5)

        def pe_s5_batch(pe, b):
            pe.wait_ge(s5_ready, b + 1)
            for g in range(8):
                if 8 * b + g >= 4:
                    pe.wait_ge(s5_turned_copied, 8 * b + g - 3)
                for d in range(2):
                    for r in range(2):
                        at = (2 * d + r) * P
                        nc.tensor.transpose(banks[TURN_BANKS[g % 4]][:, at:at + P], wb[:, r, d, g, :], ident[:, :])
                nc.tensor.drain().then_inc(s5_turned, 1)
            for n in range(4):
                if 4 * b + n >= 2:
                    pe.wait_ge(s5_k_copied, 4 * b + n - 1)
                for g in (2 * n, 2 * n + 1):
                    at = (g % 2) * 256
                    for d, q0, c0 in ((1, 1, 0), (0, 0, 112)):
                        for r in range(2):
                            nc.tensor.matmul(banks[K_BANKS[n % 2]][0:32, at + c0:at + c0 + 128], bd[:, r, d, g, :],
                                             ca[:, r, d, g, q0 * SC:q0 * SC + 128],
                                             start=(d == 1 and r == 0), stop=(d == 0 and r == 1), skip_group_check=True)
                nc.tensor.drain().then_inc(s5_k_ready, 1)

        def act_s5_batch(act, b):
            for g in range(8):
                act.wait_ge(s5_turned, 8 * b + g + 1)
                if b and g == 0:
                    act.wait_ge(s5_stored, 16 * S5_STORES * b)
                act_copy(wbt[:, g, :, :, :].rearrange("p h c n -> p c h n"),
                         banks[TURN_BANKS[g % 4]][:, :].rearrange("p (c h n) -> p c h n", c=4, h=2))
                nc.scalar.drain().then_inc(s5_turned_copied, 1)

        def pool_s5_batch(pool, b):
            st_ = lambda dst, src: nc.gpsimd.dma_start(dst, src).then_inc(s5_stored, 16)
            pool.wait_ge(s5_ready, b + 1)
            for r in range(2):
                for d in range(2):
                    q0 = (1, 0)[d]
                    st_(ca_dram[b, :, d, :, r, :], ca[:, r, d, :, q0 * SC:q0 * SC + 128])
            pool.wait_ge(s5_turned_copied, 8 * b + 8)
            wf = wbt[:, :, :, :, :].rearrange("p g h c n -> p (g h c n)")
            for k in range(2):
                st_(wbt_dram[2 * b + k], wf[:, k * 2048:(k + 1) * 2048])
            pool.wait_ge(s5_k_done, b + 1)
            for j in range(ST):
                for h in range(2):
                    st_(k_dram[b, j, :, h::2, :], kw[16 * h:16 * h + 16, :, (7 - j) * SC:(7 - j) * SC + 128])
            pool.wait_ge(s5_stored, 16 * S5_STORES * (b + 1))

        hs_ = view(0, 2, 49, DG)
        s5_gateT = view(0, KT, TOK)
        s5_uT = view(6144, KT, TOK)
        SCE = SCH + 2
        s5_u = view(12800, SG, SCE)
        s5_z = view(12800, KT, TOK)
        s_cols = view(19200, 2, 512)
        y_cols = view(20224, 2, 8, P)
        scan_t = hT_words[:, 512:1024].rearrange("p (d n r g) -> p d n r g", d=2, n=2, r=2)
        scan_u = hT_words[:, 0:512].rearrange("p (d n r g) -> p d n r g", d=2, n=2, r=2)
        st_rows = view(22272, 256)
        st_out = st_rows
        wk = [x_words[:, n * 3072:n * 3072 + 2048] for n in range(2)]
        cak = [x_words[:, n * 2048:(n + 1) * 2048].rearrange("p (d c n) -> p d c n", d=2, c=4) for n in range(2)]
        tk = [x_words[:, 4096 + n * 1024:5120 + n * 1024].rearrange("p (g n) -> p g n", g=8) for n in range(2)]
        u_parked = sem("u_parked")
        gate_parked = sem("gate_parked")
        gate_back = sem("gate_back")
        u_in = sem("u_in")
        u_zero = sem("u_zero")
        h0_in = sem("h0_in")
        wk_in = [sem("wk_in0"), sem("wk_in1")]
        cak_in = [sem("cak_in0"), sem("cak_in1")]
        tk_in = [sem("tk_in0"), sem("tk_in1")]
        cak_zero = sem("cak_zero")
        s_ready = sem("s_ready")
        s_copied = sem("s_copied")
        s_turned = sem("s_turned")
        s_taken = sem("s_taken")
        y_ready = sem("y_ready")
        y_copied = sem("y_copied")
        y_turned = sem("y_turned")
        y_taken = sem("y_taken")
        state_stored = sem("state_stored")

        def pool_s5(pool, l):
            pool.wait_ge(stage_done, after(f"norm{l}.copied1"))
            nc.gpsimd.dma_start(st_rows, w["state_s5"].rearrange("a b d (g h) n r -> (a b d g) (h n r)", h=2))\
                .then_inc(h0_in, 16)
            nc.gpsimd.memset(s5_u[:, :, SCH:SCE], 0.0).then_inc(u_zero, 1)
            pool.wait_ge(u_evacuated, 2)
            nc.gpsimd.dma_start(ud_dram.rearrange("(k p) n -> p k n", p=P), s5_uT).then_inc(u_parked, 16)
            pool.wait_ge(u_parked, 16)
            pool.wait_ge(u_zero, 1)
            for rows, col, tok in ((slice(112, 128), SCH, 0), (slice(0, 16), SCH + 1, CTX - 1)):
                at = tok % ST * SCH + tok // ST
                nc.gpsimd.dma_start(s5_u[rows, :, col:col + 1],
                                    ud_dram[:, at:at + 1].rearrange("(g p) c -> p g c", p=SC),
                                    allow_slow_non_contiguous=True).then_inc(u_in, 16)
            for j in range(ST):
                nc.gpsimd.dma_start(s5_u[16 * j:16 * j + 16, :, 0:SCH],
                                    ud_dram[:, j * SCH:(j + 1) * SCH].rearrange("(g p) c -> p g c", p=SC))\
                    .then_inc(u_in, 16)
            pool.wait_ge(stage_done, after(f"mix{l}.projected"))
            nc.gpsimd.dma_start(gate_dram, s5_gateT.rearrange("p a b -> p (a b)")).then_inc(gate_parked, 16)
            pool.wait_ge(stage_done, after(f"mix{l}.contributions"))
            for n in range(2):
                nc.gpsimd.memset(cak[n], 0.0).then_inc(cak_zero, 1)
            pool.wait_ge(stage_done, after(f"mix{l}.mixed"))
            nc.gpsimd.dma_start(s5_gateT.rearrange("p a b -> p (a b)"), gate_dram).then_inc(gate_back, 16)
            pool.wait_ge(stage_done, after(f"mix{l}.gated"))
            nc.gpsimd.dma_start(outs[4].rearrange("a b d (g h) n r -> (a b d g) (h n r)", h=2), st_rows)\
                .then_inc(state_stored, 16)
            pool.wait_ge(state_stored, 16)

        def sp_s5(sp, l):
            sp.wait_ge(stage_done, after(f"mix{l}.projected"))
            for k in range(16):
                if k >= 2:
                    sp.wait_ge(s_copied, 4 * (k - 1))
                nc.sync.dma_start(wk[k % 2], wbt_dram[k]).then_inc(wk_in[k % 2], 16)
            sp.wait_ge(stage_done, after(f"mix{l}.contributions"))
            sp.wait_ge(cak_zero, 2)
            for m in range(32):
                if m >= 2:
                    sp.wait_ge(y_ready, m - 1)
                for d in range(2):
                    for h in range(2):
                        rows = slice(64 * h, 64 * h + 64)
                        g = 2 * (m % 4)
                        nc.sync.dma_start(cak[m % 2][rows, d, :, 128 * h:128 * h + 128],
                                            ca_dram[m // 4, rows, d, g:g + 2, :, :].rearrange("p g r n -> p (g r) n"))\
                            .then_inc(cak_in[m % 2], 16)
                if m % 2 == 0:
                    k = m // 2
                    if k >= 2:
                        sp.wait_ge(y_ready, 2 * (k - 1))
                    nc.sync.dma_start(tk[k % 2].rearrange("p g n -> p (g n)"),
                                        k_dram[k // 2, :, :, 8 * (k % 2):8 * (k % 2) + 8, :]
                                        .rearrange("j p g n -> (j p) (g n)")).then_inc(tk_in[k % 2], 16)

        u_evacuated = sem("u_evacuated")

        def pe_s5(pe, st, l):
            for name in ("u", "gate"):
                def body(i, g0, u):
                    group_sums(pe, i, g0, u, [P] * 4)
                loop_groups(nc.tensor, f"{name}{l}", 4, body)
            st.at(f"mix{l}.projected")
            pe.wait_ge(h0_in, 16)
            for r in range(2):
                nc.tensor.transpose(banks[7][:, r * P:(r + 1) * P], st_rows[:, r::2], ident[:, :])
            st.at(f"mix{l}.gate_parked")
            pe.wait_ge(u_in, 16 * (ST + 2))
            for gp in range(64):
                k = gp // 4
                pe.wait_ge(wk_in[k % 2], 16 * (k // 2 + 1))
                if gp >= 2:
                    pe.wait_ge(s_copied, gp - 1)
                for h in range(2):
                    g = 2 * (gp % 4) + h
                    nc.tensor.matmul(banks[gp % 2][0:SCE, h * 256:(h + 1) * 256], s5_u[:, 2 * gp + h, :],
                                     wk[k % 2][:, g * 256:(g + 1) * 256], start=True, stop=True)
                nc.tensor.drain().then_inc(s_ready, 1)
                if gp:
                    pe_turn_contributions(pe, gp - 1)
            pe_turn_contributions(pe, 63)
            st.at(f"mix{l}.contributions")
            st.at(f"mix{l}.scanned")
            for k in range(16):
                pe.wait_ge(tk_in[k % 2], 16 * (k // 2 + 1))
                for half in range(2):
                    m = 2 * k + half
                    pe.wait_ge(cak_in[half], 16 * 4 * (k + 1))
                    if k:
                        pe.wait_ge(y_copied, m - 1)
                    for a in range(2):
                        gp = 2 * m + a
                        out = banks[half][0:SCH, a * 256:(a + 1) * 256]
                        for r in range(2):
                            for d in range(2):
                                nc.tensor.matmul(out, hs_[:, r, 0:SCH, d * 64 + gp], cak[half][:, d, 2 * a + r, :],
                                                 start=(r == 0 and d == 0), stop=False, skip_group_check=True)
                        for h in range(2):
                            nc.tensor.matmul(out[:, h * 128:(h + 1) * 128], s5_u[:, 2 * gp + h, 0:SCH],
                                             tk[k % 2][:, 4 * half + 2 * a + h, :], start=False, stop=True,
                                             skip_group_check=True)
                    nc.tensor.drain().then_inc(y_ready, 1)
                if k:
                    pe_turn_outputs(pe, k - 1)
            pe_turn_outputs(pe, 15)
            for r in range(2):
                nc.tensor.transpose(banks[7][:, r * P:(r + 1) * P], hs_[:, r, 48, :], ident[:, :])
            st.at(f"mix{l}.mixed")
            st.at(f"mix{l}.gated")
            st.at(f"mix{l}.gated_y")

            def glu_body(i, g0, u):
                group_sums(pe, i, g0, u, [P] * 4)
            loop_groups(nc.tensor, f"glu{l}", 4, glu_body)
            st.at(f"mix{l}.glu")
            st.at(f"mix{l}.split")

        def pe_turn_contributions(pe, gp):
            pe.wait_ge(s_copied, gp + 1)
            if gp >= 4 and gp % 2 == 0:
                pe.wait_ge(s_taken, gp // 2 - 1)
            for c in range(4):
                at = (gp % 2) * 256 + c * SCE
                nc.tensor.transpose(banks[2 + (gp // 2) % 2][:, at:at + SCE], s_cols[0:SCE, gp % 2, c * P:(c + 1) * P],
                                    ident[0:SCE, 0:SCE])
            if gp % 2:
                nc.tensor.drain().then_inc(s_turned, 1)

        def pe_turn_outputs(pe, k):
            pe.wait_ge(y_copied, 2 * k + 2)
            if k >= 2:
                pe.wait_ge(y_taken, k - 1)
            for j in range(ST):
                nc.tensor.transpose(banks[2 + k % 2][:, j * SCH:(j + 1) * SCH], y_cols[0:SCH, k % 2, j, :],
                                    ident[0:SCH, 0:SCH])
            nc.tensor.drain().then_inc(y_turned, 1)

        def act_s5(act, st, l):
            def u_write(i, u, half):
                for m in range(2):
                    act_copy(s5_uT[:, bass.ds(i * 8 + 4 * u + m, 1), :].rearrange("p a (j c) -> p (a j) c", j=ST),
                             banks[4 * half + m][:, 0:TOK].rearrange("p (c j) -> p j c", j=ST))
            stream("act", f"u{l}", u_write)
            nc.scalar.drain().then_inc(u_evacuated, 1)

            def gate_write(i, u, half):
                for m in range(4):
                    nc.scalar.activation(s5_gateT[:, bass.ds(i * 8 + 4 * u + m, 1), :], banks[4 * half + m][:, 0:TOK], ACT.Silu)
            stream("act", f"gate{l}", gate_write, share=2)
            st.at(f"mix{l}.projected")
            act.wait_ge(gate_parked, 16)
            st.at(f"mix{l}.gate_parked")
            for gp in range(64):
                act.wait_ge(s_ready, gp + 1)
                if gp >= 4:
                    act.wait_ge(s_turned, (gp - 2) // 2)
                act_copy(s_cols[0:SCE, gp % 2, :].rearrange("p (c h n) -> p h c n", c=4, h=2),
                         banks[gp % 2][0:SCE, :].rearrange("p (h c n) -> p h c n", h=2, c=4))
                nc.scalar.drain().then_inc(s_copied, 1)
            st.at(f"mix{l}.contributions")
            st.at(f"mix{l}.scanned")
            for k in range(16):
                for half in range(2):
                    act.wait_ge(y_ready, 2 * k + half + 1)
                    if k >= 2:
                        act.wait_ge(y_turned, k - 1)
                    act_copy(y_cols[0:SCH, k % 2, :, 64 * half:64 * half + 64].rearrange("p j (g q) -> p g j q", q=SC),
                             banks[half][0:SCH, :].rearrange("p (g j q) -> p g j q", g=4, j=ST))
                    nc.scalar.drain().then_inc(y_copied, 1)
                if k:
                    act_take_outputs(act, k - 1)
            act_take_outputs(act, 15)
            st.at(f"mix{l}.mixed")
            st.at(f"mix{l}.gated")
            split_h("act")
            st.at(f"mix{l}.gated_y")

            def glu_write(i, u, half):
                for m in range(4):
                    nc.scalar.activation(s5_z[:, bass.ds(i * 8 + 4 * u + m, 1), :], banks[4 * half + m][:, 0:TOK],
                                         ACT.Sigmoid, bias=glu_bias(i, u, m))
            stream("act", f"glu{l}", glu_write, share=2)
            st.at(f"mix{l}.glu")
            for q in range(4):
                act.wait_ge(h_ready, 4 * nth(l) + q + 1)
                split_h("act", [q])
            st.at(f"mix{l}.split")

        def glu_bias(i, u, m):
            return vecs[:, 0, bass.ds(i * 8 + (32 + 4 * u + m), 1)]

        def act_take_outputs(act, k):
            act.wait_ge(y_turned, k + 1)
            nc.scalar.activation(h32[:, k, :].rearrange("p (c j) -> p j c", j=ST),
                                 banks[2 + k % 2][:, 0:TOK].rearrange("p (j c) -> p j c", j=ST), ACT.Gelu_apprx_tanh)
            nc.scalar.drain().then_inc(y_taken, 1)

        def dve_s5(dve, st, l):
            v = nc.vector

            def u_write(i, u, half):
                for m in range(2, 4):
                    v.tensor_copy(s5_uT[:, bass.ds(i * 8 + 4 * u + m, 1), :].rearrange("p a (j c) -> p (a j) c", j=ST),
                                  banks[4 * half + m][:, 0:TOK].rearrange("p (c j) -> p j c", j=ST))
            stream("dve", f"u{l}", u_write)
            v.drain().then_inc(u_evacuated, 1)
            stream("dve", f"gate{l}")
            st.at(f"mix{l}.projected")
            dve.wait_ge(gate_parked, 16)
            dve.wait_ge(u_parked, 16)
            st.at(f"mix{l}.gate_parked")
            v.memset(hs_[:, :, 0, 0:64], 0.0)
            v.memset(hs_[:, :, SCX - 1, 64:128], 0.0)
            bk = banks[7][:, 0:2 * P].rearrange("p (r g) -> p r g", r=2)
            v.tensor_copy(hs_[:, :, SCX, 0:64], bk[:, :, 0:64])
            v.tensor_copy(hs_[:, :, SCH - 1, 64:128], bk[:, :, 64:128])
            for t in range(32):
                dve.wait_ge(s_turned, t + 1)
                src = banks[2 + t % 2][:, :].rearrange("p (g n) -> p g n", g=2)[:, :, 0:4 * SCE]\
                    .rearrange("p g (d r c) -> p g d r c", d=2, r=2)
                g = 2 * t
                for r in range(2):
                    f = src[:, :, 0, r, :].rearrange("p g c -> p c g")
                    v.tensor_copy(hs_[:, r, 1:SCX, g:g + 2], f[:, 0:SCX - 1, :])
                    v.tensor_copy(hs_[:, r, 48, g:g + 2], f[:, SCH, :])
                    v.tensor_copy(hs_[:, r, SCX + 1:SCH, g:g + 2], f[:, SCX:SCH - 1, :])
                    bw = src[:, :, 1, r, :].rearrange("p g c -> p c g")
                    v.tensor_copy(hs_[:, r, 0:SCX - 1, 64 + g:64 + g + 2], bw[:, 1:SCX, :])
                    v.tensor_copy(hs_[:, r, 48, 64 + g:64 + g + 2], bw[:, SCH + 1, :])
                    v.tensor_copy(hs_[:, r, SCX:SCH - 1, 64 + g:64 + g + 2], bw[:, SCX + 1:SCH, :])
                v.drain().then_inc(s_taken, 1)
            st.at(f"mix{l}.contributions")
            for s in range(SCH - SCX - 1):
                both = int(s < SCX - 1)
                for d in range(2):
                    dd = slice(64 * d, 64 * d + 64)
                    if d == 0:
                        steps = [(SCX + s, SCX + s + 1)] + [(s, s + 1)] * both
                    else:
                        steps = [(SCH - 1 - s, SCH - 2 - s)] + [(SCX - 1 - s, SCX - 2 - s)] * both
                    for n, (a, b) in enumerate(steps):
                        v.tensor_tensor(scan_t[:, d, n, :, :], hs_[:, :, a, dd],
                                        a8[:, 0:1, dd].broadcast_to([P, 2, 64]), ALU.mult)
                        v.tensor_tensor(scan_u[:, d, n, :, :], hs_[:, ::-1, a, dd], a8[:, 1:3, dd], ALU.mult)
                v.drain()
                for d in range(2):
                    v.tensor_tensor(scan_t[:, d, 0:1 + both], scan_t[:, d, 0:1 + both], scan_u[:, d, 0:1 + both], ALU.add)
                v.drain()
                for d in range(2):
                    dd = slice(64 * d, 64 * d + 64)
                    dst = [(SCX + s + 1, s + 1), (SCH - 2 - s, SCX - 2 - s)][d][0:1 + both]
                    for n, b in enumerate(dst):
                        v.tensor_tensor(hs_[:, :, b, dd], hs_[:, :, b, dd], scan_t[:, d, n, :, :], ALU.add)
                v.drain()
            st.at(f"mix{l}.scanned")
            st.at(f"mix{l}.mixed")
            v.tensor_copy(st_out.rearrange("p (n r) -> p r n", r=2), banks[7][:, 0:2 * P].rearrange("p (r n) -> p r n", r=2))
            dve.wait_ge(gate_back, 16)
            st.at(f"mix{l}.gated")
            v.tensor_tensor(s5_gateT, s5_gateT, h32, ALU.mult)
            v.drain()
            split_h("dve")
            st.at(f"mix{l}.gated_y")
            stream("dve", f"glu{l}")
            st.at(f"mix{l}.glu")
            for q in range(4):
                k = slice(4 * q, 4 * q + 4)
                v.tensor_tensor(h32[:, k, :], s5_z[:, k, :], s5_gateT[:, k, :], ALU.mult)
                v.drain().then_inc(h_ready, 1)
            split_h("dve")
            st.at(f"mix{l}.split")


        def pool_program(pool):
            nc.gpsimd.sem_inc(ada_used, 4)
            nc.gpsimd.sem_inc(lo_ready, 4)
            nc.gpsimd.sem_inc(chunk_used, 2)
            for half in range(2):
                nc.gpsimd.sem_inc(sums_taken[half], 2)
            xp = w["x_prompt"].rearrange("b t d -> (b t) d")
            xs = w["x_sample"].rearrange("b (a t) d -> (b t) a d", t=P)
            nc.gpsimd.dma_start(ident[:, :], consts["ident"]).then_inc(inputs_in, 16)
            nc.gpsimd.memset(rows_v, 0.0).then_inc(rows_zero, 1)
            pool.wait_ge(rows_zero, 1)
            for name, src in (("c_ctx", w["c_ctx"].rearrange("(k p) -> k p", p=P)),
                              ("c", w["c"].rearrange("b (k p) -> (b k) p", p=P)),
                              ("b_glu", w["s5_b_glu"].rearrange("b (k p) -> (b k) p", p=P)),
                              ("d", w["s5_d"].rearrange("b (k p) -> (b k) p", p=P)),
                              ("norm_pre", w["norm_pre"].rearrange("l (k p) -> (l k) p", p=P)),
                              ("norm_post", w["norm_post"].rearrange("l (k p) -> (l k) p", p=P)),
                              ("gla_b_g", w["gla_b_g"].rearrange("b d (k p) -> (b d k) p", p=P))):
                tile_, col = VEC[name]
                nc.gpsimd.dma_start(rows_v[col:col + src.shape[0], tile_, :], src).then_inc(inputs_in, 16)
            for l in range(DEPTH):
                nc.gpsimd.dma_start(rows_v[(l % 2) * 64:(l % 2) * 64 + 48, 2 + l // 2, :],
                                    w["ada_b"][l].rearrange("(j p) -> j p", p=P)).then_inc(inputs_in, 16)
            pool_s5_basics(pool)
            for b in range(8):
                pool_s5_batch(pool, b)
            nc.gpsimd.dma_start(x[:, 0, :], xp).then_inc(x_in, 16)
            nc.gpsimd.dma_start(x[:, 1:3, :], xs).then_inc(x_in, 16)
            for l in layers:
                park_x(pool, l)
                if l % 3 == 1:
                    pool_s5(pool, l)
                if l % 3 == 0:
                    pool_mla(pool, l)
                if l % 3 == 2:
                    pool_gla(pool, l)
                fetch_x(pool, l)
            pool.wait_ge(stage_done, after(stage_names[-1]))
            nc.gpsimd.dma_start(outs[0].rearrange("b t d -> (b t) d"), x[:, 0, :]).then_inc(result_out, 16)
            nc.gpsimd.dma_start(outs[1].rearrange("b (a t) d -> (b t) a d", t=P), x[:, 1:3, :]).then_inc(result_out, 16)
            pool.wait_ge(result_out, 32)


        def pool_mla(pool, l):
            j = l // 3
            pool.wait_ge(stage_done, after(f"norm{l}.copied1"))
            nc.gpsimd.dma_start(ckv_sb[:, 3, :], w["cache_mla_ckv"][0, j]).then_inc(small_in, 16)
            for d in range(2):
                nc.gpsimd.dma_start(kr_sb[:, 3, d * ROPE:(d + 1) * ROPE], w["cache_mla_krope"][0, j]).then_inc(small_in, 16)
            nc.gpsimd.dma_start(gamma, w["mla_kv_norm"][j:j + 1, :].broadcast_to([P, LORA])).then_inc(small_in, 16)
            nc.gpsimd.dma_start(cos_t, consts["rope_cos"]).then_inc(small_in, 16)
            nc.gpsimd.dma_start(sin_t, consts["rope_sin"]).then_inc(small_in, 16)
            nc.gpsimd.dma_start(swap_t, consts["rope_swap"]).then_inc(small_in, 16)
            pool.wait_ge(stage_done, after(f"mix{l}.kv_normed"))
            nc.gpsimd.dma_start(outs[2][0, j], ckv_sb[:, 0, :]).then_inc(stored, 16)
            nc.gpsimd.dma_start(outs[3][0, j], kr_sb[:, 0, 0:ROPE]).then_inc(stored, 16)
            pool.wait_ge(stored, 32 * (nth(l) + 1))

        def sp_program(sp):
            for l in range(DEPTH):
                for part in range(2):
                    load_job(sp, f"ada{l}{'ab'[part]}", 6, w["ada_w"][l], part * 6 * GC)
            sp.wait_ge(ada_used, 4 * (ADA_GROUPS + 1))
            for l in layers:
                j = l // 3
                if l % 3 == 0:
                    w_in = w["mla_w_in"][j]
                    wv = w_in.rearrange("(s k p) n -> s p k n", k=4, p=P)

                    def body(i, g0, u):
                        load_group(sp, i, g0, u, lambda s, u: wv[s, :, :, bass.ds(i * 768 + u * 384, 384)], 384)
                    loop_groups(nc.sync, f"q{l}", 8, body)
                    load_job(sp, f"ckv{l}", 1, w_in, NQ)
                    load_job(sp, f"krope{l}", 1, w_in, NQ + LORA, ROPE)
                    load_job(sp, f"gate{l}", 4, w_in, NQ + LORA + ROPE)
                    uk = w["mla_w_ukv"][j].rearrange("(k p) n -> p k n", p=P)
                    for g in range(2):
                        load_group(sp, 0, FIRST_GROUP[f"ukv{l}"], g,
                                   lambda s, u: uk[:, :, (4 * u + s) * GC:(4 * u + s + 1) * GC], GC)
                    load_job(sp, f"out{l}", 4, w["mla_w_out"][j], 0)
                if l % 3 == 1:
                    load_job(sp, f"u{l}", 4, w["s5_w_in"][j], 0)
                    load_job(sp, f"gate{l}", 4, w["s5_w_in"][j], D)
                    load_job(sp, f"glu{l}", 4, w["s5_w_glu"][j], 0, only=(0,))
                    sp_s5(sp, l)
                    load_job(sp, f"glu{l}", 4, w["s5_w_glu"][j], 0, only=(1, 2, 3))
                    load_job(sp, f"out{l}", 4, w["s5_w_out"][j], 0)
                if l % 3 == 2:
                    w_in = w["gla_w_in"][j]
                    load_job(sp, f"q{l}", 2, w_in, 0)
                    load_job(sp, f"k{l}", 2, w_in, GH * GDK)
                    load_job(sp, f"v{l}", 4, w_in, 2 * GH * GDK)
                    load_job(sp, f"r{l}", 4, w_in, 2 * GH * GDK + D)
                    load_job(sp, f"glr{l}", 1, w_in, 2 * GH * GDK + 2 * D, 2 * GRANK)
                    load_job(sp, f"out{l}", 4, w["gla_w_out"][j], 0)

        block.tensor(pe_program)
        block.scalar(act_program)
        block.vector(dve_program)
        block.gpsimd(pool_program)
        block.sync(sp_program)


_INS = ["x_prompt", "x_sample", "cache_mla_ckv", "cache_mla_krope", "state_s5", "state_gla", "c", "c_ctx",
        "ada_w", "ada_b", "norm_pre", "norm_post", "mla_w_in", "mla_kv_norm", "mla_w_ukv", "mla_w_out",
        "s5_w_in", "s5_a_re", "s5_a_im", "s5_log_dt", "s5_b_re", "s5_b_im", "s5_c_re", "s5_c_im",
        "s5_d", "s5_w_glu", "s5_b_glu", "s5_w_out", "gla_w_in", "gla_w_g2", "gla_b_g", "gla_norm", "gla_w_out"]
_OUTS = [(1, CTX, D), (1, LAT, D), (1, 2, CTX, LORA), (1, 2, CTX, ROPE), (1, 1, 2, SG, SN, 2), (1, 1, 2, GH, GDK, GDV)]


def kernel(**inputs):
    import concourse.bacc as _bacc
    from concourse.bass_utils import run_bass_kernel_spmd
    arrays = {n: np.ascontiguousarray(inputs[n]) for n in _INS}
    nc = _bacc.Bacc("TRN2", target_bir_lowering=False, num_devices=1)
    constants = shape_constants()
    ins = {n: nc.dram_tensor(f"in_{n}", arrays[n].shape, F32, kind="ExternalInput").ap() for n in _INS}
    cs = {n: nc.dram_tensor(f"const_{n}", a.shape, F32, kind="ExternalInput").ap() for n, a in constants.items()}
    outs = [nc.dram_tensor(f"out_{i}", shape, F32, kind="ExternalOutput").ap() for i, shape in enumerate(_OUTS)]
    build(nc, ins, outs, cs)
    data = {f"in_{n}": arrays[n] for n in _INS} | {f"const_{n}": a for n, a in constants.items()}
    got = run_bass_kernel_spmd(nc, [data], core_ids=[0]).results[0]
    return tuple(got[f"out_{i}"] for i in range(len(_OUTS)))
```
